# Optimizing a Trainium2 kernel written in Bass

```python
import jax, jax.numpy as jnp
from jax import lax
import numpy as np

D_MODEL = 1024
BATCH = 1
SEQ = 1024
DEPTH = 1

D_MIX = D_MODEL
HEAD_DIM = 64
CONV_WIDTH = (D_MIX * 3) // 8
FOURIER_WIDTH = D_MIX // 4
SGU_WIDTH = D_MIX - CONV_WIDTH - FOURIER_WIDTH
CONV_HEADS = CONV_WIDTH // HEAD_DIM
FOURIER_GROUPS = FOURIER_WIDTH // HEAD_DIM
SGU_HEADS = SGU_WIDTH // HEAD_DIM
W_IN_COLS = 2 * CONV_WIDTH + FOURIER_WIDTH + 2 * SGU_WIDTH
CONV_KSIZE = 31
SGU_CHUNK = 128
N_EXPERTS = 64
N_EXPERT_GROUPS = 8
EXPERTS_PER_GROUP = N_EXPERTS // N_EXPERT_GROUPS
TOP_K = 2
D_FF_EXPERT = D_MODEL // 2
EXPERT_BLOCK = 128
N_MOD = 6
EPS = 1e-6

kernel_name = "hybrid_conv_fourier_sgu_grouped_moe_encoder"

def rmsnorm(x, g):
    xf = x.astype(jnp.float32)
    y = xf * lax.rsqrt(jnp.mean(xf * xf, axis=-1, keepdims=True) + EPS)
    return (y * g.astype(jnp.float32)).astype(x.dtype)

def layernorm(x, g, b):
    xf = x.astype(jnp.float32)
    mu = jnp.mean(xf, axis=-1, keepdims=True)
    var = jnp.mean(jnp.square(xf - mu), axis=-1, keepdims=True)
    y = (xf - mu) * lax.rsqrt(var + EPS)
    return (y * g.astype(jnp.float32) + b.astype(jnp.float32)).astype(x.dtype)

def conv_module(za, conv_w, conv_b, gn_g, gn_b):
    a, g = jnp.split(za, 2, axis=-1)
    h = a * jax.nn.sigmoid(g)
    h = lax.conv_general_dilated(
        h, conv_w.reshape(CONV_KSIZE, 1, CONV_WIDTH).astype(h.dtype),
        window_strides=(1,), padding=[(CONV_KSIZE // 2, CONV_KSIZE // 2)],
        dimension_numbers=("NWC", "WIO", "NWC"),
        feature_group_count=CONV_WIDTH) + conv_b
    Bsz, S, _ = h.shape
    hg = h.reshape(Bsz, S, CONV_HEADS, HEAD_DIM)
    hg = layernorm(hg, jnp.ones((HEAD_DIM,), jnp.float32), jnp.zeros((HEAD_DIM,), jnp.float32))
    h = hg.reshape(Bsz, S, CONV_WIDTH) * gn_g + gn_b
    return jax.nn.silu(h)

def fourier_mix(zb):
    Bsz, S, _ = zb.shape
    xg = zb.reshape(Bsz, S, FOURIER_GROUPS, HEAD_DIM).astype(jnp.float32)
    f = jnp.fft.fftn(xg, axes=(1, 3), norm="ortho").real
    return f.reshape(Bsz, S, FOURIER_WIDTH).astype(zb.dtype)

def spatial_gating(zc, ln_g, ln_b, w_s, b_s):
    z = jax.nn.gelu(zc)
    u, v = jnp.split(z, 2, axis=-1)
    v = layernorm(v, ln_g, ln_b)
    Bsz, S, _ = v.shape
    vc = v.reshape(Bsz, S // SGU_CHUNK, SGU_CHUNK, SGU_HEADS, HEAD_DIM)
    vs = jnp.einsum("hpq,bnqhd->bnphd", w_s, vc) + b_s.T[:, :, None]
    return u * vs.reshape(Bsz, S, SGU_WIDTH)

def token_mixer(h, w_in, w_out, conv_w, conv_b, gn_g, gn_b, ln_g, ln_b, w_s, b_s):
    z = h @ w_in
    za = z[..., :2 * CONV_WIDTH]
    zb = z[..., 2 * CONV_WIDTH:2 * CONV_WIDTH + FOURIER_WIDTH]
    zc = z[..., 2 * CONV_WIDTH + FOURIER_WIDTH:]
    ya = conv_module(za, conv_w, conv_b, gn_g, gn_b)
    yb = fourier_mix(zb)
    yc = spatial_gating(zc, ln_g, ln_b, w_s, b_s)
    return jnp.concatenate([ya, yb, yc], axis=-1) @ w_out

def moe(h, router_w, router_b, w1, w3, w2):
    Bsz, S, D = h.shape
    N = Bsz * S
    M = N * TOP_K
    xt = h.reshape(N, D)
    probs = jax.nn.softmax((xt @ router_w).astype(jnp.float32), axis=-1)
    sel = probs + router_b.astype(jnp.float32)
    sel_g = sel.reshape(N, N_EXPERT_GROUPS, EXPERTS_PER_GROUP)
    gscore = jnp.sum(lax.top_k(sel_g, TOP_K)[0], axis=-1)
    gidx = jnp.argmax(gscore, axis=-1)
    in_grp = jnp.take_along_axis(sel_g, gidx[:, None, None], axis=1)[:, 0]
    _, local = lax.top_k(in_grp, TOP_K)
    eidx = gidx[:, None] * EXPERTS_PER_GROUP + local
    gw = jnp.take_along_axis(probs, eidx, axis=1)
    gw = gw / jnp.sum(gw, axis=-1, keepdims=True)

    e_flat = eidx.reshape(M).astype(jnp.int32)
    tok = jnp.arange(M, dtype=jnp.int32) // TOP_K
    w_flat = gw.reshape(M)
    order = jnp.argsort(e_flat)
    e_s, t_s, w_s = e_flat[order], tok[order], w_flat[order]
    counts = jnp.bincount(e_flat, length=N_EXPERTS).astype(jnp.int32)
    starts = jnp.cumsum(counts) - counts
    pcounts = (counts + EXPERT_BLOCK - 1) // EXPERT_BLOCK * EXPERT_BLOCK
    pends = jnp.cumsum(pcounts)
    pstarts = pends - pcounts
    dest = pstarts[e_s] + (jnp.arange(M, dtype=jnp.int32) - starts[e_s])
    n_blocks = (M + N_EXPERTS * (EXPERT_BLOCK - 1) + EXPERT_BLOCK - 1) // EXPERT_BLOCK
    xp = jnp.zeros((n_blocks * EXPERT_BLOCK, D), h.dtype).at[dest].set(xt[t_s])
    blk_start = jnp.arange(n_blocks, dtype=jnp.int32) * EXPERT_BLOCK
    blk_e = jnp.minimum(jnp.searchsorted(pends, blk_start, side="right"), N_EXPERTS - 1)

    def expert_block(args):
        xb, e = args
        return (jax.nn.silu(xb @ w1[e]) * (xb @ w3[e])) @ w2[e]

    yp = lax.map(expert_block, (xp.reshape(n_blocks, EXPERT_BLOCK, D), blk_e))
    yp = yp.reshape(n_blocks * EXPERT_BLOCK, D)
    contrib = (yp[dest] * w_s[:, None]).astype(h.dtype)
    y = jnp.zeros((N, D), h.dtype).at[t_s].add(contrib)
    return y.reshape(Bsz, S, D)

def setup_inputs(seed: int = 0) -> dict:
    key = jax.random.key(seed)
    ks = jax.random.split(key, 24)
    f32 = jnp.float32
    nrm = lambda k, shape, s: jax.random.normal(k, shape, f32) * s
    return {
        "x": nrm(ks[0], (BATCH, SEQ, D_MODEL), 1.0),
        "c": nrm(ks[1], (BATCH, D_MODEL), 1.0),
        "ln1_g": 1.0 + nrm(ks[2], (DEPTH, D_MODEL), 0.02),
        "ln2_g": 1.0 + nrm(ks[3], (DEPTH, D_MODEL), 0.02),
        "w_ada": nrm(ks[4], (DEPTH, D_MODEL, N_MOD * D_MODEL), 0.5 * D_MODEL ** -0.5),
        "b_ada": nrm(ks[5], (DEPTH, N_MOD * D_MODEL), 0.02),
        "w_in": nrm(ks[6], (DEPTH, D_MODEL, W_IN_COLS), D_MODEL ** -0.5),
        "w_out": nrm(ks[7], (DEPTH, D_MIX, D_MODEL), D_MIX ** -0.5),
        "conv_w": nrm(ks[8], (DEPTH, CONV_KSIZE, CONV_WIDTH), CONV_KSIZE ** -0.5),
        "conv_b": nrm(ks[9], (DEPTH, CONV_WIDTH), 0.02),
        "conv_gn_g": 1.0 + nrm(ks[10], (DEPTH, CONV_WIDTH), 0.02),
        "conv_gn_b": nrm(ks[11], (DEPTH, CONV_WIDTH), 0.02),
        "sgu_ln_g": 1.0 + nrm(ks[12], (DEPTH, SGU_WIDTH), 0.02),
        "sgu_ln_b": nrm(ks[13], (DEPTH, SGU_WIDTH), 0.02),
        "sgu_w": nrm(ks[14], (DEPTH, SGU_HEADS, SGU_CHUNK, SGU_CHUNK), SGU_CHUNK ** -0.5),
        "sgu_b": 1.0 + nrm(ks[15], (DEPTH, SGU_HEADS, SGU_CHUNK), 0.02),
        "router_w": nrm(ks[16], (D_MODEL, N_EXPERTS), D_MODEL ** -0.5),
        "router_b": nrm(ks[17], (N_EXPERTS,), 0.01),
        "exp_w1": nrm(ks[18], (DEPTH, N_EXPERTS, D_MODEL, D_FF_EXPERT), D_MODEL ** -0.5),
        "exp_w3": nrm(ks[19], (DEPTH, N_EXPERTS, D_MODEL, D_FF_EXPERT), D_MODEL ** -0.5),
        "exp_w2": nrm(ks[20], (DEPTH, N_EXPERTS, D_FF_EXPERT, D_MODEL), D_FF_EXPERT ** -0.5),
        "final_g": 1.0 + nrm(ks[21], (D_MODEL,), 0.02),
    }

def reference(x, c, ln1_g, ln2_g, w_ada, b_ada, w_in, w_out, conv_w, conv_b, conv_gn_g, conv_gn_b,
              sgu_ln_g, sgu_ln_b, sgu_w, sgu_b, router_w, router_b, exp_w1, exp_w3, exp_w2, final_g):
    c_act = jax.nn.silu(c)
    for l in range(DEPTH):
        mod = (c_act @ w_ada[l] + b_ada[l]).reshape(c.shape[0], N_MOD, D_MODEL)[:, :, None, :]
        shift1, scale1, gate1 = mod[:, 0], mod[:, 1], mod[:, 2]
        shift2, scale2, gate2 = mod[:, 3], mod[:, 4], mod[:, 5]
        h = rmsnorm(x, ln1_g[l]) * (1.0 + scale1) + shift1
        x = x + gate1 * token_mixer(h, w_in[l], w_out[l], conv_w[l], conv_b[l], conv_gn_g[l],
                                    conv_gn_b[l], sgu_ln_g[l], sgu_ln_b[l], sgu_w[l], sgu_b[l])
        h = rmsnorm(x, ln2_g[l]) * (1.0 + scale2) + shift2
        x = x + gate2 * moe(h, router_w, router_b, exp_w1[l], exp_w3[l], exp_w2[l])
    return rmsnorm(x, final_g)


_drawn_inputs = setup_inputs


def setup_inputs(seed=0):
    import zlib

    import numpy as np

    out = dict(_drawn_inputs(seed))
    spreads = {}
    factors = {'ln1_g': 2.895,
     'conv_b': 22.436,
     'conv_gn_g': 40.52,
     'conv_gn_b': 46.104,
     'sgu_ln_g': 21.15,
     'sgu_ln_b': 20.413,
     'sgu_b': 21.205,
     'final_g': 7.583,
     'ln2_g': 6.048}
    for name, (base, spread) in spreads.items():
        noise = np.random.default_rng([zlib.crc32(name.encode()), seed]).standard_normal(out[name].shape)
        drawn = base * np.exp(spread * noise) if base else spread * noise
        out[name] = __import__('jax').numpy.asarray(drawn.astype(out[name].dtype))
    for name, factor in factors.items():
        out[name] = (out[name] * factor).astype(out[name].dtype)
    return out
```

```python
from contextlib import ExitStack

import concourse.bass as bass
from concourse import mybir

ALU = mybir.AluOpType
ACT = mybir.ActivationFunctionType
AX_X = mybir.AxisListType.X
F32 = mybir.dt.float32
I32 = mybir.dt.int32

P = 128
SEQ = 1024
D = 1024
TILES = SEQ // P
CH = D // P
HALF = 512
CONV, FOUR, SGU = 384, 256, 384
TAPS = 31
PAD = TAPS // 2
PADW = SEQ + 2 * PAD
WIN = 2 * CONV + FOUR + 2 * SGU
EXPERTS, GROUPS, PER = 64, 8, 8
FF = 512
BLK = 64
SLOTS = 4
EXPERT_FLOATS = 3 * 4096
MAX_BLOCKS = EXPERTS + 2 * SEQ // BLK
XS_ROWS = 2 * SEQ + BLK
EPS = 1e-6
BANKS = 8
NEG = -3.0e38
T_ENDS, T_ROWS = 0, EXPERTS + 1

C_ID, C_TRI, C_ONE, C_BD, C_DFT, C_EXC, C_INC, C_REV = 0, 128, 256, 384, 512, 768, 832, 896
C_GREV, C_THR, C_P, C_P64, C_ALT, C_END = 960, 968, 984, 985, 986, 987

RING = SLOTS * EXPERT_FLOATS
O_V = 0
O_PADH = O_V + 8 * SGU
O_WIN = O_PADH + 3 * PADW
O_WOUT = O_WIN + 8 * WIN - 8 * D
O_Y = O_WIN + 8 * WIN
O_D = O_Y + 8 * SEQ
O_H = O_D + 2 * 4096
O_SMALL = O_H + 8 * SEQ
assert EXPERT_FLOATS <= O_WOUT and O_WOUT + 8 * D <= O_Y and 2 * EXPERT_FLOATS <= O_Y + 8 * SEQ - 8 * HALF


def build(nc, x, c, ln1_g, ln2_g, w_ada, b_ada, w_in, w_out, conv_w, conv_b, conv_gn_g, conv_gn_b,
          sgu_ln_g, sgu_ln_b, sgu_w, sgu_b, router_w, router_b, exp_w1, exp_w3, exp_w2, final_g,
          consts, dft, out):
    ctx = ExitStack()
    with ctx:
        def sem(name):
            return ctx.enter_context(nc.semaphore(name))

        banks = ctx.enter_context(nc.psum_tensor("banks", [P, BANKS, HALF], F32))
        total = RING + 3360
        arena = ctx.enter_context(nc.sbuf_tensor("arena", [P, total], F32))
        table = ctx.enter_context(nc.sbuf_tensor("table", [1, T_ROWS + P], I32))
        rows_at = ctx.enter_context(nc.sbuf_tensor("rows_at", [P, 4, TILES], I32))
        mod_dram = nc.dram_tensor("mod_dram", [6 * D], F32)
        x2_dram = nc.dram_tensor("x2_dram", [SEQ, D], F32)
        xs_dram = nc.dram_tensor("xs_dram", [XS_ROWS, D], F32)
        ys_dram = nc.dram_tensor("ys_dram", [(MAX_BLOCKS + 1) * BLK, D], F32)

        def at(offset, *shape):
            n = 1
            for s in shape:
                n *= s
            view = arena[:, offset:offset + n]
            if len(shape) == 2:
                view = view.rearrange("p (a b) -> p a b", a=shape[0])
            if len(shape) == 3:
                view = view.rearrange("p (a b c) -> p a b c", a=shape[0], b=shape[1])
            return view

        v_t = at(O_V, TILES, SGU)
        pad_h = at(O_PADH, 3, PADW)
        squares = at(O_PADH, 6, HALF)
        w_in_s = at(O_WIN, CH, WIN)
        w_out_s = at(O_WOUT, CH, D)
        y_t = at(O_Y, CH, SEQ)
        x_t = at(O_Y, TILES, D)
        xt_four = y_t[:, 3:5, :]
        ada_s = at(O_D, 2, CH * HALF).rearrange("p a (c f) -> p a c f", c=CH)
        pq = at(O_WIN, TILES, 2 * 256).rearrange("p a (c f) -> p a c f", c=2)
        dft_s = at(O_D, 2, TILES, HALF)
        xr = at(O_D, TILES, D)
        h2_t = at(O_V, 2, CH, P)
        gate1 = at(O_V + 2 * D, D)
        gate1_b = at(O_V + 3 * D, D)
        h_t = at(O_H, CH, SEQ)
        x2 = at(O_H, TILES, D)

        used = {"mixing": O_SMALL, "kept": RING}
        most = {"mixing": RING, "kept": total}

        def small(*shape, life="mixing"):
            n = 1
            for s in shape:
                n *= s
            used[life] += n
            assert used[life] <= most[life], (life, used[life] - most[life])
            return at(used[life] - n, *shape)

        cst = small(C_END)
        tri, ones, bd = (cst[:, o:o + P] for o in (C_TRI, C_ONE, C_BD))
        ws_t = small(6, P)
        vec_rows = small(P)
        vecs = small(16)
        conv_t = small(3 * TAPS)
        gain_k = small(3, P)
        bs_b = small(3, P)
        c_col, c_act, c_wide = small(CH), small(CH), small(CH, 32)
        col = small(10, CH)
        LN1, LN2, SH1, SC1, SH2, SC2, BSH1, BSC1, BSH2, BSC2 = range(10)
        ab = small(4, CH)
        stats, mv, v_rstd = small(TILES, 6), small(TILES, 2), small(TILES)
        mod_rows = small(P)
        router_s = small(CH, EXPERTS)
        router_bb = small(EXPERTS)
        ws_rows = at(O_V, 6, P)
        conv_rows = at(O_V + 6 * P, CONV)
        ident = small(P, life="kept")
        ab_jh = small(2, 4, 2, life="kept")
        ss, rstd = small(3, TILES, life="kept"), small(3, TILES, life="kept")
        eps = small(1, life="kept")
        gate_w = small(2, TILES, life="kept")
        scratch = small(D, life="kept")
        xrow = small(HALF, life="kept")
        xt_s = small(4, 2, BLK, life="kept")
        ff_silu, ff, ff_t = scratch[:, 0:256], scratch[:, 256:512], scratch[:, 512:768]
        y_s = small(HALF, life="kept")
        gate2 = small(HALF, life="kept")
        tmp_a = xrow
        tmp_b = xt_s.rearrange("p a b c -> p (a b c)")
        gate2_b = tmp_b
        logit = y_s

        r0 = O_Y + 8 * SEQ - 8 * HALF
        prob, sel, sel2, hot1, hot2, cand, ranks, before = (at(r0 + i * HALF, HALF) for i in range(8))
        r1 = O_V
        best = at(r1, 12, TILES * GROUPS)
        tok = at(r1 + 768, 8, TILES)
        cnt = at(r1 + 832, 4)
        nb_wide, ct_wide = at(r1 + 840, P), at(r1 + 968, P)
        bounds = at(r1 + 1096, 3, EXPERTS)
        in_block = at(r1 + 1288, EXPERTS)
        in_tmp = at(r1 + 1352, EXPERTS)
        tab_c = at(r1 + 1416, 1)

        def d_cols(vector):
            return vector.rearrange("(h p j) -> p h j", h=2, j=4)

        def d_tile(view):
            return view.rearrange("p (h j) -> p h j", h=2)

        s_cst, s_vrows, s_convw, s_ws, s_small, s_c, s_cols = (sem(n) for n in (
            "consts_in", "vector_rows_in", "conv_w_in", "sgu_w_in", "sgu_b_in", "c_in", "columns_in"))
        s_x = [sem(f"x_in{i}") for i in range(2)]
        s_ada = [sem(f"ada_in{i}") for i in range(2)]
        s_win = [sem(f"w_in_in{i}") for i in range(4)]
        s_dft, s_wout, s_xr, s_gate1, s_gate2, s_rb = (sem(n) for n in (
            "dft_in", "w_out_in", "x_again_in", "gate1_in", "gate2_in", "router_in"))
        filled, freed_a, freed_d = sem("bank_filled"), sem("bank_freed_by_act"), sem("bank_freed_by_dve")
        s_modout, s_modcols = sem("mod_rows_stored"), sem("mod_columns_in")
        s_eps, s_std, s_mv, s_vstd = (sem(n) for n in ("eps_ready", "deviations_ready", "v_variances", "v_deviations"))
        s_cact, s_cwide, s_ss, s_xhat, s_ab = (sem(n) for n in (
            "c_act_ready", "c_wide_ready", "squares_summed", "xhat_ready", "affine_ready"))
        s_zero, s_conv, s_gnsq, s_gnn, s_gn = (sem(n) for n in (
            "pad_zeroed", "conv_step", "centred_squared", "gn_scaled", "gn_ready"))
        s_vn, s_sg, s_x2, s_x2st, s_xs = (sem(n) for n in (
            "v_ready", "gating_ready", "x2_ready", "x2_stored", "xs_scattered"))
        s_link = sem("dve_step")
        s_expin, s_exp, s_sums, s_wide, s_tabc, s_rows, s_tab = (sem(n) for n in (
            "logits_shifted", "exp_ready", "rank_inputs_ready", "counts_wide_ready", "table_columns_ready",
            "row_numbers_ready", "table_ready"))
        s_pz, s_padz = sem("pad_rows_zero"), sem("pad_rows_stored")
        s_w = [sem(f"expert_slot_in{i}") for i in range(SLOTS)]
        s_xrow = sem("block_rows_in")
        s_xtp, s_xtm, s_xts, s_h13, s_silu, s_ff, s_ftp, s_ft, s_yp, s_y, s_yst = (sem(n) for n in (
            "block_rows_transposed", "block_x_scaled", "block_x_ready", "block_h_ready", "block_silu", "block_ff",
            "block_ff_transposed", "block_ff_t_ready", "block_y_filled", "block_y_ready_plus_one", "block_y_stored"))
        s_begun, s_through = sem("experts_begun"), sem("blocks_through")
        s_yzero = sem("left_out_blocks_zeroed")
        s_x2r, s_fg = sem("x2_again_in"), sem("final_g_in")
        s_gat = [sem(f"rows_gathered{i}") for i in range(TILES)]
        s_t1, s_t2, s_t3, s_tout, s_out = (sem(n) for n in (
            "tail_first", "tail_both", "tail_sum", "tail_ready", "out_stored"))

        order = [("small", "d"), ("ws", 0, "d"), ("ws", 1, "d"), ("rs", "d")]
        order += [("ada", n, "d") for n in range(4)]
        order += [("xt", i, h, "ad"[h]) for i in range(TILES) for h in range(2)]
        ada_left = list(range(4, 12))
        for cc in range(3):
            for s in range(2):
                order += [("g", cc, s, "a"), ("a", cc, s, "d")]
                if cc or s:
                    order += [("ada", ada_left.pop(0), "a")]
        for cc in range(2):
            for s in range(2):
                order += [("b", cc, s, "a")]
                if ada_left:
                    order += [("ada", ada_left.pop(0), "a")]
        order += [("v", i, "a") for i in range(TILES)]
        order += [("u", cc, s, "a") for cc in range(3) for s in range(2)]
        order += [("pq", i, "a") for i in range(TILES)]
        gm = [("gm", cc, s, "d") for cc in range(3) for s in range(2)]
        gv = [("gv", cc, s, "a") for cc in range(3) for s in range(2)]
        order += gm[0:3]
        order += [("V", 0, "a"), ("U", 0, "d"), ("mid", "d")] + gm[3:6] + gv[0:3] + [("V", 1, "a"), ("U", 1, "d")]
        order += gv[3:6] + [("sg", j, hh, "d") for j in range(3) for hh in range(2)]
        for i in range(TILES + 2):
            if i < TILES:
                order += [("wo", i, 0, "d"), ("wo", i, 1, "d")]
            if 1 <= i <= TILES:
                order += [("x2t", i - 1, 0, "a"), ("x2t", i - 1, 1, "d")]
            if i >= 2:
                order += [("lg", i - 2, "d")]
        order += [("rank", "d"), ("count", "d"), ("bounds", "d"), ("table", "d")]
        index = {entry[:-1]: g for g, entry in enumerate(order)}
        seen = {"a": 0, "d": 0}
        freed_at = []
        for entry in order:
            seen[entry[-1]] += 1
            freed_at.append((entry[-1], seen[entry[-1]]))

        def bank_of(*key):
            return banks[:, index[key] % BANKS, :]

        def full(eng, *key):
            eng.wait_ge(filled, index[key] + 1)

        block = ctx.enter_context(nc.Block())

        def ada_load(q, n):
            if n >= 2:
                q.wait_ge(filled, index[("ada", n - 2)] + 1)
            q.dma_start(ada_s[:, n % 2, :, :], w_ada.rearrange("(p c) f -> p c f", c=CH)[:, :, n * HALF:(n + 1) * HALF]
                        ).then_inc(s_ada[n % 2], 16)

        @block.sync
        def _(sp):
            sp.dma_start(cst, consts).then_inc(s_cst, 16)
            sp.dma_start(ident, consts[:, C_ID:C_ID + P]).then_inc(s_cst, 16)
            sp.dma_start(c_col, c.rearrange("a (p c) -> p (a c)", c=CH)).then_inc(s_c, 16)
            for n in range(2):
                ada_load(sp, n)
            sp.dma_start(x_t[:, 0:4, :], x.rearrange("(t p) d -> p t d", p=P)[:, 0:4, :]).then_inc(s_x[0], 16)
            ada_load(sp, 2)
            sp.dma_start(x_t[:, 4:8, :], x.rearrange("(t p) d -> p t d", p=P)[:, 4:8, :]).then_inc(s_x[1], 16)
            ada_load(sp, 3)
            for part, (f0, f1) in enumerate(((0, 2 * CONV), (2 * CONV, 1024), (1024 + SGU, WIN), (1024, 1024 + SGU))):
                for h in range(2):
                    sp.dma_start(w_in_s[:, 4 * h:4 * h + 4, f0:f1],
                                 w_in[h * 512:(h + 1) * 512, f0:f1].rearrange("(p j) f -> p j f", j=4)
                                 ).then_inc(s_win[part], 16)
                if part < 2:
                    for n in (4 + 2 * part, 5 + 2 * part):
                        ada_load(sp, n)
            for n in range(8, 12):
                ada_load(sp, n)
            sp.wait_ge(filled, index[("ada", 11)] + 1)
            sp.dma_start(dft_s, dft).then_inc(s_dft, 16)
            sp.wait_ge(filled, index[("u", 2, 1)] + 1)
            sp.dma_start(w_out_s, w_out.rearrange("(c p) d -> p c d", p=P)).then_inc(s_wout, 16)
            sp.wait_ge(filled, index[("U", 1)] + 1)
            sp.dma_start(xr, x.rearrange("(t p) d -> p t d", p=P)).then_inc(s_xr, 16)
            sp.wait_ge(s_modout, 16 * 4 * 12)
            sp.wait_ge(filled, index[("sg", 2, 1)] + 1)
            sp.dma_start(gate1, mod_dram.ap()[2 * D:3 * D].partition_broadcast(P)).then_inc(s_gate1, 16)
            sp.dma_start(gate1_b, b_ada[2 * D:3 * D].partition_broadcast(P)).then_inc(s_gate1, 16)

            def up_load(e, slot, u):
                for h in range(2):
                    sp.dma_start(at(slot * EXPERT_FLOATS + u * 4096 + h * 2048, 4 * FF),
                                 (exp_w1, exp_w3)[u][bass.ds(e, 1), h * 512:(h + 1) * 512, :].rearrange("e (p j) f -> (e p) (j f)", j=4)
                                 ).then_inc(s_w[slot], 16)

            def down_load(e, slot):
                for h in range(2):
                    sp.dma_start(at(slot * EXPERT_FLOATS + 8192 + h * 2048, 2 * D),
                                 exp_w2[bass.ds(e, 1), h * 256:(h + 1) * 256, :].rearrange("e (p j) f -> (e p) (j f)", j=2)
                                 ).then_inc(s_w[slot], 16)

            def expert_load(e, slot):
                up_load(e, slot, 0)
                up_load(e, slot, 1)
                down_load(e, slot)

            sp.wait_ge(s_gnn, 6)
            up_load(0, 0, 1)
            down_load(0, 0)
            sp.wait_ge(filled, index[("wo", TILES - 1, 1)] + 1)
            expert_load(1, 1)
            for i in range(TILES):
                sp.wait_ge(s_x2, 2 * i + 2)
                sp.dma_start(x2_dram.ap()[i * P:(i + 1) * P, :], x2[:, i, :]).then_inc(s_x2st, 16)
            sp.wait_ge(s_tab, 1)
            up_load(0, 0, 0)
            sp.wait_ge(s_xs, 16 * 2 * TILES)
            expert_load(2, 2)
            sp.wait_ge(s_x2st, 16 * TILES)
            expert_load(3, 3)
            with sp.Fori(0, EXPERTS // SLOTS - 1) as r:
                for slot in range(SLOTS):
                    end = sp.value_load(table[0:1, bass.ds(r * SLOTS + (T_ENDS + 1 + slot), 1)], min_val=1, max_val=MAX_BLOCKS)
                    sp.wait_ge(s_yp, end)
                    expert_load(r * SLOTS + (SLOTS + slot), slot)
            end = sp.value_load(table[0:1, T_ENDS + EXPERTS - SLOTS + 1:T_ENDS + EXPERTS - SLOTS + 2], min_val=1, max_val=MAX_BLOCKS)
            sp.wait_ge(s_yp, end)
            sp.dma_start(at(0, TILES, D), x2_dram.ap().rearrange("(t p) d -> p t d", p=P)).then_inc(s_x2r, 16)
            sp.dma_start(at(8192, D), final_g.partition_broadcast(P)).then_inc(s_fg, 16)
            for i in range(TILES):
                sp.wait_ge(s_tout, i + 1)
                sp.dma_start(out[i * P:(i + 1) * P, :], at(3 * EXPERT_FLOATS + i * D, D)).then_inc(s_out, 16)
            sp.wait_ge(s_out, 16 * TILES)

        @block.gpsimd
        def _(pool):
            for r, vec in enumerate((conv_b, conv_gn_g, conv_gn_b, sgu_ln_g, sgu_ln_b)):
                pool.dma_start(vec_rows[3 * r:3 * r + 3, :], vec.rearrange("(a f) -> a f", f=P)).then_inc(s_vrows, 16)
            pool.dma_start(conv_rows[0:TAPS, 0:CONV], conv_w).then_inc(s_convw, 16)
            pool.dma_start(ws_rows, sgu_w.rearrange("h p q -> p h q")).then_inc(s_ws, 16)
            for n, vec in ((LN1, ln1_g), (LN2, ln2_g)):
                pool.dma_start(d_tile(col[:, n, :]), d_cols(vec)).then_inc(s_cols, 16)
            for n, m in ((BSH1, 0), (BSC1, 1), (BSH2, 3), (BSC2, 4)):
                pool.dma_start(d_tile(col[:, n, :]), d_cols(b_ada[m * D:(m + 1) * D])).then_inc(s_cols, 16)
            for h in range(6):
                pool.dma_start(bs_b[64 * (h % 2):64 * (h % 2) + 64, h // 2, :], sgu_b[h, :].partition_broadcast(64)).then_inc(s_small, 16)
            for h in range(2):
                pool.dma_start(router_s[:, 4 * h:4 * h + 4, :], router_w[h * 512:(h + 1) * 512, :].rearrange("(p j) e -> p j e", j=4)
                               ).then_inc(s_rb, 16)
            pool.dma_start(router_bb, router_b.partition_broadcast(P)).then_inc(s_rb, 16)
            pool.memset(pad_h[:, :, 0:PAD], 0.0).then_inc(s_zero, 1)
            pool.memset(pad_h[:, :, PAD + SEQ:PADW], 0.0).then_inc(s_zero, 1)
            for n in range(12):
                who, count = freed_at[index[("ada", n)]]
                pool.wait_ge(freed_a if who == "a" else freed_d, count)
                for q in range(4):
                    pool.dma_start(mod_dram.ap()[n * HALF + q * P:n * HALF + (q + 1) * P].rearrange("(a f) -> a f", a=1),
                                   mod_rows[32 * q:32 * q + 1, :]).then_inc(s_modout, 16)
                if n == 3:
                    pool.wait_ge(s_modout, 16 * 16)
                    for k, m in ((SH1, 0), (SC1, 1)):
                        pool.dma_start(d_tile(col[:, k, :]), d_cols(mod_dram.ap()[m * D:(m + 1) * D])).then_inc(s_modcols, 16)
            pool.wait_ge(s_modout, 16 * 48)
            for k, m in ((SH2, 3), (SC2, 4)):
                pool.dma_start(d_tile(col[:, k, :]), d_cols(mod_dram.ap()[m * D:(m + 1) * D])).then_inc(s_modcols, 16)
            pool.wait_ge(s_vn, TILES)
            pool.wait_ge(s_sg, 6)
            pool.wait_ge(s_gn, 6)
            for hh in range(2):
                for dst, src in ((gate2, mod_dram.ap()), (gate2_b, b_ada)):
                    pool.dma_start(dst[64 * hh:64 * hh + 64, :],
                                   src[5 * D + hh * HALF:5 * D + (hh + 1) * HALF].partition_broadcast(64)).then_inc(s_gate2, 16)
            pool.wait_ge(s_ss, 2 * TILES)
            pool.memset(scratch, 0.0).then_inc(s_pz, 1)
            pool.wait_ge(s_pz, 1)
            pool.dma_start(xs_dram.ap()[2 * SEQ:XS_ROWS, :], scratch[0:BLK, :]).then_inc(s_padz, 16)
            pool.wait_ge(s_rows, 1)
            for i in range(TILES):
                for k in range(2):
                    pool.indirect_dma_start(out=xs_dram.ap(), out_offset=bass.IndirectOffsetOnAxis(ap=rows_at[:, k, i:i + 1], axis=0),
                                            in_=xr[:, i, :], in_offset=None).then_inc(s_xs, 16)
            pool.wait_ge(s_tab, 1)
            blocks = pool.value_load(table[0:1, T_ENDS + EXPERTS:T_ENDS + EXPERTS + 1], min_val=EXPERTS, max_val=MAX_BLOCKS)
            pool.wait_ge(s_yzero, (MAX_BLOCKS + 1) * 16)
            pool.wait_ge(s_yst, blocks * 32)
            pool.sem_inc(s_through, 1)
            for i in range(TILES):
                for k in range(2):
                    pool.indirect_dma_start(out=at((k + 1) * EXPERT_FLOATS + i * D, D), out_offset=None, in_=ys_dram.ap(),
                                            in_offset=bass.IndirectOffsetOnAxis(ap=rows_at[:, 2 + k, i:i + 1], axis=0)
                                            ).then_inc(s_gat[i], 16)

        @block.tensor
        def _(pe):
            def begin(*key):
                g = index[key]
                if g >= BANKS:
                    who, count = freed_at[g - BANKS]
                    pe.wait_ge(freed_a if who == "a" else freed_d, count)
                return bank_of(*key)

            pe.wait_ge(s_cst, 32)
            ps = begin("small")
            pe.wait_ge(s_vrows, 16 * 5)
            pe.wait_ge(s_convw, 16)
            pe.transpose(ps[:, 0:15], vec_rows[0:15, :], ident[0:15, 0:15])
            for cc in range(3):
                last = pe.transpose(ps[:, 16 + cc * TAPS:16 + (cc + 1) * TAPS], conv_rows[0:TAPS, cc * P:(cc + 1) * P], ident[0:TAPS, 0:TAPS])
            last.then_inc(filled, 1)
            pe.wait_ge(s_ws, 16)
            for g in range(2):
                ps = begin("ws", g)
                for k in range(3):
                    h = 3 * g + k
                    last = pe.transpose(ps[:, k * P:(k + 1) * P], ws_rows[:, h, :], ident)
                last.then_inc(filled, 1)
            ps = begin("rs")
            full_d = freed_at[index[("ws", 1)]][1]
            pe.wait_ge(freed_d, full_d)
            for h in range(6):
                last = pe.matmul(ps[64 * (h % 2):64 * (h % 2) + 64, (h // 2) * P:(h // 2 + 1) * P], ones[:, 0:64], ws_t[:, h, :],
                                 start=True, stop=True, skip_group_check=True)
            last.then_inc(filled, 1)

            def ada(n):
                ps = begin("ada", n)
                if n == 0:
                    pe.wait_ge(s_cwide, 1)
                pe.wait_ge(s_ada[n % 2], 16 * (n // 2 + 1))
                for k in range(CH):
                    for q in range(4):
                        last = pe.matmul(ps[32 * q:32 * q + 32, 0:P], c_wide[:, k, :], ada_s[:, n % 2, k, q * P:(q + 1) * P],
                                         start=(k == 0), stop=(k == CH - 1), tile_position=(0, 32 * q))
                last.then_inc(filled, 1)

            for n in range(4):
                ada(n)
            for i in range(TILES):
                pe.wait_ge(s_xhat, i + 1)
                for h in range(2):
                    ps = begin("xt", i, h)
                    for j in range(4):
                        last = pe.transpose(ps[:, j * P:(j + 1) * P], x_t[:, i, 512 * h + j:512 * h + 512:4], ident)
                    last.then_inc(filled, 1)

            def h_ready(s):
                for h in range(2):
                    who, count = freed_at[index[("xt", 4 * s + 3, h)]]
                    pe.wait_ge(freed_a if who == "a" else freed_d, count)

            def z_cols(ps, f0, s):
                for k in range(CH):
                    last = pe.matmul(ps, w_in_s[:, k, f0:f0 + P], h_t[:, k, s * HALF:(s + 1) * HALF], start=(k == 0), stop=(k == CH - 1))
                last.then_inc(filled, 1)

            for g, entry in enumerate(order):
                key = entry[:-1]
                kind = key[0]
                if kind in ("small", "ws", "rs", "xt") or kind == "ada" and key[1] < 4:
                    continue
                if kind == "ada":
                    ada(key[1])
                    continue
                ps = begin(*key)
                if kind in ("g", "a"):
                    if g == index[("g", 0, 0)]:
                        pe.wait_ge(s_win[0], 32)
                    if key[1] == 0:
                        h_ready(key[2])
                    z_cols(ps, (CONV if kind == "g" else 0) + key[1] * P, key[2])
                elif kind == "b":
                    pe.wait_ge(s_win[1], 32)
                    z_cols(ps, 2 * CONV + key[1] * P, key[2])
                elif kind == "v":
                    pe.wait_ge(s_win[2], 32)
                    i = key[1]
                    for k in range(CH):
                        last = pe.matmul(ps[:, 0:SGU], h_t[:, k, i * P:(i + 1) * P], w_in_s[:, k, 1024 + SGU:WIN], start=(k == 0), stop=(k == CH - 1))
                    last.then_inc(filled, 1)
                elif kind == "u":
                    pe.wait_ge(s_win[3], 32)
                    z_cols(ps, 1024 + key[1] * P, key[2])
                elif kind == "pq":
                    i = key[1]
                    if i == 0:
                        pe.wait_ge(freed_a, freed_at[index[("b", 1, 1)]][1])
                    for cc in range(2):
                        last = pe.matmul(ps[:, cc * 256:(cc + 1) * 256], xt_four[:, cc, i * P:(i + 1) * P], cst[:, C_DFT:C_DFT + 256],
                                         start=True, stop=True, skip_group_check=True)
                    last.then_inc(filled, 1)
                elif kind in ("U", "V"):
                    pe.wait_ge(freed_a, freed_at[index[("pq", TILES - 1)]][1])
                    pe.wait_ge(s_dft, 16)
                    t = 0 if kind == "U" else 1
                    for k in range(TILES):
                        last = pe.matmul(ps, pq[:, k, key[1], t * P:(t + 1) * P], dft_s[:, t, k, :], start=(k == 0), stop=(k == TILES - 1))
                    last.then_inc(filled, 1)
                elif kind == "mid":
                    for cc in range(2):
                        for k in range(TILES):
                            last = pe.matmul(ps[:, cc:cc + 1], pq[:, k, cc, 0:P], cst[:, C_ALT:C_ALT + 1],
                                             start=(k == 0), stop=(k == TILES - 1), skip_group_check=True)
                    last.then_inc(filled, 1)
                elif kind == "gm":
                    pe.wait_ge(s_conv, TAPS * (key[1] + 1))
                    pe.matmul(ps, bd, y_t[:, key[1], key[2] * HALF:(key[2] + 1) * HALF], start=True, stop=True).then_inc(filled, 1)
                elif kind == "gv":
                    n = 2 * key[1] + key[2]
                    pe.wait_ge(s_gnsq, n + 1)
                    pe.matmul(ps, bd, squares[:, n, :], start=True, stop=True).then_inc(filled, 1)
                elif kind == "sg":
                    j, hh = key[1:]
                    pe.wait_ge(s_vn, 4 * hh + 4)
                    for i in range(4):
                        for e in range(2):
                            h = 2 * j + e
                            last = pe.matmul(ps[64 * e:64 * e + 64, i * P:(i + 1) * P], v_t[:, 4 * hh + i, h * 64:(h + 1) * 64], ws_t[:, h, :],
                                             start=True, stop=True, skip_group_check=True)
                    last.then_inc(filled, 1)
                elif kind == "wo":
                    i, s = key[1:]
                    if (i, s) == (0, 0):
                        pe.wait_ge(s_wout, 16)
                        pe.wait_ge(freed_d, freed_at[index[("U", 1)]][1])
                        pe.wait_ge(s_sg, 6)
                        pe.wait_ge(s_gn, 6)
                    for n, k in enumerate((3, 4, 5, 6, 7, 0, 1, 2)):
                        last = pe.matmul(ps, y_t[:, k, i * P:(i + 1) * P], w_out_s[:, k, s * HALF:(s + 1) * HALF], start=(n == 0), stop=(n == CH - 1))
                    last.then_inc(filled, 1)
                elif kind == "x2t":
                    i, h = key[1:]
                    pe.wait_ge(s_xhat, TILES + i + 1)
                    for j in range(4):
                        last = pe.transpose(ps[:, j * P:(j + 1) * P], xr[:, i, 512 * h + j:512 * h + 512:4], ident)
                    last.then_inc(filled, 1)
                elif kind == "lg":
                    i = key[1]
                    if i == 0:
                        pe.wait_ge(s_rb, 48)
                    for h in range(2):
                        who, count = freed_at[index[("x2t", i, h)]]
                        pe.wait_ge(freed_a if who == "a" else freed_d, count)
                    for k in range(CH):
                        last = pe.matmul(ps[:, 0:EXPERTS], h2_t[:, i % 2, k, :], router_s[:, k, :], start=(k == 0), stop=(k == CH - 1))
                    last.then_inc(filled, 1)
                elif kind == "rank":
                    pe.wait_ge(s_sums, 1)
                    pe.matmul(ps, tri, ranks, start=True, stop=False)
                    pe.matmul(ps, ones, before, start=False, stop=True).then_inc(filled, 1)
                elif kind == "count":
                    for i in range(TILES):
                        last = pe.matmul(ps[0:EXPERTS, 0:1], ranks[:, i * EXPERTS:(i + 1) * EXPERTS], ones[:, 0:1],
                                         start=(i == 0), stop=(i == TILES - 1))
                    last.then_inc(filled, 1)
                elif kind == "bounds":
                    pe.wait_ge(s_wide, 1)
                    pe.matmul(ps[:, 0:EXPERTS], nb_wide[0:EXPERTS, :], cst[0:EXPERTS, C_INC:C_INC + EXPERTS], start=True, stop=True, skip_group_check=True)
                    pe.matmul(ps[:, EXPERTS:2 * EXPERTS], nb_wide[0:EXPERTS, :], cst[0:EXPERTS, C_EXC:C_EXC + EXPERTS], start=True, stop=True, skip_group_check=True)
                    pe.matmul(ps[:, 2 * EXPERTS:3 * EXPERTS], ct_wide[0:EXPERTS, :], cst[0:EXPERTS, C_EXC:C_EXC + EXPERTS], start=True, stop=True, skip_group_check=True).then_inc(filled, 1)
                elif kind == "table":
                    pe.wait_ge(s_tabc, 1)
                    pe.matmul(ps[0:1, 0:P], tab_c, ident, start=True, stop=True).then_inc(filled, 1)

            xt_p, h_p, ft_p, y_p = (banks[:, b, :] for b in range(4))
            pe.wait_ge(s_tab, 1)

            def x_transposes(n):
                pe.wait_ge(s_xrow, (n + 1) * 32)
                for j in range(4):
                    last = pe.transpose(xt_p[:, j * P:(j + 1) * P], xrow[:, j:HALF:4], ident)
                last.then_inc(s_xtp, 1)

            def up(n, slot):
                w13 = at(slot * EXPERT_FLOATS, 2, CH, FF)
                for k in range(CH):
                    for q in range(2):
                        last = pe.matmul(h_p[64 * q:64 * q + 64, :].rearrange("p (a b) -> p a b", a=2), xt_s[:, k % 4, k // 4, :],
                                         w13[:, :, k, q * 256:(q + 1) * 256], start=(k == 0), stop=(k == CH - 1))
                last.then_inc(s_h13, 1)

            def down(n, slot):
                w2 = at(slot * EXPERT_FLOATS + 8192, 4, D)
                for k in range(4):
                    hidden = (k % 2) * P + (k // 2) * BLK
                    for q in range(2):
                        last = pe.matmul(y_p[64 * q:64 * q + 64, :], ff_t[:, hidden:hidden + BLK],
                                         w2[:, k, q * HALF:(q + 1) * HALF], start=(k == 0), stop=(k == 3))
                last.then_inc(s_yp, 1)

            x_transposes(0)
            with pe.Fori(0, EXPERTS // SLOTS) as r:
                for slot in range(SLOTS):
                    lo = pe.value_load(table[0:1, bass.ds(r * SLOTS + (T_ENDS + slot), 1)], min_val=0, max_val=MAX_BLOCKS - 1)
                    hi = pe.value_load(table[0:1, bass.ds(r * SLOTS + (T_ENDS + slot + 1), 1)], min_val=1, max_val=MAX_BLOCKS)
                    pe.wait_ge(s_w[slot], (r + 1) * 96)
                    pe.sem_inc(s_begun, 1)
                    with pe.Fori(lo, hi) as n:
                        pe.wait_ge(s_xts, n + 1)
                        up(n, slot)
                        x_transposes(n + 1)
                        pe.wait_ge(s_ff, n + 1)
                        for j in range(2):
                            last = pe.transpose(ft_p[:, j * P:(j + 1) * P], ff[:, j:256:2], ident)
                        last.then_inc(s_ftp, 1)
                        pe.wait_ge(s_ft, n + 1)
                        pe.wait_ge(s_y, n + 1)
                        down(n, slot)

        @block.scalar
        def _(act):
            def begin(*key):
                full(act, *key)
                return bank_of(*key)

            def root(dst, src, sums):
                act.wait_ge(s_ss, sums)
                nc.scalar.activation(dst, src, ACT.Sqrt, bias=eps, scale=1.0 / D).then_inc(s_std, 1)

            act.wait_ge(s_eps, 1)
            act.wait_ge(s_c, 16)
            nc.scalar.activation(c_act, c_col, ACT.Silu).then_inc(s_cact, 1)
            for i in range(TILES):
                if i % 4 == 0:
                    act.wait_ge(s_x[i // 4], 16)
                if i:
                    act.wait_ge(s_ss, i)
                nc.scalar.activation(scratch, x_t[:, i, :], ACT.Square, accum_out=ss[:, 0, i:i + 1]).then_inc(s_ss, 1)
                if i % 4 == 3:
                    root(rstd[:, 0, i - 3:i + 1], ss[:, 0, i - 3:i + 1], i + 1)
            act.wait_ge(s_ab, 1)
            for entry in order:
                if entry[-1] != "a":
                    continue
                key = entry[:-1]
                kind = key[0]
                if kind in ("V", "gv", "x2t"):
                    break
                ps = begin(*key)
                if kind == "xt":
                    i, h = key[1:]
                    for j in range(4):
                        k = 4 * h + j
                        last = nc.scalar.activation(h_t[:, k, i * P:(i + 1) * P], ps[:, j * P:(j + 1) * P], ACT.Identity,
                                                    bias=ab[:, 1, k:k + 1], scale=ab[:, 0, k:k + 1])
                elif kind == "g":
                    n = 2 * key[1] + key[2]
                    if n >= 2:
                        act.wait_ge(freed_d, freed_at[index[("a", (n - 2) // 2, n % 2)]][1])
                    last = nc.scalar.activation((tmp_a, tmp_b)[n % 2], ps, ACT.Sigmoid)
                elif kind == "ada":
                    act.wait_ge(s_modout, 64 * key[1])
                    last = nc.scalar.activation(mod_rows, ps[:, 0:P], ACT.Copy)
                elif kind == "b":
                    last = nc.scalar.activation(xt_four[:, key[1], key[2] * HALF:(key[2] + 1) * HALF], ps, ACT.Copy)
                elif kind == "v":
                    last = nc.scalar.activation(v_t[:, key[1], :], ps[:, 0:SGU], ACT.Gelu_apprx_tanh)
                elif kind == "u":
                    last = nc.scalar.activation(y_t[:, 5 + key[1], key[2] * HALF:(key[2] + 1) * HALF], ps, ACT.Gelu_apprx_tanh)
                elif kind == "pq":
                    last = nc.scalar.activation(pq[:, key[1], :, :].rearrange("p a b -> p (a b)"), ps, ACT.Copy)
                last.then_inc(freed_a, 1)

            def gn_squares(n):
                act.wait_ge(freed_d, freed_at[index[("gm", n // 2, n % 2)]][1])
                act.wait_ge(s_conv, 3 * TAPS)
                nc.scalar.activation(squares[:, n, :], y_t[:, n // 2, (n % 2) * HALF:(n % 2 + 1) * HALF], ACT.Square).then_inc(s_gnsq, 1)

            def gn_silu(n):
                act.wait_ge(s_gnn, n + 1)
                cc, part = n // 2, y_t[:, n // 2, (n % 2) * HALF:(n % 2 + 1) * HALF]
                nc.scalar.activation(part, part, ACT.Silu, bias=vecs[:, 6 + cc:7 + cc], scale=vecs[:, 3 + cc:4 + cc]).then_inc(s_gn, 1)

            def fourier_sin(cc):
                ps = begin("V", cc)
                nc.scalar.activation(scratch[:, cc * HALF:(cc + 1) * HALF], ps, ACT.Copy).then_inc(freed_a, 1)

            def gn_root(n):
                ps = begin("gv", n // 2, n % 2)
                nc.scalar.activation(squares[:, n, :], ps, ACT.Sqrt, bias=eps).then_inc(freed_a, 1)

            act.wait_ge(s_mv, 1)
            nc.scalar.activation(v_rstd, v_rstd, ACT.Sqrt, bias=eps).then_inc(s_vstd, 1)
            for n in range(3):
                gn_squares(n)
            fourier_sin(0)
            for n in range(3, 6):
                gn_squares(n)
            for n in range(3):
                gn_root(n)
            fourier_sin(1)
            for n in range(3, 6):
                gn_root(n)
            for n in range(6):
                gn_silu(n)
            act.wait_ge(freed_d, freed_at[index[("U", 1)]][1])
            act.wait_ge(s_ab, 2)
            for i in range(TILES + 1):
                if i < TILES:
                    act.wait_ge(s_x2, 2 * i + 2)
                    act.wait_ge(s_ss, TILES + i)
                    nc.scalar.activation(scratch, x2[:, i, :], ACT.Square, accum_out=ss[:, 1, i:i + 1]).then_inc(s_ss, 1)
                    root(rstd[:, 1, i:i + 1], ss[:, 1, i:i + 1], TILES + i + 1)
                if i >= 1:
                    ps = begin("x2t", i - 1, 0)
                    if i >= 3:
                        act.wait_ge(filled, index[("lg", i - 3)] + 1)
                    for j in range(4):
                        last = nc.scalar.activation(h2_t[:, (i - 1) % 2, j, :], ps[:, j * P:(j + 1) * P], ACT.Identity,
                                                    bias=ab[:, 3, j:j + 1], scale=ab[:, 2, j:j + 1])
                    last.then_inc(freed_a, 1)
            act.wait_ge(s_expin, 1)
            nc.scalar.activation(prob, prob, ACT.Exp).then_inc(s_exp, 1)

            act.wait_ge(s_tab, 1)
            act.wait_ge(s_xs, 16 * 2 * TILES)
            act.wait_ge(s_padz, 16)

            def rows_in(n):
                start = act.value_load(table[0:1, bass.ds(n + T_ROWS, 1)], min_val=0, max_val=2 * SEQ)
                for h in range(2):
                    act.dma_start(xrow[64 * h:64 * h + 64, :], xs_dram.ap()[bass.ds(start, BLK), h * HALF:(h + 1) * HALF]).then_inc(s_xrow, 16)

            def silu(n):
                act.wait_ge(s_h13, n + 1)
                nc.scalar.activation(ff_silu, banks[:, 1, 0:256], ACT.Silu).then_inc(s_silu, 1)

            def hidden_copy(n):
                act.wait_ge(s_ftp, n + 1)
                nc.scalar.activation(ff_t, banks[:, 2, 0:256], ACT.Copy).then_inc(s_ft, 1)

            def result_out(n):
                act.wait_ge(s_y, n + 2)
                for h in range(2):
                    act.dma_start(ys_dram.ap()[bass.ds(n * BLK, BLK), h * HALF:(h + 1) * HALF], y_s[64 * h:64 * h + 64, :]).then_inc(s_yst, 16)

            def rows_next(n):
                act.wait_ge(s_xtp, n)
                rows_in(n)

            rows_in(0)
            rows_next(1)
            blocks = act.value_load(table[0:1, T_ENDS + EXPERTS:T_ENDS + EXPERTS + 1], min_val=EXPERTS, max_val=MAX_BLOCKS)
            with act.Fori(blocks, MAX_BLOCKS + 1) as n:
                act.dma_start(ys_dram.ap()[bass.ds(n * BLK, BLK), :], xs_dram.ap()[2 * SEQ:XS_ROWS, :]).then_inc(s_yzero, 16)
            with act.Fori(0, blocks) as n:
                act.sem_inc(s_yzero, 16)
                silu(n)
                rows_next(n + 2)
                hidden_copy(n)
                result_out(n)
            act.wait_ge(s_xrow, (blocks + 2) * 32)

            for i in range(TILES + 1):
                if i < TILES:
                    act.wait_ge(s_gat[i], 32)
                    first = at(EXPERT_FLOATS + i * D, D)
                    nc.scalar.activation(first, first, ACT.Copy, scale=gate_w[:, 0, i:i + 1]).then_inc(s_t1, 1)
                if i >= 1:
                    act.wait_ge(s_t3, i)
                    act.wait_ge(s_ss, 2 * TILES + i - 1)
                    nc.scalar.activation(scratch, at(3 * EXPERT_FLOATS + (i - 1) * D, D), ACT.Square,
                                         accum_out=ss[:, 2, i - 1:i]).then_inc(s_ss, 1)
                    root(rstd[:, 2, i - 1:i], ss[:, 2, i - 1:i], 2 * TILES + i)

        @block.vector
        def _(dve):
            steps = [0]

            def link(ins):
                steps[0] += 1
                ins.then_inc(s_link, 1)
                dve.wait_ge(s_link, steps[0])

            def begin(*key):
                full(dve, *key)
                return bank_of(*key)

            def wide(view, *shape):
                return view.broadcast_to(list(shape))

            v = nc.vector
            v.memset(eps, EPS).then_inc(s_eps, 1)
            dve.wait_ge(s_cact, 1)
            v.tensor_copy(c_wide, c_act.unsqueeze(2).broadcast_to([P, CH, 32])).then_inc(s_cwide, 1)
            ps = begin("small")
            v.tensor_copy(vecs[:, 0:15], ps[:, 0:15])
            v.tensor_copy(conv_t, ps[:, 16:16 + 3 * TAPS]).then_inc(freed_d, 1)
            for g in range(2):
                ps = begin("ws", g)
                v.tensor_copy(ws_t[:, 3 * g:3 * g + 3, :], ps[:, 0:3 * P].rearrange("p (h q) -> p h q", h=3)).then_inc(freed_d, 1)
            ps = begin("rs")
            dve.wait_ge(s_small, 16 * 6)
            dve.wait_ge(freed_d, 1)
            for j in range(3):
                last = v.scalar_tensor_tensor(gain_k[:, j, :], ps[:, j * P:(j + 1) * P], vecs[:, 12 + j:13 + j], bs_b[:, j, :], ALU.mult, ALU.add)
            last.then_inc(freed_d, 1)
            for n in range(4):
                ps = begin("ada", n)
                if n:
                    dve.wait_ge(s_modout, 64 * n)
                v.tensor_copy(mod_rows, ps[:, 0:P]).then_inc(freed_d, 1)

            def affine(a, b, scale, b_scale, shift, b_shift, gain):
                link(v.tensor_tensor(ab[:, a, :], col[:, scale, :], col[:, b_scale, :], ALU.add))
                link(v.scalar_tensor_tensor(ab[:, a, :], ab[:, a, :], 1.0, col[:, gain, :], ALU.add, ALU.mult))
                v.tensor_tensor(ab[:, b, :], col[:, shift, :], col[:, b_shift, :], ALU.add).then_inc(s_ab, 1)

            dve.wait_ge(s_cols, 16 * 6)
            dve.wait_ge(s_modcols, 32)
            affine(0, 1, SC1, BSC1, SH1, BSH1, LN1)
            dve.wait_ge(s_ab, 1)
            for i in range(TILES + 1):
                if i < TILES:
                    if i % 4 == 0:
                        dve.wait_ge(s_std, i // 4 + 1)
                        link(v.reciprocal(rstd[:, 0, i:i + 4], rstd[:, 0, i:i + 4]))
                    v.tensor_scalar(x_t[:, i, :], x_t[:, i, :], rstd[:, 0, i:i + 1], None, ALU.mult).then_inc(s_xhat, 1)
                if i >= 1:
                    ps = begin("xt", i - 1, 1)
                    for j in range(4):
                        last = v.tensor_scalar(h_t[:, 4 + j, (i - 1) * P:i * P], ps[:, j * P:(j + 1) * P],
                                               ab[:, 0, 4 + j:5 + j], ab[:, 1, 4 + j:5 + j], ALU.mult, ALU.add)
                    last.then_inc(freed_d, 1)

            for cc in range(3):
                for s in range(2):
                    ps = begin("a", cc, s)
                    dve.wait_ge(freed_a, freed_at[index[("g", cc, s)]][1])
                    v.tensor_tensor(pad_h[:, cc, PAD + s * HALF:PAD + (s + 1) * HALF], ps, (tmp_a, tmp_b)[s], ALU.mult).then_inc(freed_d, 1)
                dve.wait_ge(s_zero, 2)
                dve.wait_ge(freed_d, freed_at[index[("a", cc, 1)]][1])
                for k in range(TAPS):
                    src, w = pad_h[:, cc, k:k + SEQ], conv_t[:, cc * TAPS + k:cc * TAPS + k + 1]
                    if k == 0:
                        ins = v.tensor_scalar(y_t[:, cc, :], src, w, vecs[:, cc:cc + 1], ALU.mult, ALU.add)
                    else:
                        dve.wait_ge(s_conv, cc * TAPS + k)
                        ins = v.scalar_tensor_tensor(y_t[:, cc, :], src, w, y_t[:, cc, :], ALU.mult, ALU.add)
                    ins.then_inc(s_conv, 1)

            for i in range(TILES):
                dve.wait_ge(freed_a, freed_at[index[("v", i)]][1])
                last = v.bn_stats(stats[:, i, :], v_t[:, i, :])
            link(last)
            for i in range(TILES):
                last = v.bn_aggr(mv[:, i, :], stats[:, i, :])
            link(last)
            v.tensor_copy(v_rstd, mv[:, :, 1]).then_inc(s_mv, 1)
            dve.wait_ge(s_vstd, 1)
            link(v.reciprocal(v_rstd, v_rstd))
            for i in range(TILES):
                v.tensor_scalar(v_t[:, i, :], v_t[:, i, :], mv[:, i, 0:1], v_rstd[:, i:i + 1], ALU.subtract, ALU.mult).then_inc(s_vn, 1)

            def centre(n):
                ps = begin("gm", n // 2, n % 2)
                part = y_t[:, n // 2, (n % 2) * HALF:(n % 2 + 1) * HALF]
                v.tensor_tensor(part, part, ps, ALU.subtract).then_inc(freed_d, 1)

            def gn_scale(n):
                part = y_t[:, n // 2, (n % 2) * HALF:(n % 2 + 1) * HALF]
                dve.wait_ge(freed_a, freed_at[index[("gv", n // 2, n % 2)]][1])
                link(v.reciprocal(squares[:, n, :], squares[:, n, :]))
                v.tensor_tensor(part, part, squares[:, n, :], ALU.mult).then_inc(s_gnn, 1)

            def fourier(cc):
                ps = begin("U", cc)
                sin = scratch[:, cc * HALF:(cc + 1) * HALF]
                dve.wait_ge(freed_a, freed_at[index[("V", cc)]][1])
                v.tensor_tensor(y_t[:, 3 + cc, 0:HALF], ps, sin, ALU.subtract)
                v.tensor_tensor(y_t[:, 3 + cc, SEQ - 1:HALF:-1], ps[:, 1:HALF], sin[:, 1:HALF], ALU.add).then_inc(freed_d, 1)

            dve.wait_ge(s_conv, 3 * TAPS)
            for n in range(3):
                centre(n)
            fourier(0)
            ps = begin("mid")
            for cc in range(2):
                last = v.tensor_copy(y_t[:, 3 + cc, HALF:HALF + 1], ps[:, cc:cc + 1])
            last.then_inc(freed_d, 1)
            for n in range(3, 6):
                centre(n)
            for n in range(3):
                gn_scale(n)
            fourier(1)
            for n in range(3, 6):
                gn_scale(n)
            for n in range(6):
                j, hh = n // 2, n % 2
                ps = begin("sg", j, hh)
                t = (tmp_a, tmp_b)[n % 2]
                if n < 2:
                    dve.wait_ge(s_gnn, 6)
                else:
                    dve.wait_ge(s_sg, n - 1)
                v.scalar_tensor_tensor(t.rearrange("p (a b) -> p a b", a=4), ps.rearrange("p (a b) -> p a b", a=4), vecs[:, 9 + j:10 + j],
                                       gain_k[:, j, :].unsqueeze(1).broadcast_to([P, 4, P]), ALU.mult, ALU.add).then_inc(freed_d, 1)
                dve.wait_ge(freed_d, freed_at[index[("sg", j, hh)]][1])
                part = y_t[:, 5 + j, hh * HALF:(hh + 1) * HALF]
                v.tensor_tensor(part, part, t, ALU.mult).then_inc(s_sg, 1)
            dve.wait_ge(s_modcols, 64)
            affine(2, 3, SC2, BSC2, SH2, BSH2, LN2)
            dve.wait_ge(s_ab, 2)
            v.tensor_copy(ab_jh[:, 0, :, :], ab[:, 2, :].rearrange("p (h j) -> p j h", h=2))
            v.tensor_copy(ab_jh[:, 1, :, :], ab[:, 3, :].rearrange("p (h j) -> p j h", h=2))
            dve.wait_ge(s_gate1, 32)
            link(v.tensor_tensor(gate1, gate1, gate1_b, ALU.add))
            dve.wait_ge(s_xr, 16)
            for i in range(TILES + 2):
                if i < TILES:
                    for s in range(2):
                        ps = begin("wo", i, s)
                        part = x2[:, i, s * HALF:(s + 1) * HALF]
                        v.tensor_tensor(part, ps, gate1[:, s * HALF:(s + 1) * HALF], ALU.mult).then_inc(freed_d, 1)
                        dve.wait_ge(freed_d, freed_at[index[("wo", i, s)]][1])
                        v.tensor_tensor(part, part, xr[:, i, s * HALF:(s + 1) * HALF], ALU.add).then_inc(s_x2, 1)
                if 1 <= i <= TILES:
                    ps = begin("x2t", i - 1, 1)
                    if i >= 3:
                        dve.wait_ge(filled, index[("lg", i - 3)] + 1)
                    for j in range(4):
                        last = v.tensor_scalar(h2_t[:, (i - 1) % 2, 4 + j, :], ps[:, j * P:(j + 1) * P],
                                               ab[:, 2, 4 + j:5 + j], ab[:, 3, 4 + j:5 + j], ALU.mult, ALU.add)
                    last.then_inc(freed_d, 1)
                if i >= 2:
                    ps = begin("lg", i - 2)
                    v.tensor_copy(logit[:, (i - 2) * EXPERTS:(i - 1) * EXPERTS], ps[:, 0:EXPERTS]).then_inc(freed_d, 1)
                if i < TILES:
                    dve.wait_ge(s_std, 2 + i + 1)
                    link(v.reciprocal(rstd[:, 1, i:i + 1], rstd[:, 1, i:i + 1]))
                    v.tensor_scalar(xr[:, i, :], x2[:, i, :], rstd[:, 1, i:i + 1], None, ALU.mult).then_inc(s_xhat, 1)

            def te(view):
                return view.rearrange("p (t e) -> p t e", t=TILES)

            def tge(view):
                return view.rearrange("p (g e) -> p g e", e=PER)

            def tg(view):
                return view.rearrange("p (t g) -> p t g", t=TILES)

            def over_e(view, n=EXPERTS):
                return view.unsqueeze(2).broadcast_to([P, TILES, n])

            def over_pe(view):
                return view.unsqueeze(2).broadcast_to([P, TILES * GROUPS, PER])

            def over_t(view, n=EXPERTS):
                return view.unsqueeze(1).broadcast_to([P, TILES, n])

            dve.wait_ge(freed_d, freed_at[index[("lg", TILES - 1)]][1])
            link(v.tensor_reduce(tok[:, 0, :], te(logit), AX_X, ALU.max))
            v.tensor_tensor(te(prob), te(logit), over_e(tok[:, 0, :]), ALU.subtract).then_inc(s_expin, 1)
            dve.wait_ge(s_exp, 1)
            link(v.tensor_reduce(tok[:, 1, :], te(prob), AX_X, ALU.add))
            link(v.reciprocal(tok[:, 1, :], tok[:, 1, :]))
            link(v.tensor_tensor(te(prob), te(prob), over_e(tok[:, 1, :]), ALU.mult))
            dve.wait_ge(s_rb, 48)
            link(v.tensor_tensor(te(sel), te(prob), over_t(router_bb), ALU.add))

            def first_best(values, top, hot, where):
                link(v.tensor_reduce(top, tge(values), AX_X, ALU.max))
                link(v.tensor_tensor(tge(cand), tge(values), over_pe(top), ALU.is_equal))
                link(v.tensor_tensor(te(cand), te(cand), over_t(cst[:, C_REV:C_REV + EXPERTS]), ALU.mult))
                link(v.tensor_reduce(where, tge(cand), AX_X, ALU.max))
                link(v.tensor_tensor(tge(hot), tge(cand), over_pe(where), ALU.is_equal))

            first_best(sel, best[:, 0, :], hot1, best[:, 1, :])
            link(v.scalar_tensor_tensor(sel2, hot1, NEG, sel, ALU.mult, ALU.add))
            first_best(sel2, best[:, 2, :], hot2, best[:, 3, :])
            link(v.tensor_tensor(best[:, 4, :], best[:, 0, :], best[:, 2, :], ALU.add))
            link(v.tensor_reduce(tok[:, 0, :], tg(best[:, 4, :]), AX_X, ALU.max))
            link(v.tensor_tensor(tg(best[:, 5, :]), tg(best[:, 4, :]), over_e(tok[:, 0, :], GROUPS), ALU.is_equal))
            link(v.tensor_tensor(tg(best[:, 5, :]), tg(best[:, 5, :]), over_t(cst[:, C_GREV:C_GREV + GROUPS], GROUPS), ALU.mult))
            link(v.tensor_reduce(tok[:, 1, :], tg(best[:, 5, :]), AX_X, ALU.max))
            link(v.tensor_tensor(tg(best[:, 6, :]), tg(best[:, 5, :]), over_e(tok[:, 1, :], GROUPS), ALU.is_equal))
            link(v.tensor_tensor(tge(hot1), tge(hot1), over_pe(best[:, 6, :]), ALU.mult))
            link(v.tensor_tensor(tge(hot2), tge(hot2), over_pe(best[:, 6, :]), ALU.mult))
            link(v.tensor_tensor(ranks, hot1, hot2, ALU.add))
            v.memset(before[:, 0:EXPERTS], 0.0)
            link(v.tensor_copy(before[:, EXPERTS:2 * EXPERTS], ranks[:, 0:EXPERTS]))
            for i in range(2, TILES):
                ins = v.tensor_tensor(before[:, i * EXPERTS:(i + 1) * EXPERTS], before[:, (i - 1) * EXPERTS:i * EXPERTS],
                                      ranks[:, (i - 1) * EXPERTS:i * EXPERTS], ALU.add)
                if i < TILES - 1:
                    link(ins)
            ins.then_inc(s_sums, 1)

            def picked(dst, values, hot):
                link(v.tensor_tensor(cand, values, hot, ALU.mult))
                link(v.tensor_reduce(dst, te(cand), AX_X, ALU.add))

            picked(tok[:, 2, :], prob, hot1)
            picked(tok[:, 3, :], prob, hot2)
            link(v.tensor_tensor(tok[:, 4, :], tok[:, 2, :], tok[:, 3, :], ALU.add))
            link(v.reciprocal(tok[:, 4, :], tok[:, 4, :]))
            v.tensor_tensor(gate_w[:, 0, :], tok[:, 2, :], tok[:, 4, :], ALU.mult)
            v.tensor_tensor(gate_w[:, 1, :], tok[:, 3, :], tok[:, 4, :], ALU.mult)
            ps_rank = begin("rank")
            v.tensor_copy(sel, ps_rank).then_inc(freed_d, 1)
            ps = begin("count")
            link(v.tensor_copy(cnt[0:EXPERTS, 0:1], ps[0:EXPERTS, 0:1]))
            link(v.tensor_scalar(best[0:EXPERTS, 7, 0:16], cst[0:EXPERTS, C_THR:C_THR + 16], cnt[0:EXPERTS, 0:1], None, ALU.is_lt))
            link(v.tensor_reduce(cnt[0:EXPERTS, 1:2], best[0:EXPERTS, 7, 0:16], AX_X, ALU.add))
            link(v.tensor_scalar(cnt[0:EXPERTS, 1:2], cnt[0:EXPERTS, 1:2], 1.0, None, ALU.add))
            v.tensor_scalar(ct_wide[0:EXPERTS, :], ones[0:EXPERTS, :], cnt[0:EXPERTS, 0:1], None, ALU.mult).then_inc(freed_d, 1)
            v.tensor_scalar(nb_wide[0:EXPERTS, :], ones[0:EXPERTS, :], cnt[0:EXPERTS, 1:2], None, ALU.mult).then_inc(s_wide, 1)
            ps = begin("bounds")
            v.tensor_copy(bounds, ps[:, 0:3 * EXPERTS].rearrange("p (a e) -> p a e", a=3)).then_inc(freed_d, 1)
            dve.wait_ge(freed_d, freed_at[index[("bounds",)]][1])
            ends, first_block, first_row = (bounds[:, k, :] for k in range(3))
            link(v.tensor_tensor(te(sel2), te(sel), over_t(first_row), ALU.add))
            picked(tok[:, 5, :], sel2, hot1)
            picked(tok[:, 6, :], sel2, hot2)
            v.tensor_copy(rows_at[:, 0, :], tok[:, 5, :])
            v.tensor_copy(rows_at[:, 1, :], tok[:, 6, :]).then_inc(s_rows, 1)
            number, number64 = cst[:, C_P:C_P + 1], cst[:, C_P64:C_P64 + 1]
            link(v.tensor_scalar(in_tmp, first_block, number, None, ALU.is_le))
            link(v.scalar_tensor_tensor(in_block, ends, number, in_tmp, ALU.is_gt, ALU.mult))
            link(v.scalar_tensor_tensor(in_tmp, first_block, -float(BLK), first_row, ALU.mult, ALU.add))
            link(v.tensor_tensor(in_tmp, in_tmp, in_block, ALU.mult))
            link(v.tensor_reduce(tab_c, in_tmp, AX_X, ALU.add))
            v.tensor_scalar(tab_c, tab_c, number64, float(2 * SEQ), ALU.add, ALU.min).then_inc(s_tabc, 1)
            ps = begin("table")
            v.tensor_copy(table[0:1, T_ROWS:T_ROWS + P], ps[0:1, 0:P]).then_inc(freed_d, 1)
            v.tensor_copy(table[0:1, T_ENDS + 1:T_ROWS], ends[0:1, :])
            v.memset(table[0:1, T_ENDS:T_ENDS + 1], 0)
            link(v.scalar_tensor_tensor(te(before), over_t(first_block), float(BLK), te(sel), ALU.mult, ALU.add))
            picked(tok[:, 7, :], before, hot1)
            picked(tok[:, 0, :], before, hot2)
            v.tensor_copy(rows_at[:, 2, :], tok[:, 7, :])
            v.tensor_copy(rows_at[:, 3, :], tok[:, 0, :])
            dve.wait_ge(s_gate2, 64)
            link(v.tensor_tensor(gate2, gate2, gate2_b, ALU.add))
            link(v.memset(tok[:, 1, :], 0.0))
            v.memset(tok[:, 1, :], 0.0).then_inc(s_y, 1)
            v.memset(tok[:, 2, :], 0.0).then_inc(s_tab, 1)

            def x_ready(n, first=False):
                dve.wait_ge(s_xtp, n + 1)
                if not first:
                    dve.wait_ge(s_h13, n)
                xt_v = xt_s.rearrange("p j h t -> p (j h) t")
                v.tensor_tensor(xt_v, banks[:, 0, :].rearrange("p (a t) -> p a t", a=CH),
                                ab_jh[:, 0, :, :].rearrange("p j h -> p (j h)").unsqueeze(2).broadcast_to([P, CH, BLK]), ALU.mult).then_inc(s_xtm, 1)
                dve.wait_ge(s_xtm, n + 1)
                v.tensor_tensor(xt_v, xt_v, ab_jh[:, 1, :, :].rearrange("p j h -> p (j h)").unsqueeze(2).broadcast_to([P, CH, BLK]), ALU.add).then_inc(s_xts, 1)

            def hidden(n):
                dve.wait_ge(s_silu, n + 1)
                v.tensor_tensor(ff, ff_silu, banks[:, 1, 256:HALF], ALU.mult).then_inc(s_ff, 1)

            def result(n, first=False):
                dve.wait_ge(s_yp, n + 1)
                if not first:
                    dve.wait_ge(s_yst, n * 32)
                v.tensor_tensor(y_s, banks[:, 3, :], gate2, ALU.mult).then_inc(s_y, 1)

            x_ready(0, True)
            hidden(0)
            x_ready(1)
            result(0, True)
            blocks = dve.value_load(table[0:1, T_ENDS + EXPERTS:T_ENDS + EXPERTS + 1], min_val=EXPERTS, max_val=MAX_BLOCKS)
            with dve.Fori(1, blocks) as n:
                hidden(n)
                x_ready(n + 1)
                result(n)

            dve.wait_ge(s_x2r, 16)
            dve.wait_ge(s_fg, 16)
            for i in range(TILES + 1):
                if i < TILES:
                    total_i = at(3 * EXPERT_FLOATS + i * D, D)
                    dve.wait_ge(s_t1, i + 1)
                    v.scalar_tensor_tensor(total_i, at(2 * EXPERT_FLOATS + i * D, D), gate_w[:, 1, i:i + 1], at(EXPERT_FLOATS + i * D, D),
                                           ALU.mult, ALU.add).then_inc(s_t2, 1)
                    dve.wait_ge(s_t2, i + 1)
                    v.tensor_tensor(total_i, total_i, at(i * D, D), ALU.add).then_inc(s_t3, 1)
                if i >= 1:
                    dve.wait_ge(s_std, 2 + TILES + i)
                    link(v.reciprocal(rstd[:, 2, i - 1:i], rstd[:, 2, i - 1:i]))
                    total_i = at(3 * EXPERT_FLOATS + (i - 1) * D, D)
                    v.scalar_tensor_tensor(total_i, total_i, rstd[:, 2, i - 1:i], at(8192, D), ALU.mult, ALU.mult).then_inc(s_tout, 1)


def kernel(x, c, ln1_g, ln2_g, w_ada, b_ada, w_in, w_out, conv_w, conv_b, conv_gn_g, conv_gn_b,
           sgu_ln_g, sgu_ln_b, sgu_w, sgu_b, router_w, router_b, exp_w1, exp_w3, exp_w2, final_g):
    import numpy as np
    from concourse import bacc
    from concourse.bass_utils import run_bass_kernel_spmd

    p = np.arange(P)
    consts = np.zeros((P, C_END), np.float32)
    consts[:, C_ID:C_ID + P] = np.eye(P)
    consts[:, C_TRI:C_TRI + P] = p[:, None] < p[None, :]
    consts[:, C_ONE:C_ONE + P] = 1.0
    consts[:, C_BD:C_BD + P] = (p[:, None] // 64 == p[None, :] // 64) / 64.0
    angle = 2 * np.pi * ((p[:, None] % 64) * (p[None, :] % 64) % 64) / 64.0
    same = (p[:, None] // 64 == p[None, :] // 64) / np.sqrt(64.0 * SEQ)
    consts[:, C_DFT:C_DFT + P] = np.cos(angle) * same
    consts[:, C_DFT + P:C_DFT + 2 * P] = np.sin(angle) * same
    e = np.arange(EXPERTS)
    consts[0:EXPERTS, C_EXC:C_EXC + EXPERTS] = e[:, None] < e[None, :]
    consts[0:EXPERTS, C_INC:C_INC + EXPERTS] = e[:, None] <= e[None, :]
    consts[:, C_REV:C_REV + EXPERTS] = PER - e % PER
    consts[:, C_GREV:C_GREV + GROUPS] = GROUPS - np.arange(GROUPS)
    consts[:, C_THR:C_THR + 16] = BLK * (1 + np.arange(16))
    consts[:, C_P] = p
    consts[:, C_P64] = BLK * p
    consts[:, C_ALT] = 1.0 - 2.0 * (p % 2)
    pos = np.arange(SEQ)
    turn = 2 * np.pi * (pos[:, None] * np.arange(HALF)[None, :] % SEQ) / SEQ
    dft = np.stack([np.cos(turn), np.sin(turn)]).astype(np.float32).reshape(2, TILES, P, HALF)
    dft = np.ascontiguousarray(dft.transpose(2, 0, 1, 3))

    inputs = dict(x=x[0], c=c, ln1_g=ln1_g[0], ln2_g=ln2_g[0], w_ada=w_ada[0], b_ada=b_ada[0], w_in=w_in[0], w_out=w_out[0],
                  conv_w=conv_w[0], conv_b=conv_b[0], conv_gn_g=conv_gn_g[0], conv_gn_b=conv_gn_b[0], sgu_ln_g=sgu_ln_g[0],
                  sgu_ln_b=sgu_ln_b[0], sgu_w=sgu_w[0], sgu_b=sgu_b[0], router_w=router_w, router_b=router_b,
                  exp_w1=exp_w1[0], exp_w3=exp_w3[0], exp_w2=exp_w2[0], final_g=final_g, consts=consts, dft=dft)
    nc = bacc.Bacc("TRN2", target_bir_lowering=False, num_devices=1)
    arrays, args = {}, []
    for name, a in inputs.items():
        a = np.ascontiguousarray(a)
        arrays[f"in_{name}"] = a
        args.append(nc.dram_tensor(f"in_{name}", a.shape, mybir.dt.from_np(a.dtype), kind="ExternalInput").ap())
    out = nc.dram_tensor("out", (SEQ, D), F32, kind="ExternalOutput").ap()
    build(nc, *args, out)
    r = run_bass_kernel_spmd(nc, [arrays], core_ids=[0])
    return r.results[0]["out"].reshape(1, SEQ, D)
```

```python
from contextlib import ExitStack

import concourse.bass as bass
from concourse import mybir

ALU = mybir.AluOpType
ACT = mybir.ActivationFunctionType
AX_X = mybir.AxisListType.X
F32 = mybir.dt.float32
I32 = mybir.dt.int32

P = 128
SEQ = 1024
D = 1024
TILES = SEQ // P
CH = D // P
HALF = 512
QUART = D // 4
CONV, FOUR, SGU = 384, 256, 384
TAPS = 31
PAD = TAPS // 2
PADW = SEQ + 2 * PAD
WIN = 2 * CONV + FOUR + 2 * SGU
EXPERTS, GROUPS, PER = 64, 8, 8
FF = 512
BLK = 32
SLOTS = 4
EXPERT_FLOATS = 3 * 4096
MAX_BLOCKS = EXPERTS + 2 * SEQ // BLK
XS_ROWS = 2 * SEQ + BLK
EPS = 1e-6
BANKS = 8
AHEAD = 2
NEG = -3.0e38
T_ENDS, T_ROWS = 0, EXPERTS + 1

C_ID, C_TRI, C_ONE, C_BD, C_DFT, C_EXC, C_INC, C_REV = 0, 128, 256, 384, 512, 768, 832, 896
C_GREV, C_THR, C_P, C_PBLK, C_ALT, C_END = 960, 968, 1000, 1001, 1002, 1003

RING = SLOTS * EXPERT_FLOATS
O_V = 0
O_PADH = O_V + 8 * SGU
O_WIN = O_PADH + 3 * PADW
O_WOUT = O_WIN + 8 * WIN - 8 * D
O_Y = O_WIN + 8 * WIN
O_D = O_Y + 8 * SEQ
O_H = O_D + 2 * 4096
O_SMALL = O_H + 8 * SEQ
assert EXPERT_FLOATS <= O_WOUT and O_WOUT + 8 * D <= O_Y and 2 * EXPERT_FLOATS <= O_Y + 8 * SEQ - 8 * HALF


def build(nc, x, c, ln1_g, ln2_g, w_ada, b_ada, w_in, w_out, conv_w, conv_b, conv_gn_g, conv_gn_b,
          sgu_ln_g, sgu_ln_b, sgu_w, sgu_b, router_w, router_b, exp_w1, exp_w3, exp_w2, final_g,
          consts, dft, out):
    ctx = ExitStack()
    with ctx:
        def sem(name):
            return ctx.enter_context(nc.semaphore(name))

        banks = ctx.enter_context(nc.psum_tensor("banks", [P, BANKS, HALF], F32))
        total = RING + 3360
        arena = ctx.enter_context(nc.sbuf_tensor("arena", [P, total], F32))
        table = ctx.enter_context(nc.sbuf_tensor("table", [1, T_ROWS + MAX_BLOCKS + 2], I32))
        rows_at = ctx.enter_context(nc.sbuf_tensor("rows_at", [P, 4, TILES], I32))
        mod_dram = nc.dram_tensor("mod_dram", [6 * D], F32)
        x2_dram = nc.dram_tensor("x2_dram", [SEQ, D], F32)
        xs_dram = nc.dram_tensor("xs_dram", [XS_ROWS, D], F32)
        ys_dram = nc.dram_tensor("ys_dram", [(MAX_BLOCKS + 1) * BLK, D], F32)

        def at(offset, *shape):
            n = 1
            for s in shape:
                n *= s
            view = arena[:, offset:offset + n]
            if len(shape) == 2:
                view = view.rearrange("p (a b) -> p a b", a=shape[0])
            if len(shape) == 3:
                view = view.rearrange("p (a b c) -> p a b c", a=shape[0], b=shape[1])
            return view

        v_t = at(O_V, TILES, SGU)
        pad_h = at(O_PADH, 3, PADW)
        squares = at(O_PADH, 6, HALF)
        w_in_s = at(O_WIN, CH, WIN)
        w_out_s = at(O_WOUT, CH, D)
        y_t = at(O_Y, CH, SEQ)
        x_t = at(O_Y, TILES, D)
        xt_four = y_t[:, 3:5, :]
        ada_s = at(O_D, 2, CH * HALF).rearrange("p a (c f) -> p a c f", c=CH)
        pq = at(O_WIN, TILES, 2 * 256).rearrange("p a (c f) -> p a c f", c=2)
        dft_s = at(O_D, 2, TILES, HALF)
        xr = at(O_D, TILES, D)
        h2_t = at(O_V, 2, CH, P)
        gate1 = at(O_V + 2 * D, D)
        gate1_b = at(O_V + 3 * D, D)
        h_t = at(O_H, CH, SEQ)
        x2 = at(O_H, TILES, D)

        used = {"mixing": O_SMALL, "kept": RING}
        most = {"mixing": RING, "kept": total}

        def small(*shape, life="mixing"):
            n = 1
            for s in shape:
                n *= s
            used[life] += n
            assert used[life] <= most[life], (life, used[life] - most[life])
            return at(used[life] - n, *shape)

        cst = small(C_END)
        tri, ones, bd = (cst[:, o:o + P] for o in (C_TRI, C_ONE, C_BD))
        ws_t = small(6, P)
        vec_rows = small(P)
        vecs = small(16)
        conv_t = small(3 * TAPS)
        gain_k = small(3, P)
        bs_b = small(3, P)
        c_col, c_act, c_wide = small(CH), small(CH), small(CH, 32)
        col = small(10, CH)
        LN1, LN2, SH1, SC1, SH2, SC2, BSH1, BSC1, BSH2, BSC2 = range(10)
        ab = small(4, CH)
        stats, mv, v_rstd = small(TILES, 6), small(TILES, 2), small(TILES)
        mod_rows = small(P)
        router_s = small(CH, EXPERTS)
        router_bb = small(EXPERTS)
        ws_rows = at(O_V, 6, P)
        conv_rows = at(O_V + 6 * P, CONV)
        ident = small(P, life="kept")
        ab_jq = small(2, 2, 4, life="kept")
        ss, rstd = small(3, TILES, life="kept"), small(3, TILES, life="kept")
        eps = small(1, life="kept")
        gate_w = small(2, TILES, life="kept")
        scratch = small(D, life="kept")
        tmp_a, tmp_b, logit = (small(HALF, life="kept") for _ in range(3))
        gate2 = small(QUART, life="kept")
        xrow = tmp_a[:, 0:QUART]
        xt_s = tmp_b[:, 0:QUART].rearrange("p (j q t) -> p j q t", j=2, q=4)
        y_s = logit[:, 0:QUART]
        ff_silu, ff, ff_t = scratch[:, 0:P], scratch[:, 256:256 + P], scratch[:, 512:512 + P]
        gate2_b = tmp_b[:, 0:QUART]

        r0 = O_Y + 8 * SEQ - 8 * HALF
        prob, sel, sel2, hot1, hot2, cand, ranks, before = (at(r0 + i * HALF, HALF) for i in range(8))
        r1 = O_V
        best = at(r1, 12, TILES * GROUPS)
        tok = at(r1 + 768, 8, TILES)
        cnt = at(r1 + 832, 4)
        nb_wide, ct_wide = at(r1 + 840, P), at(r1 + 968, P)
        bounds = at(r1 + 1096, 3, EXPERTS)
        in_block = at(r1 + 1288, EXPERTS)
        in_tmp = at(r1 + 1352, EXPERTS)
        tab_c = at(r1 + 1416, 1)

        def d_cols(vector):
            return vector.rearrange("(q p j) -> p q j", q=4, j=2)

        def d_tile(view):
            return view.rearrange("p (q j) -> p q j", q=4)

        def chunk(view, k):
            first = QUART * (k // 2) + k % 2
            return view[:, first:first - k % 2 + QUART:2]

        s_cst, s_vrows, s_convw, s_ws, s_small, s_c, s_cols = (sem(n) for n in (
            "consts_in", "vector_rows_in", "conv_w_in", "sgu_w_in", "sgu_b_in", "c_in", "columns_in"))
        s_x = [sem(f"x_in{i}") for i in range(2)]
        s_ada = [sem(f"ada_in{i}") for i in range(2)]
        s_win = [sem(f"w_in_in{i}") for i in range(4)]
        s_xr = [sem(f"x_again_in{i}") for i in range(TILES // 2)]
        s_dft, s_wout, s_gate1, s_gate2, s_rb = (sem(n) for n in (
            "dft_in", "w_out_in", "gate1_in", "gate2_in", "router_in"))
        filled, freed_a, freed_d = sem("bank_filled"), sem("bank_freed_by_act"), sem("bank_freed_by_dve")
        s_modout, s_modcols = sem("mod_rows_stored"), sem("mod_columns_in")
        s_eps, s_std, s_mv, s_vstd = (sem(n) for n in ("eps_ready", "deviations_ready", "v_variances", "v_deviations"))
        s_cact, s_cwide, s_ss, s_xhat, s_ab = (sem(n) for n in (
            "c_act_ready", "c_wide_ready", "squares_summed", "xhat_ready", "affine_ready"))
        s_zero, s_conv, s_gnsq, s_gnn, s_gn = (sem(n) for n in (
            "pad_zeroed", "conv_step", "centred_squared", "gn_scaled", "gn_ready"))
        s_vn, s_sg, s_x2, s_x2st, s_xs = (sem(n) for n in (
            "v_ready", "gating_ready", "x2_ready", "x2_stored", "xs_scattered"))
        s_link = sem("dve_step")
        s_expin, s_exp, s_sums, s_wide, s_tabc, s_rows, s_tab = (sem(n) for n in (
            "logits_shifted", "exp_ready", "rank_inputs_ready", "counts_wide_ready", "table_columns_ready",
            "row_numbers_ready", "table_ready"))
        s_pz, s_padz = sem("pad_rows_zero"), sem("pad_rows_stored")
        s_w = [[sem(f"slot{i}_{what}_in") for what in ("w1a", "w1b", "w3a", "w3b", "w2a", "w2b")] for i in range(SLOTS)]
        s_xrow = sem("block_rows_in")
        s_xtp, s_xtm, s_xts, s_h13, s_silu, s_ff, s_ftp, s_ft, s_yp, s_y, s_yst = (sem(n) for n in (
            "block_rows_transposed", "block_x_scaled", "block_x_ready", "block_h_ready", "block_silu", "block_ff",
            "block_ff_transposed", "block_ff_t_ready", "block_y_filled", "block_y_ready_plus_one", "block_y_stored_plus_one"))
        s_begun, s_through = sem("experts_begun"), sem("blocks_through")
        s_yzero = sem("left_out_blocks_zeroed")
        s_x2r, s_fg = sem("x2_again_in"), sem("final_g_in")
        s_gat = [sem(f"rows_gathered{i}") for i in range(TILES)]
        s_t1, s_t2, s_t3, s_tout, s_out = (sem(n) for n in (
            "tail_first", "tail_both", "tail_sum", "tail_ready", "out_stored"))

        order = [("small", "d"), ("ws", 0, "d"), ("ws", 1, "d"), ("rs", "d")]
        order += [("ada", n, "d") for n in range(4)]
        order += [("xt", i, h, "ad"[h]) for i in range(TILES) for h in range(2)]
        ada_left = list(range(4, 12))
        for cc in range(3):
            for s in range(2):
                order += [("g", cc, s, "a"), ("a", cc, s, "d")]
                if cc or s:
                    order += [("ada", ada_left.pop(0), "a")]
        for cc in range(2):
            for s in range(2):
                order += [("b", cc, s, "a")]
                if ada_left:
                    order += [("ada", ada_left.pop(0), "a")]
        order += [("v", i, "a") for i in range(TILES)]
        order += [("gm", cc, s, "d") for cc in range(3) for s in range(2)]
        order += [("u", 0, s, "a") for s in range(2)]
        order += [("gv", cc, s, "a") for cc in range(3) for s in range(2)]
        order += [("u", cc, s, "a") for cc in range(1, 3) for s in range(2)]
        order += [("pq", i, "a") for i in range(TILES)]
        order += [("sg", j, hh, "d") for j in range(3) for hh in range(2)]
        order += [("V", 0, "a"), ("U", 0, "d"), ("mid", "d"), ("V", 1, "a"), ("U", 1, "d")]
        for i in range(TILES + 2):
            if i < TILES:
                order += [("wo", i, 0, "d"), ("wo", i, 1, "d")]
            if 1 <= i <= TILES:
                order += [("x2t", i - 1, 0, "a"), ("x2t", i - 1, 1, "d")]
            if i >= 2:
                order += [("lg", i - 2, "d")]
        order += [("rank", "d"), ("count", "d"), ("bounds", "d"), ("table", "d")]
        index = {entry[:-1]: g for g, entry in enumerate(order)}
        seen = {"a": 0, "d": 0}
        freed_at = []
        for entry in order:
            seen[entry[-1]] += 1
            freed_at.append((entry[-1], seen[entry[-1]]))

        def bank_of(*key):
            return banks[:, index[key] % BANKS, :]

        def full(eng, *key):
            eng.wait_ge(filled, index[key] + 1)

        block = ctx.enter_context(nc.Block())

        def ada_load(q, n):
            if n >= 2:
                q.wait_ge(filled, index[("ada", n - 2)] + 1)
            q.dma_start(ada_s[:, n % 2, :, :], w_ada.rearrange("(p c) f -> p c f", c=CH)[:, :, n * HALF:(n + 1) * HALF]
                        ).then_inc(s_ada[n % 2], 16)

        @block.sync
        def _(sp):
            sp.dma_start(cst, consts).then_inc(s_cst, 16)
            sp.dma_start(ident, consts[:, C_ID:C_ID + P]).then_inc(s_cst, 16)
            sp.dma_start(c_col, c.rearrange("a (p c) -> p (a c)", c=CH)).then_inc(s_c, 16)
            for n in range(2):
                ada_load(sp, n)
            sp.dma_start(x_t[:, 0:4, :], x.rearrange("(t p) d -> p t d", p=P)[:, 0:4, :]).then_inc(s_x[0], 16)
            ada_load(sp, 2)
            sp.dma_start(x_t[:, 4:8, :], x.rearrange("(t p) d -> p t d", p=P)[:, 4:8, :]).then_inc(s_x[1], 16)
            ada_load(sp, 3)
            for part, (f0, f1) in enumerate(((0, 2 * CONV), (2 * CONV, 1024), (1024 + SGU, WIN), (1024, 1024 + SGU))):
                for q in range(4):
                    sp.dma_start(w_in_s[:, 2 * q:2 * q + 2, f0:f1],
                                 w_in[q * QUART:(q + 1) * QUART, f0:f1].rearrange("(p j) f -> p j f", j=2)
                                 ).then_inc(s_win[part], 16)
                if part < 2:
                    for n in (4 + 2 * part, 5 + 2 * part):
                        ada_load(sp, n)
            for n in range(8, 12):
                ada_load(sp, n)
            sp.wait_ge(filled, index[("ada", 11)] + 1)
            sp.dma_start(dft_s, dft).then_inc(s_dft, 16)
            sp.wait_ge(filled, index[("u", 2, 1)] + 1)
            sp.dma_start(w_out_s, w_out.rearrange("(c p) d -> p c d", p=P)).then_inc(s_wout, 16)
            sp.wait_ge(filled, index[("U", 1)] + 1)
            for i in range(0, TILES, 2):
                sp.dma_start(xr[:, i:i + 2, :], x.rearrange("(t p) d -> p t d", p=P)[:, i:i + 2, :]).then_inc(s_xr[i // 2], 16)
            sp.wait_ge(s_modout, 64 * 8)
            sp.wait_ge(filled, index[("sg", 2, 1)] + 1)
            sp.dma_start(gate1, mod_dram.ap()[2 * D:3 * D].partition_broadcast(P)).then_inc(s_gate1, 16)
            sp.dma_start(gate1_b, b_ada[2 * D:3 * D].partition_broadcast(P)).then_inc(s_gate1, 16)

            def piece(e, slot, k):
                u, h = k // 2, k % 2
                if u < 2:
                    src = (exp_w1, exp_w3)[u][bass.ds(e, 1), h * 512:(h + 1) * 512, :].rearrange("e (q p j) f -> (e p) q (j f)", q=2, j=2)
                else:
                    src = exp_w2[bass.ds(e, 1), h * 256:(h + 1) * 256, :].rearrange("e (k p) d -> (e p) k d", k=2)
                sp.dma_start(at(slot * EXPERT_FLOATS + k * 2048, 2, D), src).then_inc(s_w[slot][k], 16)

            sp.wait_ge(s_gnn, 6)
            for k in range(2, 6):
                piece(0, 0, k)
            sp.wait_ge(filled, index[("wo", TILES - 1, 1)] + 1)
            for k in range(6):
                piece(1, 1, k)
            for i in range(TILES):
                sp.wait_ge(s_x2, 2 * i + 2)
                sp.dma_start(x2_dram.ap()[i * P:(i + 1) * P, :], x2[:, i, :]).then_inc(s_x2st, 16)
            sp.wait_ge(s_tab, 1)
            for k in range(2):
                piece(0, 0, k)
            sp.wait_ge(s_xs, 16 * 2 * TILES)
            for k in range(6):
                piece(2, 2, k)
            sp.wait_ge(s_x2st, 16 * TILES)
            for k in range(6):
                piece(3, 3, k)
            with sp.Fori(0, EXPERTS // SLOTS - 1) as r:
                for slot in range(SLOTS):
                    end = sp.value_load(table[0:1, bass.ds(r * SLOTS + (T_ENDS + 1 + slot), 1)], min_val=1, max_val=MAX_BLOCKS)
                    for k in range(6):
                        if k == 0:
                            sp.wait_ge(s_h13, end)
                        if k == 4:
                            sp.wait_ge(s_yp, end)
                        before, rounds = (slot, r + 2) if k >= AHEAD else ((slot - 1) % SLOTS, r + (2 if slot else 1))
                        sp.wait_ge(s_w[before][(k - AHEAD) % 6], rounds * 16)
                        piece(r * SLOTS + (SLOTS + slot), slot, k)
            end = sp.value_load(table[0:1, T_ENDS + EXPERTS - SLOTS + 1:T_ENDS + EXPERTS - SLOTS + 2], min_val=1, max_val=MAX_BLOCKS)
            sp.wait_ge(s_yp, end)
            sp.dma_start(at(0, TILES, D), x2_dram.ap().rearrange("(t p) d -> p t d", p=P)).then_inc(s_x2r, 16)
            sp.dma_start(at(8192, D), final_g.partition_broadcast(P)).then_inc(s_fg, 16)
            for i in range(TILES):
                sp.wait_ge(s_tout, i + 1)
                sp.dma_start(out[i * P:(i + 1) * P, :], at(3 * EXPERT_FLOATS + i * D, D)).then_inc(s_out, 16)
            sp.wait_ge(s_out, 16 * TILES)

        @block.gpsimd
        def _(pool):
            for r, vec in enumerate((conv_b, conv_gn_g, conv_gn_b, sgu_ln_g, sgu_ln_b)):
                pool.dma_start(vec_rows[3 * r:3 * r + 3, :], vec.rearrange("(a f) -> a f", f=P)).then_inc(s_vrows, 16)
            pool.dma_start(conv_rows[0:TAPS, 0:CONV], conv_w).then_inc(s_convw, 16)
            pool.dma_start(ws_rows, sgu_w.rearrange("h p q -> p h q")).then_inc(s_ws, 16)
            for n, vec in ((LN1, ln1_g), (LN2, ln2_g)):
                pool.dma_start(d_tile(col[:, n, :]), d_cols(vec)).then_inc(s_cols, 16)
            for n, m in ((BSH1, 0), (BSC1, 1), (BSH2, 3), (BSC2, 4)):
                pool.dma_start(d_tile(col[:, n, :]), d_cols(b_ada[m * D:(m + 1) * D])).then_inc(s_cols, 16)
            for h in range(6):
                pool.dma_start(bs_b[64 * (h % 2):64 * (h % 2) + 64, h // 2, :], sgu_b[h, :].partition_broadcast(64)).then_inc(s_small, 16)
            for q in range(4):
                pool.dma_start(router_s[:, 2 * q:2 * q + 2, :], router_w[q * QUART:(q + 1) * QUART, :].rearrange("(p j) e -> p j e", j=2)
                               ).then_inc(s_rb, 16)
            pool.dma_start(router_bb, router_b.partition_broadcast(P)).then_inc(s_rb, 16)
            pool.memset(pad_h[:, :, 0:PAD], 0.0).then_inc(s_zero, 1)
            pool.memset(pad_h[:, :, PAD + SEQ:PADW], 0.0).then_inc(s_zero, 1)
            for n in range(4, 12):
                who, count = freed_at[index[("ada", n)]]
                pool.wait_ge(freed_a if who == "a" else freed_d, count)
                for q in range(4):
                    pool.dma_start(mod_dram.ap()[n * HALF + q * P:n * HALF + (q + 1) * P].rearrange("(a f) -> a f", a=1),
                                   mod_rows[32 * q:32 * q + 1, :]).then_inc(s_modout, 16)
            pool.wait_ge(s_modout, 64 * 8)
            for k, m in ((SH2, 3), (SC2, 4)):
                pool.dma_start(d_tile(col[:, k, :]), d_cols(mod_dram.ap()[m * D:(m + 1) * D])).then_inc(s_modcols, 16)
            pool.wait_ge(freed_d, freed_at[index[("U", 1)]][1])
            for q in range(4):
                for dst, src in ((gate2, mod_dram.ap()), (gate2_b, b_ada)):
                    pool.dma_start(dst[32 * q:32 * q + 32, :],
                                   src[5 * D + q * QUART:5 * D + (q + 1) * QUART].partition_broadcast(32)).then_inc(s_gate2, 16)
            pool.wait_ge(s_ss, 2 * TILES)
            pool.memset(scratch, 0.0).then_inc(s_pz, 1)
            pool.wait_ge(s_pz, 1)
            pool.dma_start(xs_dram.ap()[2 * SEQ:XS_ROWS, :], scratch[0:BLK, :]).then_inc(s_padz, 16)
            pool.wait_ge(s_rows, 1)
            for i in range(TILES):
                for k in range(2):
                    pool.indirect_dma_start(out=xs_dram.ap(), out_offset=bass.IndirectOffsetOnAxis(ap=rows_at[:, k, i:i + 1], axis=0),
                                            in_=xr[:, i, :], in_offset=None).then_inc(s_xs, 16)
            pool.wait_ge(s_tab, 1)
            blocks = pool.value_load(table[0:1, T_ENDS + EXPERTS:T_ENDS + EXPERTS + 1], min_val=EXPERTS, max_val=MAX_BLOCKS)
            pool.wait_ge(s_yzero, (MAX_BLOCKS + 1) * 16)
            pool.wait_ge(s_yst, (blocks + 1) * 16)
            pool.sem_inc(s_through, 1)
            for i in range(TILES):
                for k in range(2):
                    pool.indirect_dma_start(out=at((k + 1) * EXPERT_FLOATS + i * D, D), out_offset=None, in_=ys_dram.ap(),
                                            in_offset=bass.IndirectOffsetOnAxis(ap=rows_at[:, 2 + k, i:i + 1], axis=0)
                                            ).then_inc(s_gat[i], 16)

        @block.tensor
        def _(pe):
            def begin(*key):
                g = index[key]
                if g >= BANKS:
                    who, count = freed_at[g - BANKS]
                    pe.wait_ge(freed_a if who == "a" else freed_d, count)
                return bank_of(*key)

            pe.wait_ge(s_cst, 32)
            ps = begin("small")
            pe.wait_ge(s_vrows, 16 * 5)
            pe.wait_ge(s_convw, 16)
            pe.transpose(ps[:, 0:15], vec_rows[0:15, :], ident[0:15, 0:15])
            for cc in range(3):
                last = pe.transpose(ps[:, 16 + cc * TAPS:16 + (cc + 1) * TAPS], conv_rows[0:TAPS, cc * P:(cc + 1) * P], ident[0:TAPS, 0:TAPS])
            last.then_inc(filled, 1)
            pe.wait_ge(s_ws, 16)
            for g in range(2):
                ps = begin("ws", g)
                for k in range(3):
                    h = 3 * g + k
                    last = pe.transpose(ps[:, k * P:(k + 1) * P], ws_rows[:, h, :], ident)
                last.then_inc(filled, 1)
            ps = begin("rs")
            full_d = freed_at[index[("ws", 1)]][1]
            pe.wait_ge(freed_d, full_d)
            for h in range(6):
                last = pe.matmul(ps[64 * (h % 2):64 * (h % 2) + 64, (h // 2) * P:(h // 2 + 1) * P], ones[:, 0:64], ws_t[:, h, :],
                                 start=True, stop=True, skip_group_check=True)
            last.then_inc(filled, 1)

            def ada_columns(n):
                ps = begin("ada", n)
                if n == 0:
                    pe.wait_ge(s_cact, 1)
                pe.wait_ge(s_ada[n % 2], 16 * (n // 2 + 1))
                for j in range(4):
                    for k in range(CH):
                        last = pe.matmul(ps[:, j:j + 1], chunk(ada_s[:, n % 2, k, :], j), c_act[:, k:k + 1],
                                         start=(k == 0), stop=(k == CH - 1), skip_group_check=True)
                last.then_inc(filled, 1)

            def ada(n):
                ps = begin("ada", n)
                if n == 4:
                    pe.wait_ge(s_cwide, 1)
                pe.wait_ge(s_ada[n % 2], 16 * (n // 2 + 1))
                for k in range(CH):
                    for q in range(4):
                        last = pe.matmul(ps[32 * q:32 * q + 32, 0:P], c_wide[:, k, :], ada_s[:, n % 2, k, q * P:(q + 1) * P],
                                         start=(k == 0), stop=(k == CH - 1), tile_position=(0, 32 * q))
                last.then_inc(filled, 1)

            for n in range(4):
                ada_columns(n)
            for i in range(TILES):
                pe.wait_ge(s_xhat, i + 1)
                for h in range(2):
                    ps = begin("xt", i, h)
                    for j in range(4):
                        last = pe.transpose(ps[:, j * P:(j + 1) * P], chunk(x_t[:, i, :], 4 * h + j), ident)
                    last.then_inc(filled, 1)

            def h_ready(s):
                for h in range(2):
                    who, count = freed_at[index[("xt", 4 * s + 3, h)]]
                    pe.wait_ge(freed_a if who == "a" else freed_d, count)

            def z_cols(ps, f0, s):
                for k in range(CH):
                    last = pe.matmul(ps, w_in_s[:, k, f0:f0 + P], h_t[:, k, s * HALF:(s + 1) * HALF], start=(k == 0), stop=(k == CH - 1))
                last.then_inc(filled, 1)

            for g, entry in enumerate(order):
                key = entry[:-1]
                kind = key[0]
                if kind in ("small", "ws", "rs", "xt") or kind == "ada" and key[1] < 4:
                    continue
                if kind == "ada":
                    ada(key[1])
                    continue
                ps = begin(*key)
                if kind in ("g", "a"):
                    if g == index[("g", 0, 0)]:
                        pe.wait_ge(s_win[0], 64)
                    if key[1] == 0:
                        h_ready(key[2])
                    z_cols(ps, (CONV if kind == "g" else 0) + key[1] * P, key[2])
                elif kind == "b":
                    pe.wait_ge(s_win[1], 64)
                    z_cols(ps, 2 * CONV + key[1] * P, key[2])
                elif kind == "v":
                    pe.wait_ge(s_win[2], 64)
                    i = key[1]
                    for k in range(CH):
                        last = pe.matmul(ps[:, 0:SGU], h_t[:, k, i * P:(i + 1) * P], w_in_s[:, k, 1024 + SGU:WIN], start=(k == 0), stop=(k == CH - 1))
                    last.then_inc(filled, 1)
                elif kind == "u":
                    pe.wait_ge(s_win[3], 64)
                    z_cols(ps, 1024 + key[1] * P, key[2])
                elif kind == "pq":
                    i = key[1]
                    if i == 0:
                        pe.wait_ge(freed_a, freed_at[index[("b", 1, 1)]][1])
                    for cc in range(2):
                        last = pe.matmul(ps[:, cc * 256:(cc + 1) * 256], xt_four[:, cc, i * P:(i + 1) * P], cst[:, C_DFT:C_DFT + 256],
                                         start=True, stop=True, skip_group_check=True)
                    last.then_inc(filled, 1)
                elif kind in ("U", "V"):
                    pe.wait_ge(freed_a, freed_at[index[("pq", TILES - 1)]][1])
                    pe.wait_ge(s_dft, 16)
                    t = 0 if kind == "U" else 1
                    for k in range(TILES):
                        last = pe.matmul(ps, pq[:, k, key[1], t * P:(t + 1) * P], dft_s[:, t, k, :], start=(k == 0), stop=(k == TILES - 1))
                    last.then_inc(filled, 1)
                elif kind == "mid":
                    for cc in range(2):
                        for k in range(TILES):
                            last = pe.matmul(ps[:, cc:cc + 1], pq[:, k, cc, 0:P], cst[:, C_ALT:C_ALT + 1],
                                             start=(k == 0), stop=(k == TILES - 1), skip_group_check=True)
                    last.then_inc(filled, 1)
                elif kind == "gm":
                    pe.wait_ge(s_conv, TAPS * (key[1] + 1))
                    pe.matmul(ps, bd, y_t[:, key[1], key[2] * HALF:(key[2] + 1) * HALF], start=True, stop=True).then_inc(filled, 1)
                elif kind == "gv":
                    n = 2 * key[1] + key[2]
                    pe.wait_ge(s_gnsq, n + 1)
                    pe.matmul(ps, bd, squares[:, n, :], start=True, stop=True).then_inc(filled, 1)
                elif kind == "sg":
                    j, hh = key[1:]
                    pe.wait_ge(s_vn, 4 * hh + 4)
                    for i in range(4):
                        for e in range(2):
                            h = 2 * j + e
                            last = pe.matmul(ps[64 * e:64 * e + 64, i * P:(i + 1) * P], v_t[:, 4 * hh + i, h * 64:(h + 1) * 64], ws_t[:, h, :],
                                             start=True, stop=True, skip_group_check=True)
                    last.then_inc(filled, 1)
                elif kind == "wo":
                    i, s = key[1:]
                    if (i, s) == (0, 0):
                        pe.wait_ge(s_wout, 16)
                        pe.wait_ge(freed_d, freed_at[index[("U", 1)]][1])
                        pe.wait_ge(s_sg, 6)
                        pe.wait_ge(s_gn, 6)
                    for n, k in enumerate((0, 1, 2, 5, 6, 7, 3, 4)):
                        last = pe.matmul(ps, y_t[:, k, i * P:(i + 1) * P], w_out_s[:, k, s * HALF:(s + 1) * HALF], start=(n == 0), stop=(n == CH - 1))
                    last.then_inc(filled, 1)
                elif kind == "x2t":
                    i, h = key[1:]
                    pe.wait_ge(s_xhat, TILES + i + 1)
                    for j in range(4):
                        last = pe.transpose(ps[:, j * P:(j + 1) * P], chunk(xr[:, i, :], 4 * h + j), ident)
                    last.then_inc(filled, 1)
                elif kind == "lg":
                    i = key[1]
                    if i == 0:
                        pe.wait_ge(s_rb, 80)
                    for h in range(2):
                        who, count = freed_at[index[("x2t", i, h)]]
                        pe.wait_ge(freed_a if who == "a" else freed_d, count)
                    for k in range(CH):
                        last = pe.matmul(ps[:, 0:EXPERTS], h2_t[:, i % 2, k, :], router_s[:, k, :], start=(k == 0), stop=(k == CH - 1))
                    last.then_inc(filled, 1)
                elif kind == "rank":
                    pe.wait_ge(s_sums, 1)
                    pe.matmul(ps, tri, ranks, start=True, stop=False)
                    pe.matmul(ps, ones, before, start=False, stop=True).then_inc(filled, 1)
                elif kind == "count":
                    for i in range(TILES):
                        last = pe.matmul(ps[0:EXPERTS, 0:1], ranks[:, i * EXPERTS:(i + 1) * EXPERTS], ones[:, 0:1],
                                         start=(i == 0), stop=(i == TILES - 1))
                    last.then_inc(filled, 1)
                elif kind == "bounds":
                    pe.wait_ge(s_wide, 1)
                    pe.matmul(ps[:, 0:EXPERTS], nb_wide[0:EXPERTS, :], cst[0:EXPERTS, C_INC:C_INC + EXPERTS], start=True, stop=True, skip_group_check=True)
                    pe.matmul(ps[:, EXPERTS:2 * EXPERTS], nb_wide[0:EXPERTS, :], cst[0:EXPERTS, C_EXC:C_EXC + EXPERTS], start=True, stop=True, skip_group_check=True)
                    pe.matmul(ps[:, 2 * EXPERTS:3 * EXPERTS], ct_wide[0:EXPERTS, :], cst[0:EXPERTS, C_EXC:C_EXC + EXPERTS], start=True, stop=True, skip_group_check=True).then_inc(filled, 1)
                elif kind == "table":
                    pe.wait_ge(s_tabc, 1)
                    pe.matmul(ps[0:1, 0:P], tab_c, ident, start=True, stop=True).then_inc(filled, 1)

            xt_p, h_p, ft_p, y_p = (banks[:, b, :] for b in range(4))
            pe.wait_ge(s_tab, 1)

            def x_transposes(n):
                pe.wait_ge(s_xrow, (n + 1) * 16)
                for j in range(2):
                    last = pe.transpose(xt_p[:, j * P:(j + 1) * P], xrow[:, j:QUART:2], ident)
                last.then_inc(s_xtp, 1)

            def up(n, slot):
                w13 = at(slot * EXPERT_FLOATS, 2, CH, FF)
                for k in range(CH):
                    for q in range(4):
                        last = pe.matmul(h_p[32 * q:32 * q + 32, 0:2 * P].rearrange("p (a b) -> p a b", a=2), xt_s[:, k % 2, k // 2, :],
                                         w13[:, :, k, q * P:(q + 1) * P], start=(k == 0), stop=(k == CH - 1), tile_position=(0, 32 * q))
                last.then_inc(s_h13, 1)

            def down(n, slot):
                pe.wait_ge(s_ft, n + 1)
                pe.wait_ge(s_y, n + 1)
                w2 = at(slot * EXPERT_FLOATS + 8192, 4, D)
                for k in range(4):
                    for q in range(4):
                        last = pe.matmul(y_p[32 * q:32 * q + 32, 0:QUART], ff_t[:, k * BLK:(k + 1) * BLK],
                                         w2[:, k, q * QUART:(q + 1) * QUART], start=(k == 0), stop=(k == 3), tile_position=(0, 32 * q))
                last.then_inc(s_yp, 1)

            def hidden_transposes(n):
                pe.wait_ge(s_ff, n + 1)
                pe.transpose(ft_p[:, 0:P], ff, ident).then_inc(s_ftp, 1)

            def up_and_next(n, slot):
                pe.wait_ge(s_xts, n + 1)
                up(n, slot)
                x_transposes(n + 1)

            x_transposes(0)
            with pe.Fori(0, EXPERTS // SLOTS) as r:
                for slot in range(SLOTS):
                    lo = pe.value_load(table[0:1, bass.ds(r * SLOTS + (T_ENDS + slot), 1)], min_val=0, max_val=MAX_BLOCKS - 1)
                    hi = pe.value_load(table[0:1, bass.ds(r * SLOTS + (T_ENDS + slot + 1), 1)], min_val=1, max_val=MAX_BLOCKS)
                    for k in range(6):
                        pe.wait_ge(s_w[slot][k], (r + 1) * 16)
                    pe.sem_inc(s_begun, 1)
                    up_and_next(lo, slot)
                    if slot:
                        down(lo - 1, slot - 1)
                    else:
                        with pe.If(r > 0):
                            down(lo - 1, SLOTS - 1)
                    hidden_transposes(lo)
                    with pe.If(hi > lo + 1):
                        with pe.Fori(lo + 1, hi) as n:
                            up_and_next(n, slot)
                            down(n - 1, slot)
                            hidden_transposes(n)
            blocks = pe.value_load(table[0:1, T_ENDS + EXPERTS:T_ENDS + EXPERTS + 1], min_val=EXPERTS, max_val=MAX_BLOCKS)
            down(blocks - 1, SLOTS - 1)

        @block.scalar
        def _(act):
            def begin(*key):
                full(act, *key)
                return bank_of(*key)

            def root(dst, src, sums):
                act.wait_ge(s_ss, sums)
                nc.scalar.activation(dst, src, ACT.Sqrt, bias=eps, scale=1.0 / D).then_inc(s_std, 1)

            act.wait_ge(s_eps, 1)
            act.wait_ge(s_c, 16)
            nc.scalar.activation(c_act, c_col, ACT.Silu).then_inc(s_cact, 1)
            for i in range(TILES):
                if i % 4 == 0:
                    act.wait_ge(s_x[i // 4], 16)
                if i:
                    act.wait_ge(s_ss, i)
                nc.scalar.activation(scratch, x_t[:, i, :], ACT.Square, accum_out=ss[:, 0, i:i + 1]).then_inc(s_ss, 1)
                if i % 4 == 3:
                    root(rstd[:, 0, i - 3:i + 1], ss[:, 0, i - 3:i + 1], i + 1)
            def gn_squares(n):
                act.wait_ge(freed_d, freed_at[index[("gm", n // 2, n % 2)]][1])
                act.wait_ge(s_conv, 3 * TAPS)
                nc.scalar.activation(squares[:, n, :], y_t[:, n // 2, (n % 2) * HALF:(n % 2 + 1) * HALF], ACT.Square).then_inc(s_gnsq, 1)

            def gn_silu(n):
                act.wait_ge(s_gnn, n + 1)
                cc, part = n // 2, y_t[:, n // 2, (n % 2) * HALF:(n % 2 + 1) * HALF]
                nc.scalar.activation(part, part, ACT.Silu, bias=vecs[:, 6 + cc:7 + cc], scale=vecs[:, 3 + cc:4 + cc]).then_inc(s_gn, 1)

            act.wait_ge(s_ab, 1)
            for entry in order:
                if entry[-1] != "a":
                    continue
                key = entry[:-1]
                kind = key[0]
                if kind == "x2t":
                    break
                if key == ("u", 0, 0):
                    act.wait_ge(s_mv, 1)
                    nc.scalar.activation(v_rstd, v_rstd, ACT.Sqrt, bias=eps).then_inc(s_vstd, 1)
                    for n in range(6):
                        gn_squares(n)
                ps = begin(*key)
                if kind == "xt":
                    i, h = key[1:]
                    for j in range(4):
                        k = 4 * h + j
                        last = nc.scalar.activation(h_t[:, k, i * P:(i + 1) * P], ps[:, j * P:(j + 1) * P], ACT.Identity,
                                                    bias=ab[:, 1, k:k + 1], scale=ab[:, 0, k:k + 1])
                elif kind == "g":
                    n = 2 * key[1] + key[2]
                    if n >= 2:
                        act.wait_ge(freed_d, freed_at[index[("a", (n - 2) // 2, n % 2)]][1])
                    last = nc.scalar.activation((tmp_a, tmp_b)[n % 2], ps, ACT.Sigmoid)
                elif kind == "ada":
                    if key[1] > 4:
                        act.wait_ge(s_modout, 64 * (key[1] - 4))
                    last = nc.scalar.activation(mod_rows, ps[:, 0:P], ACT.Copy)
                elif kind == "b":
                    last = nc.scalar.activation(xt_four[:, key[1], key[2] * HALF:(key[2] + 1) * HALF], ps, ACT.Copy)
                elif kind == "v":
                    last = nc.scalar.activation(v_t[:, key[1], :], ps[:, 0:SGU], ACT.Gelu_apprx_tanh)
                elif kind == "u":
                    last = nc.scalar.activation(y_t[:, 5 + key[1], key[2] * HALF:(key[2] + 1) * HALF], ps, ACT.Gelu_apprx_tanh)
                elif kind == "gv":
                    last = nc.scalar.activation(squares[:, 2 * key[1] + key[2], :], ps, ACT.Sqrt, bias=eps)
                elif kind == "V":
                    act.wait_ge(s_sg, 5 + key[1])
                    last = nc.scalar.activation((tmp_a, tmp_b)[key[1]], ps, ACT.Copy)
                elif kind == "pq":
                    last = nc.scalar.activation(pq[:, key[1], :, :].rearrange("p a b -> p (a b)"), ps, ACT.Copy)
                last.then_inc(freed_a, 1)
                if key == ("pq", TILES - 1):
                    for n in range(6):
                        gn_silu(n)

            act.wait_ge(s_ab, 2)
            for i in range(TILES + 1):
                if i < TILES:
                    act.wait_ge(s_x2, 2 * i + 2)
                    act.wait_ge(s_ss, TILES + i)
                    nc.scalar.activation(scratch, x2[:, i, :], ACT.Square, accum_out=ss[:, 1, i:i + 1]).then_inc(s_ss, 1)
                    root(rstd[:, 1, i:i + 1], ss[:, 1, i:i + 1], TILES + i + 1)
                if i >= 1:
                    ps = begin("x2t", i - 1, 0)
                    if i >= 3:
                        act.wait_ge(filled, index[("lg", i - 3)] + 1)
                    for j in range(4):
                        last = nc.scalar.activation(h2_t[:, (i - 1) % 2, j, :], ps[:, j * P:(j + 1) * P], ACT.Identity,
                                                    bias=ab[:, 3, j:j + 1], scale=ab[:, 2, j:j + 1])
                    last.then_inc(freed_a, 1)
            act.wait_ge(s_expin, 1)
            nc.scalar.activation(prob, prob, ACT.Exp).then_inc(s_exp, 1)

            act.wait_ge(s_tab, 1)
            act.wait_ge(s_xs, 16 * 2 * TILES)
            act.wait_ge(s_padz, 16)

            act.sem_inc(s_yst, 16)

            def rows_in(n):
                start = act.value_load(table[0:1, bass.ds(n + T_ROWS, 1)], min_val=0, max_val=2 * SEQ)
                act.dma_start(xrow, xs_dram.ap()[bass.ds(start, BLK), :].rearrange("r (q c) -> q r c", q=4)).then_inc(s_xrow, 16)

            def silu(n):
                act.wait_ge(s_h13, n + 1)
                nc.scalar.activation(ff_silu, banks[:, 1, 0:P], ACT.Silu).then_inc(s_silu, 1)

            def hidden_copy(n):
                act.wait_ge(s_ftp, n + 1)
                nc.scalar.activation(ff_t, banks[:, 2, 0:P], ACT.Copy).then_inc(s_ft, 1)

            def result_out(n):
                act.wait_ge(s_y, n + 2)
                act.dma_start(ys_dram.ap()[bass.ds(n * BLK, BLK), :].rearrange("r (q c) -> q r c", q=4), y_s).then_inc(s_yst, 16)

            def rows_next(n):
                act.wait_ge(s_xtp, n)
                rows_in(n)

            rows_in(0)
            rows_next(1)
            blocks = act.value_load(table[0:1, T_ENDS + EXPERTS:T_ENDS + EXPERTS + 1], min_val=EXPERTS, max_val=MAX_BLOCKS)
            with act.Fori(blocks, MAX_BLOCKS + 1) as n:
                act.dma_start(ys_dram.ap()[bass.ds(n * BLK, BLK), :], xs_dram.ap()[2 * SEQ:XS_ROWS, :]).then_inc(s_yzero, 16)
            silu(0)
            rows_next(2)
            hidden_copy(0)
            act.sem_inc(s_yzero, 16)
            with act.Fori(1, blocks) as n:
                silu(n)
                rows_next(n + 2)
                result_out(n - 1)
                hidden_copy(n)
                act.sem_inc(s_yzero, 16)
            result_out(blocks - 1)
            act.wait_ge(s_xrow, (blocks + 2) * 16)

            for i in range(TILES + 1):
                if i < TILES:
                    act.wait_ge(s_gat[i], 32)
                    first = at(EXPERT_FLOATS + i * D, D)
                    nc.scalar.activation(first, first, ACT.Copy, scale=gate_w[:, 0, i:i + 1]).then_inc(s_t1, 1)
                if i >= 1:
                    act.wait_ge(s_t3, i)
                    act.wait_ge(s_ss, 2 * TILES + i - 1)
                    nc.scalar.activation(scratch, at(3 * EXPERT_FLOATS + (i - 1) * D, D), ACT.Square,
                                         accum_out=ss[:, 2, i - 1:i]).then_inc(s_ss, 1)
                    root(rstd[:, 2, i - 1:i], ss[:, 2, i - 1:i], 2 * TILES + i)

        @block.vector
        def _(dve):
            steps = [0]

            def link(ins):
                steps[0] += 1
                ins.then_inc(s_link, 1)
                dve.wait_ge(s_link, steps[0])

            def begin(*key):
                full(dve, *key)
                return bank_of(*key)

            def wide(view, *shape):
                return view.broadcast_to(list(shape))

            v = nc.vector
            v.memset(eps, EPS).then_inc(s_eps, 1)
            dve.wait_ge(s_cact, 1)
            v.tensor_copy(c_wide, c_act.unsqueeze(2).broadcast_to([P, CH, 32])).then_inc(s_cwide, 1)
            ps = begin("small")
            v.tensor_copy(vecs[:, 0:15], ps[:, 0:15])
            v.tensor_copy(conv_t, ps[:, 16:16 + 3 * TAPS]).then_inc(freed_d, 1)
            for g in range(2):
                ps = begin("ws", g)
                v.tensor_copy(ws_t[:, 3 * g:3 * g + 3, :], ps[:, 0:3 * P].rearrange("p (h q) -> p h q", h=3)).then_inc(freed_d, 1)
            ps = begin("rs")
            dve.wait_ge(s_small, 16 * 6)
            dve.wait_ge(freed_d, 1)
            for j in range(3):
                last = v.scalar_tensor_tensor(gain_k[:, j, :], ps[:, j * P:(j + 1) * P], vecs[:, 12 + j:13 + j], bs_b[:, j, :], ALU.mult, ALU.add)
            last.then_inc(freed_d, 1)
            for n in range(4):
                ps = begin("ada", n)
                v.tensor_copy(col[:, (SH1, SC1)[n // 2], 4 * (n % 2):4 * (n % 2) + 4], ps[:, 0:4]).then_inc(freed_d, 1)

            def affine(a, b, scale, b_scale, shift, b_shift, gain):
                link(v.tensor_tensor(ab[:, a, :], col[:, scale, :], col[:, b_scale, :], ALU.add))
                link(v.scalar_tensor_tensor(ab[:, a, :], ab[:, a, :], 1.0, col[:, gain, :], ALU.add, ALU.mult))
                v.tensor_tensor(ab[:, b, :], col[:, shift, :], col[:, b_shift, :], ALU.add).then_inc(s_ab, 1)

            dve.wait_ge(s_cols, 16 * 6)
            dve.wait_ge(freed_d, freed_at[index[("ada", 3)]][1])
            affine(0, 1, SC1, BSC1, SH1, BSH1, LN1)
            dve.wait_ge(s_ab, 1)
            for i in range(TILES + 1):
                if i < TILES:
                    if i % 4 == 0:
                        dve.wait_ge(s_std, i // 4 + 1)
                        link(v.reciprocal(rstd[:, 0, i:i + 4], rstd[:, 0, i:i + 4]))
                    v.tensor_scalar(x_t[:, i, :], x_t[:, i, :], rstd[:, 0, i:i + 1], None, ALU.mult).then_inc(s_xhat, 1)
                if i >= 1:
                    ps = begin("xt", i - 1, 1)
                    for j in range(4):
                        last = v.tensor_scalar(h_t[:, 4 + j, (i - 1) * P:i * P], ps[:, j * P:(j + 1) * P],
                                               ab[:, 0, 4 + j:5 + j], ab[:, 1, 4 + j:5 + j], ALU.mult, ALU.add)
                    last.then_inc(freed_d, 1)

            for cc in range(3):
                for s in range(2):
                    ps = begin("a", cc, s)
                    dve.wait_ge(freed_a, freed_at[index[("g", cc, s)]][1])
                    v.tensor_tensor(pad_h[:, cc, PAD + s * HALF:PAD + (s + 1) * HALF], ps, (tmp_a, tmp_b)[s], ALU.mult).then_inc(freed_d, 1)
                dve.wait_ge(s_zero, 2)
                dve.wait_ge(freed_d, freed_at[index[("a", cc, 1)]][1])
                for k in range(TAPS):
                    src, w = pad_h[:, cc, k:k + SEQ], conv_t[:, cc * TAPS + k:cc * TAPS + k + 1]
                    if k == 0:
                        ins = v.tensor_scalar(y_t[:, cc, :], src, w, vecs[:, cc:cc + 1], ALU.mult, ALU.add)
                    else:
                        dve.wait_ge(s_conv, cc * TAPS + k)
                        ins = v.scalar_tensor_tensor(y_t[:, cc, :], src, w, y_t[:, cc, :], ALU.mult, ALU.add)
                    ins.then_inc(s_conv, 1)

            for i in range(TILES):
                dve.wait_ge(freed_a, freed_at[index[("v", i)]][1])
                last = v.bn_stats(stats[:, i, :], v_t[:, i, :])
            link(last)
            for i in range(TILES):
                last = v.bn_aggr(mv[:, i, :], stats[:, i, :])
            link(last)
            v.tensor_copy(v_rstd, mv[:, :, 1]).then_inc(s_mv, 1)
            dve.wait_ge(s_vstd, 1)
            link(v.reciprocal(v_rstd, v_rstd))
            for i in range(TILES):
                v.tensor_scalar(v_t[:, i, :], v_t[:, i, :], mv[:, i, 0:1], v_rstd[:, i:i + 1], ALU.subtract, ALU.mult).then_inc(s_vn, 1)

            def centre(n):
                ps = begin("gm", n // 2, n % 2)
                part = y_t[:, n // 2, (n % 2) * HALF:(n % 2 + 1) * HALF]
                v.tensor_tensor(part, part, ps, ALU.subtract).then_inc(freed_d, 1)

            def gn_scale(n):
                part = y_t[:, n // 2, (n % 2) * HALF:(n % 2 + 1) * HALF]
                dve.wait_ge(freed_a, freed_at[index[("gv", n // 2, n % 2)]][1])
                link(v.reciprocal(squares[:, n, :], squares[:, n, :]))
                v.tensor_tensor(part, part, squares[:, n, :], ALU.mult).then_inc(s_gnn, 1)

            def fourier(cc):
                ps = begin("U", cc)
                sin = (tmp_a, tmp_b)[cc]
                dve.wait_ge(freed_a, freed_at[index[("V", cc)]][1])
                v.tensor_tensor(y_t[:, 3 + cc, 0:HALF], ps, sin, ALU.subtract)
                v.tensor_tensor(y_t[:, 3 + cc, SEQ - 1:HALF:-1], ps[:, 1:HALF], sin[:, 1:HALF], ALU.add).then_inc(freed_d, 1)

            dve.wait_ge(s_conv, 3 * TAPS)
            for n in range(6):
                centre(n)
            for n in range(6):
                gn_scale(n)
            for n in range(6):
                j, hh = n // 2, n % 2
                ps = begin("sg", j, hh)
                t = (tmp_a, tmp_b)[n % 2]
                if n >= 2:
                    dve.wait_ge(s_sg, n - 1)
                v.scalar_tensor_tensor(t.rearrange("p (a b) -> p a b", a=4), ps.rearrange("p (a b) -> p a b", a=4), vecs[:, 9 + j:10 + j],
                                       gain_k[:, j, :].unsqueeze(1).broadcast_to([P, 4, P]), ALU.mult, ALU.add).then_inc(freed_d, 1)
                dve.wait_ge(freed_d, freed_at[index[("sg", j, hh)]][1])
                part = y_t[:, 5 + j, hh * HALF:(hh + 1) * HALF]
                v.tensor_tensor(part, part, t, ALU.mult).then_inc(s_sg, 1)
            fourier(0)
            ps = begin("mid")
            for cc in range(2):
                last = v.tensor_copy(y_t[:, 3 + cc, HALF:HALF + 1], ps[:, cc:cc + 1])
            last.then_inc(freed_d, 1)
            fourier(1)
            dve.wait_ge(s_modcols, 32)
            affine(2, 3, SC2, BSC2, SH2, BSH2, LN2)
            dve.wait_ge(s_ab, 2)
            v.tensor_copy(ab_jq[:, 0, :, :], ab[:, 2, :].rearrange("p (q j) -> p j q", q=4))
            v.tensor_copy(ab_jq[:, 1, :, :], ab[:, 3, :].rearrange("p (q j) -> p j q", q=4))
            dve.wait_ge(s_gate1, 32)
            link(v.tensor_tensor(gate1, gate1, gate1_b, ALU.add))
            for i in range(TILES + 2):
                if i < TILES:
                    if i % 2 == 0:
                        dve.wait_ge(s_xr[i // 2], 16)
                    for s in range(2):
                        ps = begin("wo", i, s)
                        part = x2[:, i, s * HALF:(s + 1) * HALF]
                        v.tensor_tensor(part, ps, gate1[:, s * HALF:(s + 1) * HALF], ALU.mult).then_inc(freed_d, 1)
                        dve.wait_ge(freed_d, freed_at[index[("wo", i, s)]][1])
                        v.tensor_tensor(part, part, xr[:, i, s * HALF:(s + 1) * HALF], ALU.add).then_inc(s_x2, 1)
                if 1 <= i <= TILES:
                    ps = begin("x2t", i - 1, 1)
                    if i >= 3:
                        dve.wait_ge(filled, index[("lg", i - 3)] + 1)
                    for j in range(4):
                        last = v.tensor_scalar(h2_t[:, (i - 1) % 2, 4 + j, :], ps[:, j * P:(j + 1) * P],
                                               ab[:, 2, 4 + j:5 + j], ab[:, 3, 4 + j:5 + j], ALU.mult, ALU.add)
                    last.then_inc(freed_d, 1)
                if i >= 2:
                    ps = begin("lg", i - 2)
                    v.tensor_copy(logit[:, (i - 2) * EXPERTS:(i - 1) * EXPERTS], ps[:, 0:EXPERTS]).then_inc(freed_d, 1)
                if i < TILES:
                    dve.wait_ge(s_std, 2 + i + 1)
                    link(v.reciprocal(rstd[:, 1, i:i + 1], rstd[:, 1, i:i + 1]))
                    v.tensor_scalar(xr[:, i, :], x2[:, i, :], rstd[:, 1, i:i + 1], None, ALU.mult).then_inc(s_xhat, 1)

            def te(view):
                return view.rearrange("p (t e) -> p t e", t=TILES)

            def tge(view):
                return view.rearrange("p (g e) -> p g e", e=PER)

            def tg(view):
                return view.rearrange("p (t g) -> p t g", t=TILES)

            def over_e(view, n=EXPERTS):
                return view.unsqueeze(2).broadcast_to([P, TILES, n])

            def over_pe(view):
                return view.unsqueeze(2).broadcast_to([P, TILES * GROUPS, PER])

            def over_t(view, n=EXPERTS):
                return view.unsqueeze(1).broadcast_to([P, TILES, n])

            dve.wait_ge(freed_d, freed_at[index[("lg", TILES - 1)]][1])
            link(v.tensor_reduce(tok[:, 0, :], te(logit), AX_X, ALU.max))
            v.tensor_tensor(te(prob), te(logit), over_e(tok[:, 0, :]), ALU.subtract).then_inc(s_expin, 1)
            dve.wait_ge(s_exp, 1)
            link(v.tensor_reduce(tok[:, 1, :], te(prob), AX_X, ALU.add))
            link(v.reciprocal(tok[:, 1, :], tok[:, 1, :]))
            link(v.tensor_tensor(te(prob), te(prob), over_e(tok[:, 1, :]), ALU.mult))
            dve.wait_ge(s_rb, 80)
            link(v.tensor_tensor(te(sel), te(prob), over_t(router_bb), ALU.add))

            def first_best(values, top, hot, where):
                link(v.tensor_reduce(top, tge(values), AX_X, ALU.max))
                link(v.tensor_tensor(tge(cand), tge(values), over_pe(top), ALU.is_equal))
                link(v.tensor_tensor(te(cand), te(cand), over_t(cst[:, C_REV:C_REV + EXPERTS]), ALU.mult))
                link(v.tensor_reduce(where, tge(cand), AX_X, ALU.max))
                link(v.tensor_tensor(tge(hot), tge(cand), over_pe(where), ALU.is_equal))

            first_best(sel, best[:, 0, :], hot1, best[:, 1, :])
            link(v.scalar_tensor_tensor(sel2, hot1, NEG, sel, ALU.mult, ALU.add))
            first_best(sel2, best[:, 2, :], hot2, best[:, 3, :])
            link(v.tensor_tensor(best[:, 4, :], best[:, 0, :], best[:, 2, :], ALU.add))
            link(v.tensor_reduce(tok[:, 0, :], tg(best[:, 4, :]), AX_X, ALU.max))
            link(v.tensor_tensor(tg(best[:, 5, :]), tg(best[:, 4, :]), over_e(tok[:, 0, :], GROUPS), ALU.is_equal))
            link(v.tensor_tensor(tg(best[:, 5, :]), tg(best[:, 5, :]), over_t(cst[:, C_GREV:C_GREV + GROUPS], GROUPS), ALU.mult))
            link(v.tensor_reduce(tok[:, 1, :], tg(best[:, 5, :]), AX_X, ALU.max))
            link(v.tensor_tensor(tg(best[:, 6, :]), tg(best[:, 5, :]), over_e(tok[:, 1, :], GROUPS), ALU.is_equal))
            link(v.tensor_tensor(tge(hot1), tge(hot1), over_pe(best[:, 6, :]), ALU.mult))
            link(v.tensor_tensor(tge(hot2), tge(hot2), over_pe(best[:, 6, :]), ALU.mult))
            link(v.tensor_tensor(ranks, hot1, hot2, ALU.add))
            v.memset(before[:, 0:EXPERTS], 0.0)
            link(v.tensor_copy(before[:, EXPERTS:2 * EXPERTS], ranks[:, 0:EXPERTS]))
            for i in range(2, TILES):
                ins = v.tensor_tensor(before[:, i * EXPERTS:(i + 1) * EXPERTS], before[:, (i - 1) * EXPERTS:i * EXPERTS],
                                      ranks[:, (i - 1) * EXPERTS:i * EXPERTS], ALU.add)
                if i < TILES - 1:
                    link(ins)
            ins.then_inc(s_sums, 1)

            def picked(dst, values, hot):
                link(v.tensor_tensor(cand, values, hot, ALU.mult))
                link(v.tensor_reduce(dst, te(cand), AX_X, ALU.add))

            picked(tok[:, 2, :], prob, hot1)
            picked(tok[:, 3, :], prob, hot2)
            link(v.tensor_tensor(tok[:, 4, :], tok[:, 2, :], tok[:, 3, :], ALU.add))
            link(v.reciprocal(tok[:, 4, :], tok[:, 4, :]))
            v.tensor_tensor(gate_w[:, 0, :], tok[:, 2, :], tok[:, 4, :], ALU.mult)
            v.tensor_tensor(gate_w[:, 1, :], tok[:, 3, :], tok[:, 4, :], ALU.mult)
            ps_rank = begin("rank")
            v.tensor_copy(sel, ps_rank).then_inc(freed_d, 1)
            ps = begin("count")
            link(v.tensor_copy(cnt[0:EXPERTS, 0:1], ps[0:EXPERTS, 0:1]))
            link(v.tensor_scalar(best[0:EXPERTS, 7, 0:SEQ // BLK], cst[0:EXPERTS, C_THR:C_THR + SEQ // BLK], cnt[0:EXPERTS, 0:1], None, ALU.is_lt))
            link(v.tensor_reduce(cnt[0:EXPERTS, 1:2], best[0:EXPERTS, 7, 0:SEQ // BLK], AX_X, ALU.add))
            link(v.tensor_scalar(cnt[0:EXPERTS, 1:2], cnt[0:EXPERTS, 1:2], 1.0, None, ALU.add))
            v.tensor_scalar(ct_wide[0:EXPERTS, :], ones[0:EXPERTS, :], cnt[0:EXPERTS, 0:1], None, ALU.mult).then_inc(freed_d, 1)
            v.tensor_scalar(nb_wide[0:EXPERTS, :], ones[0:EXPERTS, :], cnt[0:EXPERTS, 1:2], None, ALU.mult).then_inc(s_wide, 1)
            ps = begin("bounds")
            v.tensor_copy(bounds, ps[:, 0:3 * EXPERTS].rearrange("p (a e) -> p a e", a=3)).then_inc(freed_d, 1)
            dve.wait_ge(freed_d, freed_at[index[("bounds",)]][1])
            ends, first_block, first_row = (bounds[:, k, :] for k in range(3))
            link(v.tensor_tensor(te(sel2), te(sel), over_t(first_row), ALU.add))
            picked(tok[:, 5, :], sel2, hot1)
            picked(tok[:, 6, :], sel2, hot2)
            v.tensor_copy(rows_at[:, 0, :], tok[:, 5, :])
            v.tensor_copy(rows_at[:, 1, :], tok[:, 6, :]).then_inc(s_rows, 1)
            number, number_rows = cst[:, C_P:C_P + 1], cst[:, C_PBLK:C_PBLK + 1]
            link(v.tensor_scalar(in_tmp, first_block, number, None, ALU.is_le))
            link(v.scalar_tensor_tensor(in_block, ends, number, in_tmp, ALU.is_gt, ALU.mult))
            link(v.scalar_tensor_tensor(in_tmp, first_block, -float(BLK), first_row, ALU.mult, ALU.add))
            link(v.tensor_tensor(in_tmp, in_tmp, in_block, ALU.mult))
            link(v.tensor_reduce(tab_c, in_tmp, AX_X, ALU.add))
            v.tensor_scalar(tab_c, tab_c, number_rows, float(2 * SEQ), ALU.add, ALU.min).then_inc(s_tabc, 1)
            ps = begin("table")
            v.tensor_copy(table[0:1, T_ROWS:T_ROWS + P], ps[0:1, 0:P]).then_inc(freed_d, 1)
            v.tensor_copy(table[0:1, T_ENDS + 1:T_ROWS], ends[0:1, :])
            v.memset(table[0:1, T_ENDS:T_ENDS + 1], 0)
            v.memset(table[0:1, T_ROWS + P:T_ROWS + MAX_BLOCKS + 2], 2 * SEQ)
            link(v.scalar_tensor_tensor(te(before), over_t(first_block), float(BLK), te(sel), ALU.mult, ALU.add))
            picked(tok[:, 7, :], before, hot1)
            picked(tok[:, 0, :], before, hot2)
            v.tensor_copy(rows_at[:, 2, :], tok[:, 7, :])
            v.tensor_copy(rows_at[:, 3, :], tok[:, 0, :])
            dve.wait_ge(s_gate2, 128)
            link(v.tensor_tensor(gate2, gate2, gate2_b, ALU.add))
            link(v.memset(tok[:, 1, :], 0.0))
            v.memset(tok[:, 1, :], 0.0).then_inc(s_y, 1)
            v.memset(tok[:, 2, :], 0.0).then_inc(s_tab, 1)

            def x_ready(n, first=False):
                dve.wait_ge(s_xtp, n + 1)
                if not first:
                    dve.wait_ge(s_h13, n)
                xt_v = xt_s.rearrange("p j q t -> p (j q) t")
                v.tensor_tensor(xt_v, banks[:, 0, 0:QUART].rearrange("p (a t) -> p a t", a=CH),
                                ab_jq[:, 0, :, :].rearrange("p j q -> p (j q)").unsqueeze(2).broadcast_to([P, CH, BLK]), ALU.mult).then_inc(s_xtm, 1)
                dve.wait_ge(s_xtm, n + 1)
                v.tensor_tensor(xt_v, xt_v, ab_jq[:, 1, :, :].rearrange("p j q -> p (j q)").unsqueeze(2).broadcast_to([P, CH, BLK]), ALU.add).then_inc(s_xts, 1)

            def hidden(n):
                dve.wait_ge(s_silu, n + 1)
                v.tensor_tensor(ff, ff_silu, banks[:, 1, P:2 * P], ALU.mult).then_inc(s_ff, 1)

            def result(n, first=False):
                dve.wait_ge(s_yp, n + 1)
                if not first:
                    dve.wait_ge(s_yst, (n + 1) * 16)
                v.tensor_tensor(y_s, banks[:, 3, 0:QUART], gate2, ALU.mult).then_inc(s_y, 1)

            x_ready(0, True)
            hidden(0)
            x_ready(1)
            hidden(1)
            x_ready(2)
            result(0, True)
            blocks = dve.value_load(table[0:1, T_ENDS + EXPERTS:T_ENDS + EXPERTS + 1], min_val=EXPERTS, max_val=MAX_BLOCKS)
            with dve.Fori(2, blocks) as n:
                hidden(n)
                x_ready(n + 1)
                result(n - 1)
            result(blocks - 1)

            dve.wait_ge(s_x2r, 16)
            dve.wait_ge(s_fg, 16)
            for i in range(TILES + 1):
                if i < TILES:
                    total_i = at(3 * EXPERT_FLOATS + i * D, D)
                    dve.wait_ge(s_t1, i + 1)
                    v.scalar_tensor_tensor(total_i, at(2 * EXPERT_FLOATS + i * D, D), gate_w[:, 1, i:i + 1], at(EXPERT_FLOATS + i * D, D),
                                           ALU.mult, ALU.add).then_inc(s_t2, 1)
                    dve.wait_ge(s_t2, i + 1)
                    v.tensor_tensor(total_i, total_i, at(i * D, D), ALU.add).then_inc(s_t3, 1)
                if i >= 1:
                    dve.wait_ge(s_std, 2 + TILES + i)
                    link(v.reciprocal(rstd[:, 2, i - 1:i], rstd[:, 2, i - 1:i]))
                    total_i = at(3 * EXPERT_FLOATS + (i - 1) * D, D)
                    v.scalar_tensor_tensor(total_i, total_i, rstd[:, 2, i - 1:i], at(8192, D), ALU.mult, ALU.mult).then_inc(s_tout, 1)


def kernel(x, c, ln1_g, ln2_g, w_ada, b_ada, w_in, w_out, conv_w, conv_b, conv_gn_g, conv_gn_b,
           sgu_ln_g, sgu_ln_b, sgu_w, sgu_b, router_w, router_b, exp_w1, exp_w3, exp_w2, final_g):
    import numpy as np
    from concourse import bacc
    from concourse.bass_utils import run_bass_kernel_spmd

    p = np.arange(P)
    consts = np.zeros((P, C_END), np.float32)
    consts[:, C_ID:C_ID + P] = np.eye(P)
    consts[:, C_TRI:C_TRI + P] = p[:, None] < p[None, :]
    consts[:, C_ONE:C_ONE + P] = 1.0
    consts[:, C_BD:C_BD + P] = (p[:, None] // 64 == p[None, :] // 64) / 64.0
    angle = 2 * np.pi * ((p[:, None] % 64) * (p[None, :] % 64) % 64) / 64.0
    same = (p[:, None] // 64 == p[None, :] // 64) / np.sqrt(64.0 * SEQ)
    consts[:, C_DFT:C_DFT + P] = np.cos(angle) * same
    consts[:, C_DFT + P:C_DFT + 2 * P] = np.sin(angle) * same
    e = np.arange(EXPERTS)
    consts[0:EXPERTS, C_EXC:C_EXC + EXPERTS] = e[:, None] < e[None, :]
    consts[0:EXPERTS, C_INC:C_INC + EXPERTS] = e[:, None] <= e[None, :]
    consts[:, C_REV:C_REV + EXPERTS] = PER - e % PER
    consts[:, C_GREV:C_GREV + GROUPS] = GROUPS - np.arange(GROUPS)
    consts[:, C_THR:C_THR + SEQ // BLK] = BLK * (1 + np.arange(SEQ // BLK))
    consts[:, C_P] = p
    consts[:, C_PBLK] = BLK * p
    consts[:, C_ALT] = 1.0 - 2.0 * (p % 2)
    pos = np.arange(SEQ)
    turn = 2 * np.pi * (pos[:, None] * np.arange(HALF)[None, :] % SEQ) / SEQ
    dft = np.stack([np.cos(turn), np.sin(turn)]).astype(np.float32).reshape(2, TILES, P, HALF)
    dft = np.ascontiguousarray(dft.transpose(2, 0, 1, 3))

    inputs = dict(x=x[0], c=c, ln1_g=ln1_g[0], ln2_g=ln2_g[0], w_ada=w_ada[0], b_ada=b_ada[0], w_in=w_in[0], w_out=w_out[0],
                  conv_w=conv_w[0], conv_b=conv_b[0], conv_gn_g=conv_gn_g[0], conv_gn_b=conv_gn_b[0], sgu_ln_g=sgu_ln_g[0],
                  sgu_ln_b=sgu_ln_b[0], sgu_w=sgu_w[0], sgu_b=sgu_b[0], router_w=router_w, router_b=router_b,
                  exp_w1=exp_w1[0], exp_w3=exp_w3[0], exp_w2=exp_w2[0], final_g=final_g, consts=consts, dft=dft)
    nc = bacc.Bacc("TRN2", target_bir_lowering=False, num_devices=1)
    arrays, args = {}, []
    for name, a in inputs.items():
        a = np.ascontiguousarray(a)
        arrays[f"in_{name}"] = a
        args.append(nc.dram_tensor(f"in_{name}", a.shape, mybir.dt.from_np(a.dtype), kind="ExternalInput").ap())
    out = nc.dram_tensor("out", (SEQ, D), F32, kind="ExternalOutput").ap()
    build(nc, *args, out)
    r = run_bass_kernel_spmd(nc, [arrays], core_ids=[0])
    return r.results[0]["out"].reshape(1, SEQ, D)
```

```python
from contextlib import ExitStack

import concourse.bass as bass
from concourse import mybir

ALU = mybir.AluOpType
ACT = mybir.ActivationFunctionType
AX_X = mybir.AxisListType.X
F32 = mybir.dt.float32
I32 = mybir.dt.int32

P = 128
SEQ = 1024
D = 1024
TILES = SEQ // P
CH = D // P
HALF = 512
QUART = D // 4
CONV, FOUR, SGU = 384, 256, 384
TAPS = 31
PAD = TAPS // 2
PADW = SEQ + 2 * PAD
WIN = 2 * CONV + FOUR + 2 * SGU
EXPERTS, GROUPS, PER = 64, 8, 8
FF = 512
BLK = 32
SLOTS = 4
EXPERT_FLOATS = 3 * 4096
MAX_BLOCKS = EXPERTS + 2 * SEQ // BLK
EPS = 1e-6
BANKS = 8
EARLY = 4
AHEAD = 2
NEG = -3.0e38
C_ID, C_TRI, C_ONE, C_BD, C_DFT, C_EXC, C_INC, C_REV = 0, 128, 256, 384, 512, 768, 832, 896
C_GREV, C_THR, C_ALT, C_END = 960, 968, 1000, 1001
L_BLOCK, L_ROW, L_INDEX, L_QUARTER, L_REPEAT, L_END = 0, 128, 160, 168, 169, 297

RING = SLOTS * EXPERT_FLOATS
O_V = 0
O_WIN = O_V + 8 * SGU
O_WOUT = O_WIN + 8 * WIN - 8 * D
O_Y = O_WIN + 8 * WIN
O_D = O_Y + 8 * SEQ
O_H = O_D + 2 * 4096
O_PADH = O_H + 8 * SEQ
O_SMALL = O_PADH + 3 * PADW
assert O_H <= 3 * EXPERT_FLOATS - 2048 and 3 * EXPERT_FLOATS + 8192 <= O_SMALL and 8192 <= O_WOUT


def build(nc, x, c, ln1_g, ln2_g, w_ada, b_ada, w_in, w_out, conv_w, conv_b, conv_gn_g, conv_gn_b,
          sgu_ln_g, sgu_ln_b, sgu_w, sgu_b, router_w, router_b, exp_w1, exp_w3, exp_w2, final_g,
          consts, dft, out):
    ctx = ExitStack()
    with ctx:
        def sem(name):
            return ctx.enter_context(nc.semaphore(name))

        banks = ctx.enter_context(nc.psum_tensor("banks", [P, BANKS, HALF], F32))
        total = RING + 3360
        arena = ctx.enter_context(nc.sbuf_tensor("arena", [P, total], F32))
        table = ctx.enter_context(nc.sbuf_tensor("table", [1, EXPERTS + 1], I32))
        rows_at = ctx.enter_context(nc.sbuf_tensor("rows_at", [P, 3, 2 * TILES], I32))
        where = ctx.enter_context(nc.sbuf_tensor("where", [P, 1], I32))
        quarters = ctx.enter_context(nc.sbuf_tensor("quarters", [P, MAX_BLOCKS + 2], I32))
        mod_dram = nc.dram_tensor("mod_dram", [6 * D], F32)
        x2_dram = nc.dram_tensor("x2_dram", [SEQ, D], F32)
        xh_dram = nc.dram_tensor("xh_dram", [SEQ * 4, QUART], F32)
        ys_dram = nc.dram_tensor("ys_dram", [(MAX_BLOCKS + 1) * BLK, D], F32)

        def at(offset, *shape):
            n = 1
            for s in shape:
                n *= s
            view = arena[:, offset:offset + n]
            if len(shape) == 2:
                view = view.rearrange("p (a b) -> p a b", a=shape[0])
            if len(shape) == 3:
                view = view.rearrange("p (a b c) -> p a b c", a=shape[0], b=shape[1])
            return view

        v_t = at(O_V, TILES, SGU)
        pad_h = at(O_PADH, 3, PADW)
        squares = at(O_PADH, 6, HALF)
        w_in_s = at(O_WIN, CH, WIN)
        w_out_s = at(O_WOUT, CH, D)
        y_t = at(O_Y, CH, SEQ)
        x_t = at(O_Y, TILES, D)
        xt_four = y_t[:, 3:5, :]
        ada_s = at(O_D, 2, CH * HALF).rearrange("p a (c f) -> p a c f", c=CH)
        pq = at(O_WIN, TILES, 2 * 256).rearrange("p a (c f) -> p a c f", c=2)
        dft_s = at(O_D, 2, TILES, HALF)
        xr = at(O_D, 4, D)
        h2_t = at(O_V, 2, CH, P)
        gate1 = at(O_V + 2 * D, D)
        gate1_b = at(O_V + 3 * D, D)
        h_t = at(O_H, CH, SEQ)
        x2 = at(O_D + 4 * D, 4, D)

        used = {"mixing": O_SMALL, "kept": RING}
        most = {"mixing": RING, "kept": total}

        def small(*shape, life="mixing"):
            n = 1
            for s in shape:
                n *= s
            used[life] += n
            assert used[life] <= most[life], (life, used[life] - most[life])
            return at(used[life] - n, *shape)

        cst = small(C_END)
        tri, ones, bd = (cst[:, o:o + P] for o in (C_TRI, C_ONE, C_BD))
        ws_t = small(6, P)
        vec_rows = small(P)
        vecs = small(16)
        conv_t = small(3 * TAPS)
        gain_k = small(3, P)
        bs_b = small(3, P)
        c_col, c_act, c_wide = small(CH), small(CH), small(CH, 32)
        col = small(10, CH)
        LN1, LN2, SH1, SC1, SH2, SC2, BSH1, BSC1, BSH2, BSC2 = range(10)
        ab = small(4, CH)
        stats, mv, v_rstd = small(TILES, 6), small(TILES, 2), small(TILES)
        mod_rows = small(P)
        head_rows = at(O_V + 9 * P, 4, P)
        router_s = small(CH, EXPERTS)
        router_bb = small(EXPERTS)
        ws_rows = at(O_V, 6, P)
        conv_rows = at(O_V + 6 * P, CONV)
        ident = small(P, life="kept")
        ab_jq = small(2, 2, 4, life="kept")
        ss, rstd = small(3, TILES, life="kept"), small(3, TILES, life="kept")
        eps = small(1, life="kept")
        gate_w = small(2, TILES, life="kept")
        scratch = small(D, life="kept")
        tmp_a, tmp_b, logit = (small(HALF, life="kept") for _ in range(3))
        gate2 = small(QUART, life="kept")
        xrow = tmp_a[:, 0:QUART]
        xrow_next = tmp_a[:, QUART:2 * QUART]
        xt_s = tmp_b[:, 0:QUART].rearrange("p (j q t) -> p j q t", j=2, q=4)
        y_s = logit[:, 0:QUART]
        ff_silu, ff, ff_t = scratch[:, 0:P], scratch[:, 256:256 + P], scratch[:, 512:512 + P]
        gate2_b = tmp_b[:, 0:QUART]
        late = tmp_a[:, 0:L_END]

        r0 = 4096
        prob, sel, sel2, hot1, hot2, cand, ranks, before = (at(r0 + i * HALF, HALF) for i in range(8))
        best = tmp_b.rearrange("p (a g) -> p a g", a=8)
        tok = tmp_a[:, 304:368].rearrange("p (a t) -> p a t", a=8)
        cnt, nb_wide = scratch[:, 0:4], scratch[:, P:2 * P]
        bounds = scratch[:, 2 * P:3 * P].rearrange("p (a e) -> p a e", a=2)
        in_block, in_row = at(r0, 2 * TILES, P), at(r0 + 2 * TILES * P, 2 * TILES, BLK)
        rows_list = at(r0 + 2 * TILES * (P + BLK), P)
        place = scratch[:, 3 * P:3 * P + 4 * TILES].rearrange("p (a m) -> p a m", a=2)

        def d_cols(vector):
            return vector.rearrange("(q p j) -> p q j", q=4, j=2)

        def d_tile(view):
            return view.rearrange("p (q j) -> p q j", q=4)

        def chunk(view, k):
            first = QUART * (k // 2) + k % 2
            return view[:, first:first - k % 2 + QUART:2]

        s_cst, s_vrows, s_convw, s_ws, s_small, s_c, s_cols = (sem(n) for n in (
            "consts_in", "vector_rows_in", "conv_w_in", "sgu_w_in", "sgu_b_in", "c_in", "columns_in"))
        s_x = [sem(f"x_in{i}") for i in range(2)]
        s_ada = [sem(f"ada_in{i}") for i in range(2)]
        s_win = [sem(f"w_in_in{i}") for i in range(4)]
        s_xr = [sem(f"x_again_in{i}") for i in range(TILES)]
        s_dft, s_wout, s_gate1, s_gate2, s_rb = (sem(n) for n in (
            "dft_in", "w_out_in", "gate1_in", "gate2_in", "router_in"))
        filled, freed_a, freed_d = sem("bank_filled"), sem("bank_freed_by_act"), sem("bank_freed_by_dve")
        s_modout, s_modcols = sem("mod_rows_stored"), sem("mod_columns_in")
        s_eps, s_std, s_mv, s_vstd = (sem(n) for n in ("eps_ready", "deviations_ready", "v_variances", "v_deviations"))
        s_cact, s_cwide, s_ss, s_xhat, s_ab = (sem(n) for n in (
            "c_act_ready", "c_wide_ready", "squares_summed", "xhat_ready", "affine_ready"))
        s_zero, s_conv, s_gnsq, s_gnn, s_gn = (sem(n) for n in (
            "pad_zeroed", "conv_step", "centred_squared", "gn_scaled", "gn_ready"))
        s_vn, s_sg, s_x2, s_x2st, s_xhst = (sem(n) for n in (
            "v_ready", "gating_ready", "x2_ready", "x2_stored", "xhat_stored"))
        s_link = sem("dve_step")
        s_expin, s_exp, s_sums, s_wide, s_hot, s_late, s_tab, s_index = (sem(n) for n in (
            "logits_shifted", "exp_ready", "rank_inputs_ready", "counts_wide_ready", "places_ready",
            "late_constants_in", "table_ready", "index_list_ready"))
        s_zeros, s_yzero = sem("zeros_ready"), sem("result_rows_zeroed")
        s_w = [[sem(f"slot{i}_{what}_in") for what in ("w1a", "w1b", "w3a", "w3b", "w2a", "w2b")] for i in range(SLOTS)]
        s_xrow, s_xcopy = sem("block_rows_in"), sem("block_rows_moved")
        s_xtp, s_xtm, s_xts, s_h13, s_silu, s_ff, s_ftp, s_ft, s_yp, s_y, s_yst = (sem(n) for n in (
            "block_rows_transposed", "block_x_scaled", "block_x_ready", "block_h_ready", "block_silu", "block_ff",
            "block_ff_transposed", "block_ff_t_ready", "block_y_filled", "block_y_ready_plus_one", "block_y_stored_plus_one"))
        s_begun, s_where, s_gathers, s_through = sem("experts_begun"), sem("column_ready"), sem("gathers_begun"), sem("blocks_through")
        s_x2r, s_fg = sem("x2_again_in"), sem("final_g_in")
        s_gat = [sem(f"rows_gathered{i}") for i in range(TILES)]
        s_t1, s_t2, s_t3, s_tout, s_out = (sem(n) for n in (
            "tail_first", "tail_both", "tail_sum", "tail_ready", "out_stored"))

        order = []
        for n in range(5):
            if n < 4:
                order += [("ada", n, "d")]
            if n:
                order += [("column", n - 1, "d")]
            if n == 2:
                order += [("small", "d"), ("ws", 0, "d"), ("ws", 1, "d"), ("rs", "d")]
        order += [("xt", i, h, "ad"[h]) for i in range(TILES // 2) for h in range(2)]
        order += [("g", 0, 0, "a")]
        order += [("xt", i, h, "ad"[h]) for i in range(TILES // 2, TILES) for h in range(2)]
        ada_left = list(range(4, 12))
        for cc in range(3):
            for s in range(2):
                if cc or s:
                    order += [("g", cc, s, "a")]
                order += [("a", cc, s, "d")]
                if cc or s:
                    order += [("ada", ada_left.pop(0), "a")]
        for cc in range(2):
            for s in range(2):
                order += [("b", cc, s, "a")]
                if ada_left:
                    order += [("ada", ada_left.pop(0), "a")]
        order += [("v", i, "a") for i in range(TILES)]
        order += [("gm", cc, s, "d") for cc in range(3) for s in range(2)]
        order += [("u", 0, s, "a") for s in range(2)]
        order += [("gv", cc, s, "a") for cc in range(3) for s in range(2)]
        order += [("u", cc, s, "a") for cc in range(1, 3) for s in range(2)]
        order += [("pq", i, "a") for i in range(TILES)]
        order += [("sg", j, hh, "d") for j in range(3) for hh in range(2)]
        order += [("V", 0, "a"), ("U", 0, "d"), ("mid", "d"), ("V", 1, "a"), ("U", 1, "d")]
        for i in range(TILES + 2):
            if i < TILES:
                order += [("wo", i, 0, "d"), ("wo", i, 1, "d")]
            if 1 <= i <= TILES:
                order += [("x2t", i - 1, 0, "a"), ("x2t", i - 1, 1, "d")]
            if i >= 2:
                order += [("lg", i - 2, "d")]
        order += [("rank", "d"), ("count", "d"), ("bounds", "d"), ("index", "d"), ("repeat", "d")]
        index = {entry[:-1]: g for g, entry in enumerate(order)}
        seen = {"a": 0, "d": 0}
        freed_at = []
        for entry in order:
            seen[entry[-1]] += 1
            freed_at.append((entry[-1], seen[entry[-1]]))

        def bank_of(*key):
            return banks[:, index[key] % BANKS, :]

        def full(eng, *key):
            eng.wait_ge(filled, index[key] + 1)

        block = ctx.enter_context(nc.Block())

        def ada_load(q, n):
            if n >= 2:
                q.wait_ge(filled, index[("ada", n - 2)] + 1)
            q.dma_start(ada_s[:, n % 2, :, :], w_ada.rearrange("(p c) f -> p c f", c=CH)[:, :, n * HALF:(n + 1) * HALF]
                        ).then_inc(s_ada[n % 2], 16)

        @block.sync
        def _(sp):
            sp.dma_start(cst, consts[:, 0:C_END]).then_inc(s_cst, 16)
            sp.dma_start(ident, consts[:, C_ID:C_ID + P]).then_inc(s_cst, 16)
            sp.dma_start(c_col, c.rearrange("a (p c) -> p (a c)", c=CH)).then_inc(s_c, 16)
            for n in range(2):
                ada_load(sp, n)
            sp.dma_start(x_t[:, 0:4, :], x.rearrange("(t p) d -> p t d", p=P)[:, 0:4, :]).then_inc(s_x[0], 16)
            ada_load(sp, 2)
            ada_load(sp, 3)
            sp.dma_start(x_t[:, 4:8, :], x.rearrange("(t p) d -> p t d", p=P)[:, 4:8, :]).then_inc(s_x[1], 16)
            for part, (f0, f1) in enumerate(((0, 2 * CONV), (2 * CONV, 1024), (1024 + SGU, WIN), (1024, 1024 + SGU))):
                for q in range(4):
                    sp.dma_start(w_in_s[:, 2 * q:2 * q + 2, f0:f1],
                                 w_in[q * QUART:(q + 1) * QUART, f0:f1].rearrange("(p j) f -> p j f", j=2)
                                 ).then_inc(s_win[part], 16)
                if part < 2:
                    for n in (4 + 2 * part, 5 + 2 * part):
                        ada_load(sp, n)
            for n in range(8, 12):
                ada_load(sp, n)
            sp.wait_ge(filled, index[("ada", 11)] + 1)
            sp.dma_start(dft_s, dft).then_inc(s_dft, 16)
            sp.wait_ge(filled, index[("u", 2, 1)] + 1)
            sp.dma_start(w_out_s, w_out.rearrange("(c p) d -> p c d", p=P)).then_inc(s_wout, 16)
            def piece(e, slot, k):
                u, h = k // 2, k % 2
                if u < 2:
                    src = (exp_w1, exp_w3)[u][bass.ds(e, 1), h * 512:(h + 1) * 512, :].rearrange("e (q p j) f -> (e p) q (j f)", q=2, j=2)
                else:
                    src = exp_w2[bass.ds(e, 1), h * 256:(h + 1) * 256, :].rearrange("e (k p) d -> (e p) k d", k=2)
                sp.dma_start(at(slot * EXPERT_FLOATS + k * 2048, 2, D), src).then_inc(s_w[slot][k], 16)

            for k in range(2):
                piece(3, 3, k)
            piece(2, 2, 5)
            sp.wait_ge(filled, index[("U", 1)] + 1)

            def x_again(i):
                sp.dma_start(xr[:, i % 4, :], x[i * P:(i + 1) * P, :]).then_inc(s_xr[i], 16)

            for i in range(4):
                x_again(i)
            sp.wait_ge(s_modout, 64 * 8)
            sp.wait_ge(filled, index[("sg", 2, 1)] + 1)
            sp.dma_start(gate1, mod_dram.ap()[2 * D:3 * D].partition_broadcast(P)).then_inc(s_gate1, 16)
            sp.dma_start(gate1_b, b_ada[2 * D:3 * D].partition_broadcast(P)).then_inc(s_gate1, 16)

            sp.wait_ge(s_gnn, 6)
            for k in range(2, 4):
                piece(3, 3, k)
            sp.wait_ge(freed_d, freed_at[index[("U", 1)]][1])
            sp.dma_start(late, consts[:, C_END:C_END + L_END]).then_inc(s_late, 16)

            def rows_out(i):
                sp.wait_ge(s_x2, 2 * i + 2)
                sp.dma_start(x2_dram.ap()[i * P:(i + 1) * P, :], x2[:, i % 4, :]).then_inc(s_x2st, 16)
                sp.wait_ge(s_xhat, TILES + i + 1)
                sp.dma_start(xh_dram.ap()[4 * i * P:4 * (i + 1) * P, :].rearrange("(t q) c -> t (q c)", q=4), xr[:, i % 4, :]).then_inc(s_xhst, 16)

            for i in range(TILES - 1):
                rows_out(i)
                if i < 4:
                    sp.wait_ge(filled, index[("x2t", i, 1)] + 1)
                    sp.wait_ge(s_xhst, 16 * (i + 1))
                    x_again(i + 4)
            sp.wait_ge(filled, index[("wo", TILES - 1, 1)] + 1)
            for k in range(6):
                piece(1, 1, k)
            for k in range(4, 6):
                piece(0, 0, k)
            rows_out(TILES - 1)
            sp.wait_ge(filled, index[("lg", TILES - 1)] + 1)
            for k in range(2):
                piece(0, 0, k)
            sp.wait_ge(s_xhst, 16 * TILES)
            sp.wait_ge(s_x2st, 16 * TILES)
            for k in range(5):
                piece(2, 2, k)
            sp.wait_ge(s_index, 1)
            for k in range(2, 4):
                piece(0, 0, k)
            for k in range(4, 6):
                piece(3, 3, k)
            with sp.Fori(0, EXPERTS // SLOTS - 1) as r:
                for slot in range(SLOTS):
                    end = sp.value_load(table[0:1, bass.ds(r * SLOTS + (1 + slot), 1)], min_val=1, max_val=MAX_BLOCKS)
                    for k in range(6):
                        if k == 0:
                            sp.wait_ge(s_h13, end)
                        if k == 4:
                            sp.wait_ge(s_yp, end)
                        before, rounds = (slot, r + 2) if k >= AHEAD else ((slot - 1) % SLOTS, r + (2 if slot else 1))
                        sp.wait_ge(s_w[before][(k - AHEAD) % 6], rounds * 16)
                        piece(r * SLOTS + (SLOTS + slot), slot, k)
            end = sp.value_load(table[0:1, EXPERTS - SLOTS + 1:EXPERTS - SLOTS + 2], min_val=1, max_val=MAX_BLOCKS)
            sp.wait_ge(s_yp, end)
            sp.dma_start(at(0, TILES, D), x2_dram.ap().rearrange("(t p) d -> p t d", p=P)).then_inc(s_x2r, 16)
            sp.dma_start(at(8192, D), final_g.partition_broadcast(P)).then_inc(s_fg, 16)
            for i in range(TILES):
                sp.wait_ge(s_tout, i + 1)
                sp.dma_start(out[i * P:(i + 1) * P, :], at(3 * EXPERT_FLOATS + i * D, D)).then_inc(s_out, 16)
            sp.wait_ge(s_out, 16 * TILES)

        @block.gpsimd
        def _(pool):
            for r, vec in enumerate((conv_b, conv_gn_g, conv_gn_b, sgu_ln_g, sgu_ln_b)):
                pool.dma_start(vec_rows[3 * r:3 * r + 3, :], vec.rearrange("(a f) -> a f", f=P)).then_inc(s_vrows, 16)
            pool.dma_start(conv_rows[0:TAPS, 0:CONV], conv_w).then_inc(s_convw, 16)
            pool.dma_start(ws_rows, sgu_w.rearrange("h p q -> p h q")).then_inc(s_ws, 16)
            for n, vec in ((LN1, ln1_g), (LN2, ln2_g)):
                pool.dma_start(d_tile(col[:, n, :]), d_cols(vec)).then_inc(s_cols, 16)
            for n, m in ((BSH1, 0), (BSC1, 1), (BSH2, 3), (BSC2, 4)):
                pool.dma_start(d_tile(col[:, n, :]), d_cols(b_ada[m * D:(m + 1) * D])).then_inc(s_cols, 16)
            for h in range(6):
                pool.dma_start(bs_b[64 * (h % 2):64 * (h % 2) + 64, h // 2, :], sgu_b[h, :].partition_broadcast(64)).then_inc(s_small, 16)
            for q in range(4):
                pool.dma_start(router_s[:, 2 * q:2 * q + 2, :], router_w[q * QUART:(q + 1) * QUART, :].rearrange("(p j) e -> p j e", j=2)
                               ).then_inc(s_rb, 16)
            pool.dma_start(router_bb, router_b.partition_broadcast(P)).then_inc(s_rb, 16)
            pool.memset(pad_h[:, :, 0:PAD], 0.0).then_inc(s_zero, 1)
            pool.memset(pad_h[:, :, PAD + SEQ:PADW], 0.0).then_inc(s_zero, 1)
            for n in range(4, 12):
                who, count = freed_at[index[("ada", n)]]
                pool.wait_ge(freed_a if who == "a" else freed_d, count)
                for q in range(4):
                    pool.dma_start(mod_dram.ap()[n * HALF + q * P:n * HALF + (q + 1) * P].rearrange("(a f) -> a f", a=1),
                                   mod_rows[32 * q:32 * q + 1, :]).then_inc(s_modout, 16)
            pool.wait_ge(s_modout, 64 * 8)
            for k, m in ((SH2, 3), (SC2, 4)):
                pool.dma_start(d_tile(col[:, k, :]), d_cols(mod_dram.ap()[m * D:(m + 1) * D])).then_inc(s_modcols, 16)
            pool.wait_ge(s_ss, TILES)
            pool.memset(scratch, 0.0).then_inc(s_zeros, 1)
            pool.wait_ge(s_zeros, 1)
            for n in range(EXPERTS * BLK, (MAX_BLOCKS + 1) * BLK, P):
                rows = min(P, (MAX_BLOCKS + 1) * BLK - n)
                pool.dma_start(ys_dram.ap()[n:n + rows, :], scratch[0:rows, :]).then_inc(s_yzero, 16)
            pool.wait_ge(freed_d, freed_at[index[("U", 1)]][1])
            for q in range(4):
                for dst, src in ((gate2, mod_dram.ap()), (gate2_b, b_ada)):
                    pool.dma_start(dst[32 * q:32 * q + 32, :],
                                   src[5 * D + q * QUART:5 * D + (q + 1) * QUART].partition_broadcast(32)).then_inc(s_gate2, 16)
            pool.wait_ge(s_index, 1)
            pool.wait_ge(s_xhst, 16 * TILES)

            def rows_in(n):
                pool.tensor_copy(where[:, 0:1], quarters[:, bass.ds(n, 1)]).then_inc(s_where, 1)
                pool.wait_ge(s_where, n + 1)
                pool.sem_inc(s_gathers, 1)
                pool.indirect_dma_start(out=xrow_next, out_offset=None, in_=xh_dram.ap(),
                                        in_offset=bass.IndirectOffsetOnAxis(ap=where[:, 0:1], axis=0)).then_inc(s_xrow, 16)

            rows_in(0)
            blocks = pool.value_load(table[0:1, EXPERTS:EXPERTS + 1], min_val=EXPERTS, max_val=MAX_BLOCKS)
            with pool.Fori(1, blocks + 2) as n:
                pool.wait_ge(s_xcopy, n)
                rows_in(n)
            pool.wait_ge(s_yst, (blocks + 1) * 16)
            pool.sem_inc(s_through, 1)
            for i in range(TILES):
                for k in range(2):
                    pool.indirect_dma_start(out=at((k + 1) * EXPERT_FLOATS + i * D, D), out_offset=None, in_=ys_dram.ap(),
                                            in_offset=bass.IndirectOffsetOnAxis(ap=rows_at[:, 0, k * TILES + i:k * TILES + i + 1], axis=0)
                                            ).then_inc(s_gat[i], 16)

        @block.tensor
        def _(pe):
            def begin(*key):
                g = index[key]
                if g >= BANKS:
                    who, count = freed_at[g - BANKS]
                    pe.wait_ge(freed_a if who == "a" else freed_d, count)
                return bank_of(*key)

            pe.wait_ge(s_cst, 32)
            def ada_columns(n):
                ps = begin("column", n)
                pe.wait_ge(freed_d, freed_at[index[("ada", n)]][1])
                for q in range(2):
                    for j in range(2):
                        for e in range(2):
                            k, lane = 2 * q + j, 32 * (2 * q + e)
                            last = pe.matmul(ps[64 * e:64 * e + 64, k:k + 1], head_rows[:, n, j:P:2], ident[:, lane:lane + 1],
                                             start=True, stop=True, skip_group_check=True)
                last.then_inc(filled, 1)

            def ada(n):
                ps = begin("ada", n)
                if n == 0:
                    pe.wait_ge(s_cwide, 1)
                pe.wait_ge(s_ada[n % 2], 16 * (n // 2 + 1))
                for k in range(CH):
                    for q in range(4):
                        last = pe.matmul(ps[32 * q:32 * q + 32, 0:P], c_wide[:, k, :], ada_s[:, n % 2, k, q * P:(q + 1) * P],
                                         start=(k == 0), stop=(k == CH - 1), tile_position=(0, 32 * q))
                last.then_inc(filled, 1)

            def small_ones():
                ps = begin("small")
                pe.wait_ge(s_vrows, 16 * 5)
                pe.wait_ge(s_convw, 16)
                pe.transpose(ps[:, 0:15], vec_rows[0:15, :], ident[0:15, 0:15])
                for cc in range(3):
                    last = pe.transpose(ps[:, 16 + cc * TAPS:16 + (cc + 1) * TAPS], conv_rows[0:TAPS, cc * P:(cc + 1) * P], ident[0:TAPS, 0:TAPS])
                last.then_inc(filled, 1)
                pe.wait_ge(s_ws, 16)
                for g in range(2):
                    ps = begin("ws", g)
                    for k in range(3):
                        h = 3 * g + k
                        last = pe.transpose(ps[:, k * P:(k + 1) * P], ws_rows[:, h, :], ident)
                    last.then_inc(filled, 1)
                ps = begin("rs")
                pe.wait_ge(freed_d, freed_at[index[("ws", 1)]][1])
                for h in range(6):
                    last = pe.matmul(ps[64 * (h % 2):64 * (h % 2) + 64, (h // 2) * P:(h // 2 + 1) * P], ones[:, 0:64], ws_t[:, h, :],
                                     start=True, stop=True, skip_group_check=True)
                last.then_inc(filled, 1)

            for n in range(5):
                if n < 4:
                    ada(n)
                if n:
                    ada_columns(n - 1)
                if n == 2:
                    small_ones()

            def x_tiles(half):
                for i in range(4 * half, 4 * half + 4):
                    pe.wait_ge(s_xhat, i + 1)
                    for h in range(2):
                        ps = begin("xt", i, h)
                        for j in range(4):
                            last = pe.transpose(ps[:, j * P:(j + 1) * P], chunk(x_t[:, i, :], 4 * h + j), ident)
                        last.then_inc(filled, 1)

            def h_ready(s):
                for h in range(2):
                    who, count = freed_at[index[("xt", 4 * s + 3, h)]]
                    pe.wait_ge(freed_a if who == "a" else freed_d, count)

            def z_cols(ps, f0, s):
                for k in range(CH):
                    last = pe.matmul(ps, w_in_s[:, k, f0:f0 + P], h_t[:, k, s * HALF:(s + 1) * HALF], start=(k == 0), stop=(k == CH - 1))
                last.then_inc(filled, 1)

            x_tiles(0)
            for g, entry in enumerate(order):
                key = entry[:-1]
                kind = key[0]
                if kind in ("small", "ws", "rs", "xt", "column") or kind == "ada" and key[1] < 4:
                    continue
                if kind == "ada":
                    ada(key[1])
                    continue
                ps = begin(*key)
                if kind in ("g", "a"):
                    if g == index[("g", 0, 0)]:
                        pe.wait_ge(s_win[0], 64)
                    if key[1] == 0:
                        h_ready(key[2])
                    z_cols(ps, (CONV if kind == "g" else 0) + key[1] * P, key[2])
                    if key == ("g", 0, 0):
                        x_tiles(1)
                elif kind == "b":
                    pe.wait_ge(s_win[1], 64)
                    z_cols(ps, 2 * CONV + key[1] * P, key[2])
                elif kind == "v":
                    pe.wait_ge(s_win[2], 64)
                    i = key[1]
                    for k in range(CH):
                        last = pe.matmul(ps[:, 0:SGU], h_t[:, k, i * P:(i + 1) * P], w_in_s[:, k, 1024 + SGU:WIN], start=(k == 0), stop=(k == CH - 1))
                    last.then_inc(filled, 1)
                elif kind == "u":
                    pe.wait_ge(s_win[3], 64)
                    z_cols(ps, 1024 + key[1] * P, key[2])
                elif kind == "pq":
                    i = key[1]
                    if i == 0:
                        pe.wait_ge(freed_a, freed_at[index[("b", 1, 1)]][1])
                    for cc in range(2):
                        last = pe.matmul(ps[:, cc * 256:(cc + 1) * 256], xt_four[:, cc, i * P:(i + 1) * P], cst[:, C_DFT:C_DFT + 256],
                                         start=True, stop=True, skip_group_check=True)
                    last.then_inc(filled, 1)
                elif kind in ("U", "V"):
                    pe.wait_ge(freed_a, freed_at[index[("pq", TILES - 1)]][1])
                    pe.wait_ge(s_dft, 16)
                    t = 0 if kind == "U" else 1
                    for k in range(TILES):
                        last = pe.matmul(ps, pq[:, k, key[1], t * P:(t + 1) * P], dft_s[:, t, k, :], start=(k == 0), stop=(k == TILES - 1))
                    last.then_inc(filled, 1)
                elif kind == "mid":
                    for cc in range(2):
                        for k in range(TILES):
                            last = pe.matmul(ps[:, cc:cc + 1], pq[:, k, cc, 0:P], cst[:, C_ALT:C_ALT + 1],
                                             start=(k == 0), stop=(k == TILES - 1), skip_group_check=True)
                    last.then_inc(filled, 1)
                elif kind == "gm":
                    pe.wait_ge(s_conv, TAPS * (key[1] + 1))
                    pe.matmul(ps, bd, y_t[:, key[1], key[2] * HALF:(key[2] + 1) * HALF], start=True, stop=True).then_inc(filled, 1)
                elif kind == "gv":
                    n = 2 * key[1] + key[2]
                    pe.wait_ge(s_gnsq, n + 1)
                    pe.matmul(ps, bd, squares[:, n, :], start=True, stop=True).then_inc(filled, 1)
                elif kind == "sg":
                    j, hh = key[1:]
                    pe.wait_ge(s_vn, 4 * hh + 4)
                    for i in range(4):
                        for e in range(2):
                            h = 2 * j + e
                            last = pe.matmul(ps[64 * e:64 * e + 64, i * P:(i + 1) * P], v_t[:, 4 * hh + i, h * 64:(h + 1) * 64], ws_t[:, h, :],
                                             start=True, stop=True, skip_group_check=True)
                    last.then_inc(filled, 1)
                elif kind == "wo":
                    i, s = key[1:]
                    if (i, s) == (0, 0):
                        pe.wait_ge(s_wout, 16)
                        pe.wait_ge(freed_d, freed_at[index[("U", 1)]][1])
                        pe.wait_ge(s_sg, 6)
                        pe.wait_ge(s_gn, 6)
                    for n, k in enumerate((0, 1, 2, 5, 6, 7, 3, 4)):
                        last = pe.matmul(ps, y_t[:, k, i * P:(i + 1) * P], w_out_s[:, k, s * HALF:(s + 1) * HALF], start=(n == 0), stop=(n == CH - 1))
                    last.then_inc(filled, 1)
                elif kind == "x2t":
                    i, h = key[1:]
                    pe.wait_ge(s_xhat, TILES + i + 1)
                    for j in range(4):
                        last = pe.transpose(ps[:, j * P:(j + 1) * P], chunk(xr[:, i % 4, :], 4 * h + j), ident)
                    last.then_inc(filled, 1)
                elif kind == "lg":
                    i = key[1]
                    if i == 0:
                        pe.wait_ge(s_rb, 80)
                    for h in range(2):
                        who, count = freed_at[index[("x2t", i, h)]]
                        pe.wait_ge(freed_a if who == "a" else freed_d, count)
                    for k in range(CH):
                        last = pe.matmul(ps[:, 0:EXPERTS], h2_t[:, i % 2, k, :], router_s[:, k, :], start=(k == 0), stop=(k == CH - 1))
                    last.then_inc(filled, 1)
                elif kind == "rank":
                    pe.wait_ge(s_sums, 1)
                    pe.matmul(ps, tri, ranks, start=True, stop=False)
                    pe.matmul(ps, ones, before, start=False, stop=True).then_inc(filled, 1)
                elif kind == "count":
                    for i in range(TILES):
                        last = pe.matmul(ps[0:EXPERTS, 0:1], ranks[:, i * EXPERTS:(i + 1) * EXPERTS], ones[:, 0:1],
                                         start=(i == 0), stop=(i == TILES - 1))
                    last.then_inc(filled, 1)
                elif kind == "bounds":
                    pe.wait_ge(s_wide, 1)
                    pe.matmul(ps[:, 0:EXPERTS], nb_wide[0:EXPERTS, :], cst[0:EXPERTS, C_INC:C_INC + EXPERTS], start=True, stop=True, skip_group_check=True)
                    pe.matmul(ps[:, EXPERTS:2 * EXPERTS], nb_wide[0:EXPERTS, :], cst[0:EXPERTS, C_EXC:C_EXC + EXPERTS], start=True, stop=True, skip_group_check=True).then_inc(filled, 1)
                elif kind == "index":
                    for m in range(2 * TILES):
                        pe.wait_ge(s_hot, m // TILES + 1)
                        last = pe.matmul(ps[0:BLK, 0:P], in_row[:, m, :], in_block[:, m, :], start=(m == 0), stop=(m == 2 * TILES - 1))
                    last.then_inc(filled, 1)

                elif kind == "repeat":
                    pe.wait_ge(freed_d, freed_at[index[("index",)]][1])
                    pe.matmul(ps[:, 0:P], late[0:BLK, L_REPEAT:L_REPEAT + P], rows_list[0:BLK, :], start=True, stop=True).then_inc(filled, 1)

            xt_p, h_p, ft_p, y_p = (banks[:, b, :] for b in range(4))
            pe.wait_ge(s_index, 1)

            def x_transposes(n):
                pe.wait_ge(s_xcopy, n + 1)
                for j in range(2):
                    last = pe.transpose(xt_p[:, j * P:(j + 1) * P], xrow[:, j:QUART:2], ident)
                last.then_inc(s_xtp, 1)

            def up(n, slot):
                w13 = at(slot * EXPERT_FLOATS, 2, CH, FF)
                for k in range(CH):
                    for q in range(4):
                        last = pe.matmul(h_p[32 * q:32 * q + 32, 0:2 * P].rearrange("p (a b) -> p a b", a=2), xt_s[:, k % 2, k // 2, :],
                                         w13[:, :, k, q * P:(q + 1) * P], start=(k == 0), stop=(k == CH - 1), tile_position=(0, 32 * q))
                last.then_inc(s_h13, 1)

            def down(n, slot):
                pe.wait_ge(s_ft, n + 1)
                pe.wait_ge(s_y, n + 1)
                w2 = at(slot * EXPERT_FLOATS + 8192, 4, D)
                for k in range(4):
                    for q in range(4):
                        last = pe.matmul(y_p[32 * q:32 * q + 32, 0:QUART], ff_t[:, k * BLK:(k + 1) * BLK],
                                         w2[:, k, q * QUART:(q + 1) * QUART], start=(k == 0), stop=(k == 3), tile_position=(0, 32 * q))
                last.then_inc(s_yp, 1)

            def hidden_transposes(n):
                pe.wait_ge(s_ff, n + 1)
                pe.transpose(ft_p[:, 0:P], ff, ident).then_inc(s_ftp, 1)

            def up_and_next(n, slot):
                pe.wait_ge(s_xts, n + 1)
                up(n, slot)
                x_transposes(n + 1)

            x_transposes(0)
            with pe.Fori(0, EXPERTS // SLOTS) as r:
                for slot in range(SLOTS):
                    lo = pe.value_load(table[0:1, bass.ds(r * SLOTS + slot, 1)], min_val=0, max_val=MAX_BLOCKS - 1)
                    hi = pe.value_load(table[0:1, bass.ds(r * SLOTS + (slot + 1), 1)], min_val=1, max_val=MAX_BLOCKS)
                    for k in range(4):
                        pe.wait_ge(s_w[slot][k], (r + 1) * 16)
                    pe.sem_inc(s_begun, 1)
                    up_and_next(lo, slot)
                    if slot:
                        down(lo - 1, slot - 1)
                    else:
                        with pe.If(r > 0):
                            down(lo - 1, SLOTS - 1)
                    hidden_transposes(lo)
                    for k in range(4, 6):
                        pe.wait_ge(s_w[slot][k], (r + 1) * 16)
                    pe.sem_inc(s_begun, 1)
                    with pe.If(hi > lo + 1):
                        with pe.Fori(lo + 1, hi) as n:
                            up_and_next(n, slot)
                            down(n - 1, slot)
                            hidden_transposes(n)
            blocks = pe.value_load(table[0:1, EXPERTS:EXPERTS + 1], min_val=EXPERTS, max_val=MAX_BLOCKS)
            down(blocks - 1, SLOTS - 1)

        @block.scalar
        def _(act):
            def begin(*key):
                full(act, *key)
                return bank_of(*key)

            def root(dst, src, sums):
                act.wait_ge(s_ss, sums)
                nc.scalar.activation(dst, src, ACT.Sqrt, bias=eps, scale=1.0 / D).then_inc(s_std, 1)

            act.wait_ge(s_eps, 1)
            act.wait_ge(s_c, 16)
            nc.scalar.activation(c_act, c_col, ACT.Silu).then_inc(s_cact, 1)
            for i in range(TILES):
                if i % 4 == 0:
                    act.wait_ge(s_x[i // 4], 16)
                if i:
                    act.wait_ge(s_ss, i)
                nc.scalar.activation(scratch, x_t[:, i, :], ACT.Square, accum_out=ss[:, 0, i:i + 1]).then_inc(s_ss, 1)
                if i % 4 == 3:
                    root(rstd[:, 0, i - 3:i + 1], ss[:, 0, i - 3:i + 1], i + 1)
            def gn_squares(n):
                act.wait_ge(freed_d, freed_at[index[("gm", n // 2, n % 2)]][1])
                act.wait_ge(s_conv, 3 * TAPS)
                nc.scalar.activation(squares[:, n, :], y_t[:, n // 2, (n % 2) * HALF:(n % 2 + 1) * HALF], ACT.Square).then_inc(s_gnsq, 1)

            def gn_silu(n):
                act.wait_ge(s_gnn, n + 1)
                cc, part = n // 2, y_t[:, n // 2, (n % 2) * HALF:(n % 2 + 1) * HALF]
                nc.scalar.activation(part, part, ACT.Silu, bias=vecs[:, 6 + cc:7 + cc], scale=vecs[:, 3 + cc:4 + cc]).then_inc(s_gn, 1)

            act.wait_ge(s_ab, 1)
            for entry in order:
                if entry[-1] != "a":
                    continue
                key = entry[:-1]
                kind = key[0]
                if kind == "x2t":
                    break
                if key == ("u", 0, 0):
                    act.wait_ge(s_mv, 1)
                    nc.scalar.activation(v_rstd, v_rstd, ACT.Sqrt, bias=eps).then_inc(s_vstd, 1)
                    for n in range(6):
                        gn_squares(n)
                ps = begin(*key)
                if kind == "xt":
                    i, h = key[1:]
                    for j in range(4):
                        k = 4 * h + j
                        last = nc.scalar.activation(h_t[:, k, i * P:(i + 1) * P], ps[:, j * P:(j + 1) * P], ACT.Identity,
                                                    bias=ab[:, 1, k:k + 1], scale=ab[:, 0, k:k + 1])
                elif kind == "g":
                    n = 2 * key[1] + key[2]
                    if n >= 2:
                        act.wait_ge(freed_d, freed_at[index[("a", (n - 2) // 2, n % 2)]][1])
                    last = nc.scalar.activation((tmp_a, tmp_b)[n % 2], ps, ACT.Sigmoid)
                elif kind == "ada":
                    if key[1] > 4:
                        act.wait_ge(s_modout, 64 * (key[1] - 4))
                    last = nc.scalar.activation(mod_rows, ps[:, 0:P], ACT.Copy)
                elif kind == "b":
                    last = nc.scalar.activation(xt_four[:, key[1], key[2] * HALF:(key[2] + 1) * HALF], ps, ACT.Copy)
                elif kind == "v":
                    last = nc.scalar.activation(v_t[:, key[1], :], ps[:, 0:SGU], ACT.Gelu_apprx_tanh)
                elif kind == "u":
                    last = nc.scalar.activation(y_t[:, 5 + key[1], key[2] * HALF:(key[2] + 1) * HALF], ps, ACT.Gelu_apprx_tanh)
                elif kind == "gv":
                    last = nc.scalar.activation(squares[:, 2 * key[1] + key[2], :], ps, ACT.Sqrt, bias=eps)
                elif kind == "V":
                    act.wait_ge(s_sg, 5 + key[1])
                    last = nc.scalar.activation((tmp_a, tmp_b)[key[1]], ps, ACT.Copy)
                elif kind == "pq":
                    last = nc.scalar.activation(pq[:, key[1], :, :].rearrange("p a b -> p (a b)"), ps, ACT.Copy)
                last.then_inc(freed_a, 1)
                if key == ("pq", TILES - 1):
                    for n in range(6):
                        gn_silu(n)

            act.wait_ge(s_ab, 2)
            zeroed = 16 * -(-(MAX_BLOCKS + 1 - EXPERTS) * BLK // P)
            act.wait_ge(s_yzero, zeroed)
            for i in range(TILES + 1):
                if i < TILES:
                    act.wait_ge(s_x2, 2 * i + 2)
                    act.wait_ge(s_ss, TILES + i)
                    nc.scalar.activation(scratch, x2[:, i % 4, :], ACT.Square, accum_out=ss[:, 1, i:i + 1]).then_inc(s_ss, 1)
                    root(rstd[:, 1, i:i + 1], ss[:, 1, i:i + 1], TILES + i + 1)
                if i >= 1:
                    ps = begin("x2t", i - 1, 0)
                    if i >= 3:
                        act.wait_ge(filled, index[("lg", i - 3)] + 1)
                    for j in range(4):
                        last = nc.scalar.activation(h2_t[:, (i - 1) % 2, j, :], ps[:, j * P:(j + 1) * P], ACT.Identity,
                                                    bias=ab[:, 3, j:j + 1], scale=ab[:, 2, j:j + 1])
                    last.then_inc(freed_a, 1)
                if i == EARLY + 1:
                    act.wait_ge(s_expin, 1)
                    part = prob[:, 0:EARLY * EXPERTS]
                    nc.scalar.activation(part, part, ACT.Exp).then_inc(s_exp, 1)
            act.wait_ge(s_expin, 2)
            part = prob[:, EARLY * EXPERTS:]
            nc.scalar.activation(part, part, ACT.Exp).then_inc(s_exp, 1)

            act.wait_ge(s_tab, 1)
            act.sem_inc(s_yst, 16)

            def silu(n):
                act.wait_ge(s_h13, n + 1)
                nc.scalar.activation(ff_silu, banks[:, 1, 0:P], ACT.Silu).then_inc(s_silu, 1)

            def hidden_copy(n):
                act.wait_ge(s_ftp, n + 1)
                nc.scalar.activation(ff_t, banks[:, 2, 0:P], ACT.Copy).then_inc(s_ft, 1)

            def result_out(n):
                act.wait_ge(s_y, n + 2)
                act.dma_start(ys_dram.ap()[bass.ds(n * BLK, BLK), :].rearrange("r (q c) -> q r c", q=4), y_s).then_inc(s_yst, 16)

            def rows_on(n, first=False):
                act.wait_ge(s_xrow, (n + 1) * 16)
                if not first:
                    act.wait_ge(s_xtp, n)
                nc.scalar.activation(xrow, xrow_next, ACT.Copy).then_inc(s_xcopy, 1)

            rows_on(0, True)
            rows_on(1)
            blocks = act.value_load(table[0:1, EXPERTS:EXPERTS + 1], min_val=EXPERTS, max_val=MAX_BLOCKS)
            silu(0)
            hidden_copy(0)
            rows_on(2)
            with act.Fori(1, blocks) as n:
                silu(n)
                hidden_copy(n)
                rows_on(n + 2)
                result_out(n - 1)
            result_out(blocks - 1)

            for i in range(TILES + 1):
                if i < TILES:
                    act.wait_ge(s_gat[i], 32)
                    first = at(EXPERT_FLOATS + i * D, D)
                    nc.scalar.activation(first, first, ACT.Copy, scale=gate_w[:, 0, i:i + 1]).then_inc(s_t1, 1)
                if i >= 1:
                    act.wait_ge(s_t3, i)
                    act.wait_ge(s_ss, 2 * TILES + i - 1)
                    nc.scalar.activation(scratch, at(3 * EXPERT_FLOATS + (i - 1) * D, D), ACT.Square,
                                         accum_out=ss[:, 2, i - 1:i]).then_inc(s_ss, 1)
                    root(rstd[:, 2, i - 1:i], ss[:, 2, i - 1:i], 2 * TILES + i)

        @block.vector
        def _(dve):
            steps = [0]

            def link(ins):
                steps[0] += 1
                ins.then_inc(s_link, 1)
                dve.wait_ge(s_link, steps[0])

            def begin(*key):
                full(dve, *key)
                return bank_of(*key)

            v = nc.vector
            v.memset(eps, EPS).then_inc(s_eps, 1)
            dve.wait_ge(s_cact, 1)
            v.tensor_copy(c_wide, c_act.unsqueeze(2).broadcast_to([P, CH, 32])).then_inc(s_cwide, 1)
            def x_hat(half):
                first = 4 * half
                dve.wait_ge(s_std, half + 1)
                link(v.reciprocal(rstd[:, 0, first:first + 4], rstd[:, 0, first:first + 4]))
                for i in range(first, first + 4):
                    v.tensor_scalar(x_t[:, i, :], x_t[:, i, :], rstd[:, 0, i:i + 1], None, ALU.mult).then_inc(s_xhat, 1)

            for n in range(5):
                if n == 2:
                    x_hat(0)
                if n < 4:
                    ps = begin("ada", n)
                    v.tensor_copy(head_rows[:, n, :], ps[:, 0:P]).then_inc(freed_d, 1)
                if n:
                    ps = begin("column", n - 1)
                    v.tensor_copy(col[:, (SH1, SC1)[(n - 1) // 2], 4 * ((n - 1) % 2):4 * ((n - 1) % 2) + 4], ps[:, 0:4]).then_inc(freed_d, 1)
                if n == 2:
                    ps = begin("small")
                    v.tensor_copy(vecs[:, 0:15], ps[:, 0:15])
                    v.tensor_copy(conv_t, ps[:, 16:16 + 3 * TAPS]).then_inc(freed_d, 1)
                    for g in range(2):
                        ps = begin("ws", g)
                        v.tensor_copy(ws_t[:, 3 * g:3 * g + 3, :], ps[:, 0:3 * P].rearrange("p (h q) -> p h q", h=3)).then_inc(freed_d, 1)
                    ps = begin("rs")
                    dve.wait_ge(s_small, 16 * 6)
                    dve.wait_ge(freed_d, freed_at[index[("small",)]][1])
                    for j in range(3):
                        last = v.scalar_tensor_tensor(gain_k[:, j, :], ps[:, j * P:(j + 1) * P], vecs[:, 12 + j:13 + j], bs_b[:, j, :], ALU.mult, ALU.add)
                    last.then_inc(freed_d, 1)

            def affine(a, b, scale, b_scale, shift, b_shift, gain):
                link(v.tensor_tensor(ab[:, a, :], col[:, scale, :], col[:, b_scale, :], ALU.add))
                link(v.scalar_tensor_tensor(ab[:, a, :], ab[:, a, :], 1.0, col[:, gain, :], ALU.add, ALU.mult))
                v.tensor_tensor(ab[:, b, :], col[:, shift, :], col[:, b_shift, :], ALU.add).then_inc(s_ab, 1)

            dve.wait_ge(s_cols, 16 * 6)
            dve.wait_ge(freed_d, freed_at[index[("column", 3)]][1])
            affine(0, 1, SC1, BSC1, SH1, BSH1, LN1)
            dve.wait_ge(s_ab, 1)
            for i in range(TILES):
                if i == TILES // 2:
                    x_hat(1)
                ps = begin("xt", i, 1)
                for j in range(4):
                    last = v.tensor_scalar(h_t[:, 4 + j, i * P:(i + 1) * P], ps[:, j * P:(j + 1) * P],
                                           ab[:, 0, 4 + j:5 + j], ab[:, 1, 4 + j:5 + j], ALU.mult, ALU.add)
                last.then_inc(freed_d, 1)

            for cc in range(3):
                for s in range(2):
                    ps = begin("a", cc, s)
                    dve.wait_ge(freed_a, freed_at[index[("g", cc, s)]][1])
                    v.tensor_tensor(pad_h[:, cc, PAD + s * HALF:PAD + (s + 1) * HALF], ps, (tmp_a, tmp_b)[s], ALU.mult).then_inc(freed_d, 1)
                dve.wait_ge(s_zero, 2)
                dve.wait_ge(freed_d, freed_at[index[("a", cc, 1)]][1])
                for k in range(TAPS):
                    src, w = pad_h[:, cc, k:k + SEQ], conv_t[:, cc * TAPS + k:cc * TAPS + k + 1]
                    if k == 0:
                        ins = v.tensor_scalar(y_t[:, cc, :], src, w, vecs[:, cc:cc + 1], ALU.mult, ALU.add)
                    else:
                        dve.wait_ge(s_conv, cc * TAPS + k)
                        ins = v.scalar_tensor_tensor(y_t[:, cc, :], src, w, y_t[:, cc, :], ALU.mult, ALU.add)
                    ins.then_inc(s_conv, 1)

            for i in range(TILES):
                dve.wait_ge(freed_a, freed_at[index[("v", i)]][1])
                last = v.bn_stats(stats[:, i, :], v_t[:, i, :])
            link(last)
            for i in range(TILES):
                last = v.bn_aggr(mv[:, i, :], stats[:, i, :])
            link(last)
            v.tensor_copy(v_rstd, mv[:, :, 1]).then_inc(s_mv, 1)
            dve.wait_ge(s_vstd, 1)
            link(v.reciprocal(v_rstd, v_rstd))
            for i in range(TILES):
                v.tensor_scalar(v_t[:, i, :], v_t[:, i, :], mv[:, i, 0:1], v_rstd[:, i:i + 1], ALU.subtract, ALU.mult).then_inc(s_vn, 1)

            def centre(n):
                ps = begin("gm", n // 2, n % 2)
                part = y_t[:, n // 2, (n % 2) * HALF:(n % 2 + 1) * HALF]
                v.tensor_tensor(part, part, ps, ALU.subtract).then_inc(freed_d, 1)

            def gn_scale(n):
                part = y_t[:, n // 2, (n % 2) * HALF:(n % 2 + 1) * HALF]
                dve.wait_ge(freed_a, freed_at[index[("gv", n // 2, n % 2)]][1])
                link(v.reciprocal(squares[:, n, :], squares[:, n, :]))
                v.tensor_tensor(part, part, squares[:, n, :], ALU.mult).then_inc(s_gnn, 1)

            def fourier(cc):
                ps = begin("U", cc)
                sin = (tmp_a, tmp_b)[cc]
                dve.wait_ge(freed_a, freed_at[index[("V", cc)]][1])
                v.tensor_tensor(y_t[:, 3 + cc, 0:HALF], ps, sin, ALU.subtract)
                v.tensor_tensor(y_t[:, 3 + cc, SEQ - 1:HALF:-1], ps[:, 1:HALF], sin[:, 1:HALF], ALU.add).then_inc(freed_d, 1)

            dve.wait_ge(s_conv, 3 * TAPS)
            for n in range(6):
                centre(n)
            for n in range(6):
                gn_scale(n)
            for n in range(6):
                j, hh = n // 2, n % 2
                ps = begin("sg", j, hh)
                t = (tmp_a, tmp_b)[n % 2]
                if n >= 2:
                    dve.wait_ge(s_sg, n - 1)
                v.scalar_tensor_tensor(t.rearrange("p (a b) -> p a b", a=4), ps.rearrange("p (a b) -> p a b", a=4), vecs[:, 9 + j:10 + j],
                                       gain_k[:, j, :].unsqueeze(1).broadcast_to([P, 4, P]), ALU.mult, ALU.add).then_inc(freed_d, 1)
                dve.wait_ge(freed_d, freed_at[index[("sg", j, hh)]][1])
                part = y_t[:, 5 + j, hh * HALF:(hh + 1) * HALF]
                v.tensor_tensor(part, part, t, ALU.mult).then_inc(s_sg, 1)
            fourier(0)
            ps = begin("mid")
            for cc in range(2):
                last = v.tensor_copy(y_t[:, 3 + cc, HALF:HALF + 1], ps[:, cc:cc + 1])
            last.then_inc(freed_d, 1)
            fourier(1)
            def te(view):
                return view.rearrange("p (t e) -> p t e", t=TILES)

            def over_t(view, tiles=TILES, n=EXPERTS):
                return view.unsqueeze(1).broadcast_to([P, tiles, n])

            def picked(dst, values, hot, t0=0, t1=TILES):
                link(v.tensor_tensor(te(cand)[:, t0:t1, :], te(values)[:, t0:t1, :], te(hot)[:, t0:t1, :], ALU.mult))
                link(v.tensor_reduce(dst, te(cand)[:, t0:t1, :], AX_X, ALU.add))

            def route(part, t0, t1):
                n = t1 - t0

                def tiles(view):
                    return te(view)[:, t0:t1, :]

                def tge(view):
                    return view.rearrange("p (g e) -> p g e", e=PER)[:, t0 * GROUPS:t1 * GROUPS, :]

                def groups(row):
                    return best[:, row, t0 * GROUPS:t1 * GROUPS]

                def tg(row):
                    return groups(row).rearrange("p (t g) -> p t g", t=n)

                def over_e(view, m=EXPERTS):
                    return view.unsqueeze(2).broadcast_to([P, n, m])

                def over_pe(row):
                    return groups(row).unsqueeze(2).broadcast_to([P, n * GROUPS, PER])

                dve.wait_ge(freed_d, freed_at[index[("lg", t1 - 1)]][1])
                top, total_e = tok[:, 0, t0:t1], tok[:, 1, t0:t1]
                link(v.tensor_reduce(top, tiles(logit), AX_X, ALU.max))
                v.tensor_tensor(tiles(prob), tiles(logit), over_e(top), ALU.subtract).then_inc(s_expin, 1)
                dve.wait_ge(s_exp, part + 1)
                link(v.tensor_reduce(total_e, tiles(prob), AX_X, ALU.add))
                link(v.reciprocal(total_e, total_e))
                link(v.tensor_tensor(tiles(prob), tiles(prob), over_e(total_e), ALU.mult))
                dve.wait_ge(s_rb, 80)
                link(v.tensor_tensor(tiles(sel), tiles(prob), over_t(router_bb, n), ALU.add))

                def first_best(values, top_row, hot, where_row):
                    link(v.tensor_reduce(groups(top_row), tge(values), AX_X, ALU.max))
                    link(v.tensor_tensor(tge(cand), tge(values), over_pe(top_row), ALU.is_equal))
                    link(v.tensor_tensor(tiles(cand), tiles(cand), over_t(cst[:, C_REV:C_REV + EXPERTS], n), ALU.mult))
                    link(v.tensor_reduce(groups(where_row), tge(cand), AX_X, ALU.max))
                    link(v.tensor_tensor(tge(hot), tge(cand), over_pe(where_row), ALU.is_equal))

                first_best(sel, 0, hot1, 1)
                link(v.scalar_tensor_tensor(tiles(sel2), tiles(hot1), NEG, tiles(sel), ALU.mult, ALU.add))
                first_best(sel2, 2, hot2, 3)
                link(v.tensor_tensor(groups(4), groups(0), groups(2), ALU.add))
                link(v.tensor_reduce(top, tg(4), AX_X, ALU.max))
                link(v.tensor_tensor(tg(5), tg(4), over_e(top, GROUPS), ALU.is_equal))
                link(v.tensor_tensor(tg(5), tg(5), over_t(cst[:, C_GREV:C_GREV + GROUPS], n, GROUPS), ALU.mult))
                link(v.tensor_reduce(total_e, tg(5), AX_X, ALU.max))
                link(v.tensor_tensor(tg(6), tg(5), over_e(total_e, GROUPS), ALU.is_equal))
                v.tensor_tensor(tge(hot1), tge(hot1), over_pe(6), ALU.mult)
                link(v.tensor_tensor(tge(hot2), tge(hot2), over_pe(6), ALU.mult))
                link(v.tensor_tensor(tiles(ranks), tiles(hot1), tiles(hot2), ALU.add))
                if t0 == 0:
                    link(v.memset(before[:, 0:EXPERTS], 0.0))
                for i in range(t0 + 1, min(t1 + 1, TILES)):
                    link(v.tensor_tensor(before[:, i * EXPERTS:(i + 1) * EXPERTS], before[:, (i - 1) * EXPERTS:i * EXPERTS],
                                         ranks[:, (i - 1) * EXPERTS:i * EXPERTS], ALU.add))

            def weights(t0, t1):
                first, second, both = (tok[:, k, t0:t1] for k in (2, 3, 4))
                picked(first, prob, hot1, t0, t1)
                picked(second, prob, hot2, t0, t1)
                link(v.tensor_tensor(both, first, second, ALU.add))
                link(v.reciprocal(both, both))
                v.tensor_tensor(gate_w[:, 0, t0:t1], first, both, ALU.mult)
                link(v.tensor_tensor(gate_w[:, 1, t0:t1], second, both, ALU.mult))

            dve.wait_ge(s_modcols, 32)
            affine(2, 3, SC2, BSC2, SH2, BSH2, LN2)
            dve.wait_ge(s_ab, 2)
            v.tensor_copy(ab_jq[:, 0, :, :], ab[:, 2, :].rearrange("p (q j) -> p j q", q=4))
            v.tensor_copy(ab_jq[:, 1, :, :], ab[:, 3, :].rearrange("p (q j) -> p j q", q=4))
            dve.wait_ge(s_gate1, 32)
            link(v.tensor_tensor(gate1, gate1, gate1_b, ALU.add))
            for i in range(TILES + 2):
                if i < TILES:
                    dve.wait_ge(s_xr[i], 16)
                    if i >= 4:
                        dve.wait_ge(s_x2st, 16 * (i - 3))
                    for s in range(2):
                        ps = begin("wo", i, s)
                        part = x2[:, i % 4, s * HALF:(s + 1) * HALF]
                        v.tensor_tensor(part, ps, gate1[:, s * HALF:(s + 1) * HALF], ALU.mult).then_inc(freed_d, 1)
                        dve.wait_ge(freed_d, freed_at[index[("wo", i, s)]][1])
                        v.tensor_tensor(part, part, xr[:, i % 4, s * HALF:(s + 1) * HALF], ALU.add).then_inc(s_x2, 1)
                if 1 <= i <= TILES:
                    ps = begin("x2t", i - 1, 1)
                    if i >= 3:
                        dve.wait_ge(filled, index[("lg", i - 3)] + 1)
                    for j in range(4):
                        last = v.tensor_scalar(h2_t[:, (i - 1) % 2, 4 + j, :], ps[:, j * P:(j + 1) * P],
                                               ab[:, 2, 4 + j:5 + j], ab[:, 3, 4 + j:5 + j], ALU.mult, ALU.add)
                    last.then_inc(freed_d, 1)
                if i >= 2:
                    ps = begin("lg", i - 2)
                    v.tensor_copy(logit[:, (i - 2) * EXPERTS:(i - 1) * EXPERTS], ps[:, 0:EXPERTS]).then_inc(freed_d, 1)
                if i < TILES:
                    dve.wait_ge(s_std, 2 + i + 1)
                    link(v.reciprocal(rstd[:, 1, i:i + 1], rstd[:, 1, i:i + 1]))
                    v.tensor_scalar(xr[:, i % 4, :], x2[:, i % 4, :], rstd[:, 1, i:i + 1], None, ALU.mult).then_inc(s_xhat, 1)
                if i == 1:
                    dve.wait_ge(s_gate2, 128)
                    link(v.tensor_tensor(gate2, gate2, gate2_b, ALU.add))
                if i == EARLY + 1:
                    route(0, 0, EARLY)
                    weights(0, EARLY)

            route(1, EARLY, TILES)
            v.memset(tok[:, 7, :], 0.0).then_inc(s_sums, 1)
            ps_rank = begin("rank")
            v.tensor_copy(sel, ps_rank).then_inc(freed_d, 1)
            ps = begin("count")
            v.tensor_copy(cnt[0:EXPERTS, 0:1], ps[0:EXPERTS, 0:1]).then_inc(freed_d, 1)
            dve.wait_ge(freed_d, freed_at[index[("count",)]][1])
            link(v.tensor_scalar(best[0:EXPERTS, 7, 0:SEQ // BLK], cst[0:EXPERTS, C_THR:C_THR + SEQ // BLK], cnt[0:EXPERTS, 0:1], None, ALU.is_lt))
            link(v.tensor_reduce(cnt[0:EXPERTS, 1:2], best[0:EXPERTS, 7, 0:SEQ // BLK], AX_X, ALU.add))
            link(v.tensor_scalar(cnt[0:EXPERTS, 1:2], cnt[0:EXPERTS, 1:2], 1.0, None, ALU.add))
            v.tensor_scalar(nb_wide[0:EXPERTS, :], ones[0:EXPERTS, :], cnt[0:EXPERTS, 1:2], None, ALU.mult).then_inc(s_wide, 1)
            weights(EARLY, TILES)
            ps = begin("bounds")
            v.tensor_copy(bounds, ps[:, 0:2 * EXPERTS].rearrange("p (a e) -> p a e", a=2)).then_inc(freed_d, 1)
            dve.wait_ge(freed_d, freed_at[index[("bounds",)]][1])
            ends, first_block = bounds[:, 0, :], bounds[:, 1, :]
            link(v.scalar_tensor_tensor(te(sel2), over_t(first_block), float(BLK), te(sel), ALU.mult, ALU.add))
            picked(tok[:, 5, :], sel2, hot1)
            picked(tok[:, 6, :], sel2, hot2)
            link(v.tensor_copy(rows_at[:, 0, :], tok[:, 5:7, :].rearrange("p k t -> p (k t)")))
            shift = BLK.bit_length() - 1
            v.tensor_scalar(rows_at[:, 1, :], rows_at[:, 0, :], shift, None, ALU.arith_shift_right)
            link(v.tensor_scalar(rows_at[:, 2, :], rows_at[:, 0, :], BLK - 1, None, ALU.bitwise_and))
            link(v.tensor_copy(place, rows_at[:, 1:3, :]))
            dve.wait_ge(s_late, 16)

            def same(dst, choice, numbers, n):
                return v.tensor_tensor(dst, choice.unsqueeze(2).broadcast_to([P, choice.shape[1], n]),
                                       late[:, numbers:numbers + n].unsqueeze(1).broadcast_to([P, choice.shape[1], n]), ALU.is_equal)

            link(same(in_row, place[:, 1, :], L_ROW, BLK))
            v.tensor_tensor(in_row.rearrange("p (k t) r -> p k t r", k=2), in_row.rearrange("p (k t) r -> p k t r", k=2),
                            late[:, L_INDEX:L_INDEX + TILES].unsqueeze(1).unsqueeze(3).broadcast_to([P, 2, TILES, BLK]), ALU.mult)
            for k in range(2):
                same(in_block[:, k * TILES:(k + 1) * TILES, :], place[:, 0, k * TILES:(k + 1) * TILES], L_BLOCK, P).then_inc(s_hot, 1)
            v.tensor_copy(table[0:1, 1:EXPERTS + 1], ends[0:1, :])
            v.memset(table[0:1, 0:1], 0).then_inc(s_tab, 1)
            v.memset(quarters[:, MAX_BLOCKS:MAX_BLOCKS + 2], 0)
            ps = begin("index")
            v.tensor_copy(rows_list[0:BLK, :], ps[0:BLK, 0:P]).then_inc(freed_d, 1)
            ps = begin("repeat")
            v.tensor_scalar(quarters[:, 0:P], ps[:, 0:P], late[:, L_QUARTER:L_QUARTER + 1], None, ALU.add).then_inc(freed_d, 1)
            v.memset(tok[:, 1, :], 0.0).then_inc(s_y, 1)
            dve.wait_ge(freed_d, freed_at[index[("repeat",)]][1])
            v.memset(tok[:, 2, :], 0.0).then_inc(s_index, 1)

            def x_ready(n, first=False):
                dve.wait_ge(s_xtp, n + 1)
                if not first:
                    dve.wait_ge(s_h13, n)
                xt_v = xt_s.rearrange("p j q t -> p (j q) t")
                v.tensor_tensor(xt_v, banks[:, 0, 0:QUART].rearrange("p (a t) -> p a t", a=CH),
                                ab_jq[:, 0, :, :].rearrange("p j q -> p (j q)").unsqueeze(2).broadcast_to([P, CH, BLK]), ALU.mult).then_inc(s_xtm, 1)
                dve.wait_ge(s_xtm, n + 1)
                v.tensor_tensor(xt_v, xt_v, ab_jq[:, 1, :, :].rearrange("p j q -> p (j q)").unsqueeze(2).broadcast_to([P, CH, BLK]), ALU.add).then_inc(s_xts, 1)

            def hidden(n):
                dve.wait_ge(s_silu, n + 1)
                v.tensor_tensor(ff, ff_silu, banks[:, 1, P:2 * P], ALU.mult).then_inc(s_ff, 1)

            def result(n, first=False):
                dve.wait_ge(s_yp, n + 1)
                if not first:
                    dve.wait_ge(s_yst, (n + 1) * 16)
                v.tensor_tensor(y_s, banks[:, 3, 0:QUART], gate2, ALU.mult).then_inc(s_y, 1)

            x_ready(0, True)
            hidden(0)
            x_ready(1)
            hidden(1)
            x_ready(2)
            result(0, True)
            blocks = dve.value_load(table[0:1, EXPERTS:EXPERTS + 1], min_val=EXPERTS, max_val=MAX_BLOCKS)
            with dve.Fori(2, blocks) as n:
                hidden(n)
                x_ready(n + 1)
                result(n - 1)
            result(blocks - 1)

            dve.wait_ge(s_x2r, 16)
            dve.wait_ge(s_fg, 16)
            for i in range(TILES + 1):
                if i < TILES:
                    total_i = at(3 * EXPERT_FLOATS + i * D, D)
                    dve.wait_ge(s_t1, i + 1)
                    v.scalar_tensor_tensor(total_i, at(2 * EXPERT_FLOATS + i * D, D), gate_w[:, 1, i:i + 1], at(EXPERT_FLOATS + i * D, D),
                                           ALU.mult, ALU.add).then_inc(s_t2, 1)
                    dve.wait_ge(s_t2, i + 1)
                    v.tensor_tensor(total_i, total_i, at(i * D, D), ALU.add).then_inc(s_t3, 1)
                if i >= 1:
                    dve.wait_ge(s_std, 2 + TILES + i)
                    link(v.reciprocal(rstd[:, 2, i - 1:i], rstd[:, 2, i - 1:i]))
                    total_i = at(3 * EXPERT_FLOATS + (i - 1) * D, D)
                    v.scalar_tensor_tensor(total_i, total_i, rstd[:, 2, i - 1:i], at(8192, D), ALU.mult, ALU.mult).then_inc(s_tout, 1)


def kernel(x, c, ln1_g, ln2_g, w_ada, b_ada, w_in, w_out, conv_w, conv_b, conv_gn_g, conv_gn_b,
           sgu_ln_g, sgu_ln_b, sgu_w, sgu_b, router_w, router_b, exp_w1, exp_w3, exp_w2, final_g):
    import numpy as np
    from concourse import bacc
    from concourse.bass_utils import run_bass_kernel_spmd

    p = np.arange(P)
    consts = np.zeros((P, C_END + L_END), np.float32)
    consts[:, C_ID:C_ID + P] = np.eye(P)
    consts[:, C_TRI:C_TRI + P] = p[:, None] < p[None, :]
    consts[:, C_ONE:C_ONE + P] = 1.0
    consts[:, C_BD:C_BD + P] = (p[:, None] // 64 == p[None, :] // 64) / 64.0
    angle = 2 * np.pi * ((p[:, None] % 64) * (p[None, :] % 64) % 64) / 64.0
    same = (p[:, None] // 64 == p[None, :] // 64) / np.sqrt(64.0 * SEQ)
    consts[:, C_DFT:C_DFT + P] = np.cos(angle) * same
    consts[:, C_DFT + P:C_DFT + 2 * P] = np.sin(angle) * same
    e = np.arange(EXPERTS)
    consts[0:EXPERTS, C_EXC:C_EXC + EXPERTS] = e[:, None] < e[None, :]
    consts[0:EXPERTS, C_INC:C_INC + EXPERTS] = e[:, None] <= e[None, :]
    consts[:, C_REV:C_REV + EXPERTS] = PER - e % PER
    consts[:, C_GREV:C_GREV + GROUPS] = GROUPS - np.arange(GROUPS)
    consts[:, C_THR:C_THR + SEQ // BLK] = BLK * (1 + np.arange(SEQ // BLK))
    consts[:, C_ALT] = 1.0 - 2.0 * (p % 2)
    late = consts[:, C_END:]
    late[:, L_BLOCK:L_BLOCK + P] = p
    late[:, L_ROW:L_ROW + BLK] = np.arange(BLK)
    late[:, L_INDEX:L_INDEX + TILES] = 4 * (p[:, None] + P * np.arange(TILES)[None, :])
    late[:, L_QUARTER] = p // 32
    late[0:BLK, L_REPEAT:L_REPEAT + P] = p[:BLK, None] == p[None, :] % BLK
    pos = np.arange(SEQ)
    turn = 2 * np.pi * (pos[:, None] * np.arange(HALF)[None, :] % SEQ) / SEQ
    dft = np.stack([np.cos(turn), np.sin(turn)]).astype(np.float32).reshape(2, TILES, P, HALF)
    dft = np.ascontiguousarray(dft.transpose(2, 0, 1, 3))

    inputs = dict(x=x[0], c=c, ln1_g=ln1_g[0], ln2_g=ln2_g[0], w_ada=w_ada[0], b_ada=b_ada[0], w_in=w_in[0], w_out=w_out[0],
                  conv_w=conv_w[0], conv_b=conv_b[0], conv_gn_g=conv_gn_g[0], conv_gn_b=conv_gn_b[0], sgu_ln_g=sgu_ln_g[0],
                  sgu_ln_b=sgu_ln_b[0], sgu_w=sgu_w[0], sgu_b=sgu_b[0], router_w=router_w, router_b=router_b,
                  exp_w1=exp_w1[0], exp_w3=exp_w3[0], exp_w2=exp_w2[0], final_g=final_g, consts=consts, dft=dft)
    nc = bacc.Bacc("TRN2", target_bir_lowering=False, num_devices=1)
    arrays, args = {}, []
    for name, a in inputs.items():
        a = np.ascontiguousarray(a)
        arrays[f"in_{name}"] = a
        args.append(nc.dram_tensor(f"in_{name}", a.shape, mybir.dt.from_np(a.dtype), kind="ExternalInput").ap())
    out = nc.dram_tensor("out", (SEQ, D), F32, kind="ExternalOutput").ap()
    build(nc, *args, out)
    r = run_bass_kernel_spmd(nc, [arrays], core_ids=[0])
    return r.results[0]["out"].reshape(1, SEQ, D)
```
